# Optimizing a Trainium2 kernel written in Bass

```python
import jax, jax.numpy as jnp
from jax import lax
import numpy as np

D_MODEL = 1024
BATCH = 1
SEQ = 256
DEPTH = 2

RMS_EPS = 1e-6
GLA_HEADS = 4
GLA_KEY_DIM = 64
GLA_VALUE_DIM = 128
GLA_GATE_RANK = 16
GLA_GATE_NORMALIZER = 16.0
GLA_CHUNK = 64
LRU_WIDTH = 512
LRU_BLOCKS = 8
LRU_CONV_WIDTH = 4
LRU_C = 8.0
DIL_PATTERNS = ((128, 1), (512, 4), (2048, 16))
N_PATTERNS = 3
DIL_HEADS = 4
DIL_HEAD_DIM = 128
ATTN_BLOCK = 128
ROPE_THETA = 500000.0
ROPE_DIMS = DIL_HEAD_DIM // 4
N_BRANCHES = 3
BRANCH_WIDTH = 512
N_EXPERTS = 16
N_GROUPS = 4
EXPERTS_PER_GROUP = N_EXPERTS // N_GROUPS
TOPK_GROUPS = 1
TOP_K = 2
EXPERT_FF = 512
MOE_BLOCK = 256

IN_SPLITS = (GLA_HEADS * GLA_KEY_DIM, GLA_HEADS * GLA_KEY_DIM, GLA_HEADS * GLA_VALUE_DIM,
             GLA_HEADS * GLA_VALUE_DIM, GLA_GATE_RANK, LRU_WIDTH, LRU_WIDTH,
             3 * N_PATTERNS * DIL_HEADS * DIL_HEAD_DIM, N_BRANCHES * D_MODEL)
IN_COLS = sum(IN_SPLITS)

kernel_name = 'hybrid_gla_rglru_dilated_moe'

def rmsnorm(x, gain):
    xf = x.astype(jnp.float32)
    y = xf * lax.rsqrt(jnp.mean(xf * xf, axis=-1, keepdims=True) + RMS_EPS)
    return (y * gain.astype(jnp.float32)).astype(x.dtype)

def gla_branch(q, k, v, og, g_low, w_gate_up, b_gate, out_gain):
    B, S, _ = q.shape
    H, DK, DV, C = GLA_HEADS, GLA_KEY_DIM, GLA_VALUE_DIM, GLA_CHUNK
    N = S // C
    f32 = jnp.float32
    log_alpha = jax.nn.log_sigmoid(jnp.einsum('bsr,rk->bsk', g_low, w_gate_up).astype(f32)
                                   + b_gate.astype(f32)) / GLA_GATE_NORMALIZER

    def to_chunks(t, d):
        return t.astype(f32).reshape(B, N, C, H, d).transpose(0, 3, 1, 2, 4)

    qc = to_chunks(q, DK) * (DK ** -0.5)
    kc = to_chunks(k, DK)
    vc = to_chunks(v, DV)
    cum = jnp.cumsum(to_chunks(log_alpha, DK), axis=3)
    q_dec = qc * jnp.exp(cum)
    k_inv = kc * jnp.exp(-cum)
    causal = jnp.tril(jnp.ones((C, C), dtype=bool))
    scores = jnp.where(causal, jnp.einsum('bhnid,bhnjd->bhnij', q_dec, k_inv), 0.0)
    o_intra = jnp.einsum('bhnij,bhnjv->bhniv', scores, vc)
    total = cum[:, :, :, -1]
    kv_chunk = jnp.einsum('bhncd,bhncv->bhndv', kc * jnp.exp(total[:, :, :, None] - cum), vc)

    def step(state, inp):
        decay, kv = inp
        return state * jnp.exp(decay)[..., None] + kv, state

    init = jnp.zeros((B, H, DK, DV), f32)
    _, prev = lax.scan(step, init, (jnp.moveaxis(total, 2, 0), jnp.moveaxis(kv_chunk, 2, 0)))
    prev = jnp.moveaxis(prev, 0, 2)
    o = o_intra + jnp.einsum('bhncd,bhndv->bhncv', q_dec, prev)
    o = o.transpose(0, 2, 3, 1, 4).reshape(B, S, H, DV).astype(v.dtype)
    o = rmsnorm(o, out_gain).reshape(B, S, H * DV)
    return o * jax.nn.silu(og)

def rglru_branch(xb, yb, conv_w, conv_b, w_a, b_a, w_x, b_x, lam):
    B, S, W = xb.shape
    f32 = jnp.float32
    xc = lax.conv_general_dilated(xb, conv_w[:, None, :], window_strides=(1,),
                                  padding=((LRU_CONV_WIDTH - 1, 0),),
                                  dimension_numbers=('NWC', 'WIO', 'NWC'),
                                  feature_group_count=W) + conv_b
    xg = xc.reshape(B, S, LRU_BLOCKS, W // LRU_BLOCKS)
    r = jax.nn.sigmoid(jnp.einsum('bsnc,ncd->bsnd', xg, w_a).reshape(B, S, W).astype(f32) + b_a.astype(f32))
    i = jax.nn.sigmoid(jnp.einsum('bsnc,ncd->bsnd', xg, w_x).reshape(B, S, W).astype(f32) + b_x.astype(f32))
    log_a = -LRU_C * r * jax.nn.softplus(-lam.astype(f32))
    a = jnp.exp(log_a)
    u = jnp.sqrt(-jnp.expm1(2.0 * log_a)) * i * xc.astype(f32)

    def combine(left, right):
        a_l, h_l = left
        a_r, h_r = right
        return a_l * a_r, a_r * h_l + h_r

    _, h = lax.associative_scan(combine, (a, u), axis=1)
    return (h * jax.nn.gelu(yb.astype(f32))).astype(xb.dtype)

def partial_rope(t, positions):
    half = ROPE_DIMS // 2
    f32 = jnp.float32
    inv_freq = ROPE_THETA ** (-jnp.arange(half, dtype=f32) / half)
    ang = positions.astype(f32)[:, :, None] * inv_freq
    cos = jnp.cos(ang)[:, :, None, None, :]
    sin = jnp.sin(ang)[:, :, None, None, :]
    tf = t.astype(f32)
    x1 = tf[..., :half]
    x2 = tf[..., half:ROPE_DIMS]
    return jnp.concatenate([x1 * cos - x2 * sin, x2 * cos + x1 * sin, tf[..., ROPE_DIMS:]],
                           axis=-1).astype(t.dtype)

def banded_causal_attention(q, k, v, span):
    Bp, L, H, Dh = q.shape
    BLK = ATTN_BLOCK
    nb = -(-L // BLK)
    pad = nb * BLK - L
    f32 = jnp.float32

    def blocks(t):
        return jnp.pad(t.astype(f32), ((0, 0), (0, pad), (0, 0), (0, 0))).reshape(Bp, nb, BLK, H, Dh)

    def with_prev(t):
        prev = jnp.pad(t, ((0, 0), (1, 0), (0, 0), (0, 0), (0, 0)))[:, :-1]
        return jnp.concatenate([prev, t], axis=2)

    qb = blocks(q)
    kk = with_prev(blocks(k))
    vv = with_prev(blocks(v))
    s = jnp.einsum('bnqhd,bnkhd->bnhqk', qb, kk) * (Dh ** -0.5)
    qi = jnp.arange(BLK)[:, None]
    kj = jnp.arange(2 * BLK)[None, :]
    dist = qi + BLK - kj
    band = (dist >= 0) & (dist <= span)
    first = jnp.arange(nb)[:, None, None] == 0
    valid = band[None] & ~(first & (kj < BLK)[None])
    s = jnp.where(valid[None, :, None], s, -jnp.inf)
    m = jnp.max(s, axis=-1, keepdims=True)
    p = jnp.exp(s - m)
    denom = jnp.sum(p, axis=-1)
    o = jnp.einsum('bnhqk,bnkhd->bnqhd', p, vv) / jnp.transpose(denom, (0, 1, 3, 2))[..., None]
    lse = jnp.transpose(m[..., 0] + jnp.log(denom), (0, 1, 3, 2))
    return o.reshape(Bp, nb * BLK, H, Dh)[:, :L], lse.reshape(Bp, nb * BLK, H)[:, :L]

def stride_gather(t, dil):
    B, S, H, Dh = t.shape
    return t.reshape(B, S // dil, dil, H, Dh).transpose(0, 2, 1, 3, 4).reshape(B * dil, S // dil, H, Dh)

def stride_scatter(t, B, dil):
    L = t.shape[1]
    rest = t.shape[2:]
    t = t.reshape((B, dil, L) + rest)
    t = jnp.moveaxis(t, 1, 2)
    return t.reshape((B, L * dil) + rest)

def dilated_branch(q, k, v, positions, q_gain, k_gain):
    B, S, P, H, Dh = q.shape
    q = partial_rope(rmsnorm(q, q_gain), positions)
    k = partial_rope(rmsnorm(k, k_gain), positions)
    outs, lses = [], []
    for p, (window, dil) in enumerate(DIL_PATTERNS):
        o, lse = banded_causal_attention(stride_gather(q[:, :, p], dil), stride_gather(k[:, :, p], dil),
                                         stride_gather(v[:, :, p], dil), window // dil)
        outs.append(stride_scatter(o, B, dil))
        lses.append(stride_scatter(lse, B, dil))
    w = jax.nn.softmax(jnp.stack(lses, axis=-1), axis=-1)
    o = jnp.einsum('bshpd,bshp->bshd', jnp.stack(outs, axis=3), w)
    return o.reshape(B, S, H * Dh).astype(v.dtype)

def mixer_block(h, positions, w_in, gla_gate_up, gla_gate_bias, gla_out_gain, lru_conv_w, lru_conv_b,
                lru_w_a, lru_b_a, lru_w_x, lru_b_x, lru_lambda, q_norm_gain, k_norm_gain, w_branch, w_out):
    B, S, D = h.shape
    proj = jnp.einsum('bsd,de->bse', h, w_in)
    cuts = np.cumsum(IN_SPLITS)[:-1].tolist()
    q_a, k_a, v_a, og_a, glow_a, x_b, y_b, qkv_c, gate_logits = jnp.split(proj, cuts, axis=-1)
    br_a = gla_branch(q_a, k_a, v_a, og_a, glow_a, gla_gate_up, gla_gate_bias, gla_out_gain)
    br_b = rglru_branch(x_b, y_b, lru_conv_w, lru_conv_b, lru_w_a, lru_b_a, lru_w_x, lru_b_x, lru_lambda)
    qkv = qkv_c.reshape(B, S, 3, N_PATTERNS, DIL_HEADS, DIL_HEAD_DIM)
    br_c = dilated_branch(qkv[:, :, 0], qkv[:, :, 1], qkv[:, :, 2], positions, q_norm_gain, k_norm_gain)
    gates = jax.nn.sigmoid(gate_logits.astype(jnp.float32)).reshape(B, S, N_BRANCHES, D)
    merged = sum(gates[:, :, n] * jnp.einsum('bsw,wd->bsd', br, w_branch[n]).astype(jnp.float32)
                 for n, br in enumerate((br_a, br_b, br_c)))
    return jnp.einsum('bsd,de->bse', merged.astype(h.dtype), w_out)

def moe_ffn(h, router_w, router_b, w_gate, w_up, w_down):
    B, S, D = h.shape
    T = B * S
    TK = T * TOP_K
    xt = h.reshape(T, D)
    logits = jnp.einsum('td,de->te', xt, router_w).astype(jnp.float32) + router_b.astype(jnp.float32)
    scores = jax.nn.softmax(logits, axis=-1)
    group_score = lax.top_k(scores.reshape(T, N_GROUPS, EXPERTS_PER_GROUP), TOP_K)[0].sum(-1)
    _, gsel = lax.top_k(group_score, TOPK_GROUPS)
    gmask = jnp.any(gsel[..., None] == jnp.arange(N_GROUPS), axis=-2)
    emask = jnp.repeat(gmask, EXPERTS_PER_GROUP, axis=-1)
    topw, topi = lax.top_k(jnp.where(emask, scores, -jnp.inf), TOP_K)
    topw = topw / jnp.sum(topw, axis=-1, keepdims=True)
    flat_e = topi.reshape(TK)
    order = jnp.argsort(flat_e)
    sorted_e = flat_e[order]
    tok = order // TOP_K
    counts = jnp.bincount(flat_e, length=N_EXPERTS)
    starts = jnp.cumsum(counts) - counts
    padded = (counts + MOE_BLOCK - 1) // MOE_BLOCK * MOE_BLOCK
    pad_ends = jnp.cumsum(padded)
    pad_starts = pad_ends - padded
    dest = pad_starts[sorted_e] + jnp.arange(TK) - starts[sorted_e]
    n_rows = TK + N_EXPERTS * MOE_BLOCK
    n_blocks = n_rows // MOE_BLOCK
    xs = jnp.zeros((n_rows, D), h.dtype).at[dest].set(xt[tok])
    block_e = jnp.minimum(jnp.searchsorted(pad_ends, jnp.arange(n_blocks) * MOE_BLOCK, side='right'),
                          N_EXPERTS - 1)

    def expert_rows(args):
        xb, e = args
        return (jax.nn.silu(xb @ w_gate[e]) * (xb @ w_up[e])) @ w_down[e]

    ys = lax.map(expert_rows, (xs.reshape(n_blocks, MOE_BLOCK, D), block_e)).reshape(n_rows, D)
    contrib = ys[dest] * topw.reshape(TK)[order][:, None].astype(ys.dtype)
    return jax.ops.segment_sum(contrib, tok, num_segments=T).reshape(B, S, D)

def setup_inputs(seed: int = 0) -> dict:
    key = jax.random.key(seed)
    ks = jax.random.split(key, 26)
    f32 = jnp.float32
    nrm = lambda k, shape, scale: jax.random.normal(k, shape, f32) * scale
    W = LRU_WIDTH
    u = jax.random.uniform(ks[13], (DEPTH, W), f32, minval=0.9, maxval=0.999) ** (1.0 / LRU_C)
    offsets = jax.random.randint(ks[1], (BATCH, 1), 0, 4096, dtype=jnp.int32)
    res_scale = (2 * DEPTH) ** -0.5
    return {
        'x': nrm(ks[0], (BATCH, SEQ, D_MODEL), 1.0),
        'positions': offsets + jnp.arange(SEQ, dtype=jnp.int32)[None, :],
        'norm1_gain': 1.0 + nrm(ks[2], (DEPTH, D_MODEL), 0.02),
        'w_in': nrm(ks[3], (DEPTH, D_MODEL, IN_COLS), D_MODEL ** -0.5),
        'gla_gate_up': nrm(ks[4], (DEPTH, GLA_GATE_RANK, GLA_HEADS * GLA_KEY_DIM), GLA_GATE_RANK ** -0.5),
        'gla_gate_bias': nrm(ks[5], (DEPTH, GLA_HEADS * GLA_KEY_DIM), 0.1),
        'gla_out_gain': 1.0 + nrm(ks[6], (DEPTH, GLA_VALUE_DIM), 0.02),
        'lru_conv_w': nrm(ks[7], (DEPTH, LRU_CONV_WIDTH, W), LRU_CONV_WIDTH ** -0.5),
        'lru_conv_b': nrm(ks[8], (DEPTH, W), 0.02),
        'lru_w_a': nrm(ks[9], (DEPTH, LRU_BLOCKS, W // LRU_BLOCKS, W // LRU_BLOCKS), (W // LRU_BLOCKS) ** -0.5),
        'lru_b_a': nrm(ks[10], (DEPTH, W), 0.02),
        'lru_w_x': nrm(ks[11], (DEPTH, LRU_BLOCKS, W // LRU_BLOCKS, W // LRU_BLOCKS), (W // LRU_BLOCKS) ** -0.5),
        'lru_b_x': nrm(ks[12], (DEPTH, W), 0.02),
        'lru_lambda': jnp.log(u) - jnp.log1p(-u),
        'q_norm_gain': 1.0 + nrm(ks[14], (DEPTH, DIL_HEAD_DIM), 0.02),
        'k_norm_gain': 1.0 + nrm(ks[15], (DEPTH, DIL_HEAD_DIM), 0.02),
        'w_branch': nrm(ks[16], (DEPTH, N_BRANCHES, BRANCH_WIDTH, D_MODEL), BRANCH_WIDTH ** -0.5),
        'w_out': nrm(ks[17], (DEPTH, D_MODEL, D_MODEL), D_MODEL ** -0.5 * res_scale),
        'norm2_gain': 1.0 + nrm(ks[18], (DEPTH, D_MODEL), 0.02),
        'router_w': nrm(ks[19], (D_MODEL, N_EXPERTS), D_MODEL ** -0.5),
        'router_b': nrm(ks[20], (N_EXPERTS,), 0.01),
        'w_gate': nrm(ks[21], (DEPTH, N_EXPERTS, D_MODEL, EXPERT_FF), D_MODEL ** -0.5),
        'w_up': nrm(ks[22], (DEPTH, N_EXPERTS, D_MODEL, EXPERT_FF), D_MODEL ** -0.5),
        'w_down': nrm(ks[23], (DEPTH, N_EXPERTS, EXPERT_FF, D_MODEL), EXPERT_FF ** -0.5 * res_scale),
    }

def reference(x, positions, norm1_gain, w_in, gla_gate_up, gla_gate_bias, gla_out_gain, lru_conv_w,
              lru_conv_b, lru_w_a, lru_b_a, lru_w_x, lru_b_x, lru_lambda, q_norm_gain, k_norm_gain,
              w_branch, w_out, norm2_gain, router_w, router_b, w_gate, w_up, w_down):
    for l in range(DEPTH):
        h = rmsnorm(x, norm1_gain[l])
        x = x + mixer_block(h, positions, w_in[l], gla_gate_up[l], gla_gate_bias[l], gla_out_gain[l],
                            lru_conv_w[l], lru_conv_b[l], lru_w_a[l], lru_b_a[l], lru_w_x[l], lru_b_x[l],
                            lru_lambda[l], q_norm_gain[l], k_norm_gain[l], w_branch[l], w_out[l])
        h = rmsnorm(x, norm2_gain[l])
        x = x + moe_ffn(h, router_w, router_b, w_gate[l], w_up[l], w_down[l])
    return x


_drawn_inputs = setup_inputs


def setup_inputs(seed=0):
    import zlib

    import numpy as np

    out = dict(_drawn_inputs(seed))
    spreads = {}
    factors = {'lru_b_a': 8.0, 'lru_b_x': 8.0, 'q_norm_gain': 8.0, 'k_norm_gain': 8.0}
    for name, (base, spread) in spreads.items():
        noise = np.random.default_rng([zlib.crc32(name.encode()), seed]).standard_normal(out[name].shape)
        drawn = base * np.exp(spread * noise) if base else spread * noise
        out[name] = __import__('jax').numpy.asarray(drawn.astype(out[name].dtype))
    for name, factor in factors.items():
        out[name] = (out[name] * factor).astype(out[name].dtype)
    return out
```

```python
from contextlib import ExitStack

import numpy as np
import concourse.bass as bass
from concourse import mybir

F32 = mybir.dt.float32
I32 = mybir.dt.int32
ALU = mybir.AluOpType
ACT = mybir.ActivationFunctionType
AX = mybir.AxisListType

P = 128
D = 1024
T = 256
NT = T // P
DC = D // P
DEPTH = 2
EPS = 1e-6
HG, DK, DV, CH = 4, 64, 128, 64
RANK = 16
W = 512
WC = W // P
TAPS = 4
NPAT, NH, DH = 3, 4, 128
PATTERNS = ((128, 1), (512, 4), (2048, 16))
ROPE = 16
THETA = 500000.0
ASCALE = float(DH) ** -0.5
NE, NG, FF = 16, 4, 512
FC = FF // P
CAP = 64
PAIRS = NE // 2
NPASS = T // CAP
RING = 6
BASE = 1
UNIT = 4096
BLK = 1024

C_QK, C_VA, C_OG, C_LOW = 0, 512, 1024, 1536
C_XB = C_LOW + RANK
C_YB = C_XB + W
C_Q = C_YB + W
C_K = C_Q + NPAT * 512
C_V = C_K + NPAT * 512
C_G = C_V + NPAT * 512

MIXER_UNITS = ([("in", C_QK), ("in", C_VA), ("in", C_XB), ("in", C_YB), ("in", C_OG)]
               + [("in", C_Q + 512 * p) for p in range(NPAT)]
               + [("in", C_K + 512 * p) for p in range(NPAT)]
               + [("in", C_V + 512 * p) for p in range(NPAT)]
               + [("in", C_G), ("branch", 0), ("in", C_G + 512),
                  ("in", C_G + 1024), ("branch", 1), ("in", C_G + 1536),
                  ("in", C_G + 2048), ("in", C_G + 2560), ("branch", 2),
                  ("out", 0), ("out", 1)])
MIX_USES = [len(MIXER_UNITS[s::RING]) for s in range(RING)]
UNIT_JOBS = list(range(2, 16)) + [16, 19, 18, 20, 23, 22, 24, 25, 27, 29, 29]
GATE, UP, DOWN = (0, 1), (2, 3), (4, 5)

J_NORM1, J_QK, J_VA, J_XB, J_YB, J_OG, J_Q, J_K, J_V, J_G = 0, 2, 3, 4, 5, 6, 7, 10, 13, 16
GATE_JOBS = (("g", 0, 0), ("p", 0, 0), ("g", 0, 1), ("p", 0, 1),
             ("g", 1, 0), ("p", 1, 0), ("g", 1, 1), ("p", 1, 1),
             ("g", 2, 0), ("g", 2, 1), ("p", 2, 0), ("p", 2, 1))
J_OUT = J_G + len(GATE_JOBS)
J_NORM2 = J_OUT + NT
JOBS = J_NORM2 + NT
STEPS = NH * NT


def columns(widths):
    out, at = {}, 0
    for name, width in widths:
        out[name] = (at, at + width)
        at += width
    return out, at


CONST, NCONST = columns([
    ("ident", P), ("mean", P), ("ones", P), ("before", P), ("gla_mask", P), ("reset", NT * T),
    ("band0", NPAT * P), ("band1", NPAT * T), ("iota", T + CAP), ("caps", NPASS), ("key4", NG), ("key16", NE),
    ("freq", ROPE), ("eps", 1), ("one", 1), ("router_w", DC * NE), ("router_b", NE)])
PAR, NPAR = columns([
    ("gain1", DC), ("gate_b", 2), ("out_gain", 1), ("conv_w", TAPS * WC), ("conv_b", WC), ("b_a", WC),
    ("b_x", WC), ("lam", WC), ("w_a", WC * P), ("w_x", WC * P), ("q_gain", P), ("k_gain", P),
    ("low", DC * RANK), ("gate_up", 2 * P)])


def build(nc, x, positions, const, par, gain2, w_in, w_branch, w_out, w_gate, w_up, w_down, out):
    with ExitStack() as ctx:
        def sb(name, shape, dt=F32):
            return ctx.enter_context(nc.sbuf_tensor(name, shape, dt))

        class Signal:

            def __init__(self, name, per, base=0):
                self.sem = ctx.enter_context(nc.semaphore(name))
                self.per = per
                self.base = base

            def at(self, l, k):
                return l * self.per + k + self.base

        def sem(name):
            return ctx.enter_context(nc.semaphore(name))

        ring = sb("ring", [P, RING, UNIT])
        arena = sb("arena", [P, 16 * BLK])
        hn = sb("hn", [P, NT * D])
        hT = sb("hT", [P, DC, T])
        xs = sb("xs", [P, NT, D])
        cst = sb("cst", [P, NCONST])
        prm = sb("prm", [P, NPAR])
        g2 = sb("g2", [P, DC])
        rope_tmp = sb("rope_tmp", [P, 4, P])
        cosb = sb("cosb", [P, NT, ROPE])
        sinb = sb("sinb", [P, NT, ROPE])
        small = sb("small", [P, 96])
        pairs_end = sb("pairs_end", [1, 1], I32)
        pos_i = sb("pos_i", [P, NT], I32)

        slotp = [ctx.enter_context(nc.psum_tensor(f"slot{i}", [P, 1024], F32)) for i in range(2)]
        M0 = ctx.enter_context(nc.psum_tensor("M0", [P, 1024], F32))
        M1 = ctx.enter_context(nc.psum_tensor("M1", [P, 1024], F32))

        def c(name):
            a, b = CONST[name]
            return cst[:, a:b]

        def q(name):
            a, b = PAR[name]
            return prm[:, a:b]

        def blk(i, n=1, off=0, width=None):
            a = i * BLK + off
            return arena[:, a:a + (width or n * BLK)]

        def h0(a, b):
            return hn[:, a:b]

        ident, ones = c("ident"), c("ones")
        eps, one = c("eps"), c("one")

        qk_raw = [blk(u) for u in range(2 * NPAT)]
        xc, gate_r, tanh_y, gate_i = blk(3), blk(4), blk(5), blk(6)
        xpad = arena[:, 7 * BLK:7 * BLK + WC * (T + TAPS - 1)].rearrange("p (c t) -> p c t", c=WC)
        a_sq = arena[:, 7 * BLK:8 * BLK]
        k_dec = blk(8, off=512, width=512)
        kdT = k_dec
        br = [blk(9), blk(10), blk(11)]
        qk_ch, sq_att = blk(11), blk(11)
        va, og = blk(12), blk(13)
        gsc, gsq = blk(14), blk(15)
        la, cum = h0(0, 512), h0(512, 1024)
        q_dec, k_inv = h0(1024, 1536), h0(1536, 2048)
        state = h0(0, 768)
        v_att = [blk(6), blk(7), blk(8)]
        merged = blk(12, 2)
        sig = [blk(14), blk(15)]
        sc = h0(0, 768)
        prob = h0(1024, 1792)
        wa0 = PAR["w_a"][0]
        probT = prm[:, wa0:wa0 + 768]
        xgT = blk(0).rearrange("p (c s) -> p c s", c=DC)
        sel = blk(1, width=256)
        selw = blk(1, off=256, width=256)
        selT = blk(1, off=512, width=256)
        silu_g = blk(2, width=FF)
        hs = blk(2, off=FF, width=FF)
        hTs = blk(3, width=FC * P)
        ysb = blk(4)
        rank2 = blk(6, width=NE * NT).rearrange("p (e t) -> p e t", e=NE)
        gw2 = blk(6, off=64, width=NE * NT).rearrange("p (e t) -> p e t", e=NE)

        def rt(i, n=NT * NE):
            return blk(5, off=32 * i, width=n)

        ss, sd, rinv = small[:, 0:2], small[:, 2:4], small[:, 4:6]
        etot = small[:, 6:14]
        asum, asd, arinv = small[:, 14:22], small[:, 22:30], small[:, 30:38]
        amax, anegm, aden, arden = (small[:, 38 + i:39 + i] for i in range(4))
        posf = small[:, 42:44]
        spz, sps, sp2, spp, sp_neg, sp_pos = (small[:, 44 + 4 * i:48 + 4 * i] for i in range(6))
        total_pairs = small[0:1, 68:69]
        npass = small[0:1, 69:70]
        cmp4 = small[0:1, 70:74]
        mxc = small[0:1, 74:75]

        loaded = [sem(f"loaded{s}") for s in range(RING)]
        consts_in, x_in, x_out = sem("consts_in"), sem("x_in"), sem("x_out")
        par_in, gain2_in = sem("par_in"), sem("gain2_in")
        setup_step, setup_act, rope_ready = sem("setup_step"), sem("setup_act"), sem("rope_ready")
        pairs_known = sem("pairs_known")
        job_done = Signal("job_done", JOBS)
        taken = [Signal(f"taken{i}", JOBS // 2, BASE) for i in range(2)]
        dve_step = Signal("dve_step", 126)
        rms_sq, rms_sd, hn_ready = Signal("rms_sq", 4), Signal("rms_sd", 2), Signal("hn_ready", 4)
        low_ps, low_sb, z_ps = Signal("low_ps", 1), Signal("low_sb", 1), Signal("z_ps", 1)
        z_abs, decay_exp, decay_ln = Signal("z_abs", 1), Signal("decay_exp", 1), Signal("decay_ln", 1)
        cum_ready, exps_ready, gqk_ready = Signal("cum_ready", 1), Signal("exps_ready", 1), Signal("gqk_ready", 1)
        gsc_ps, gsc_sb = Signal("gsc_ps", 1), Signal("gsc_sb", 1)
        kdT_ps, kdT_sb = Signal("kdT_ps", 1), Signal("kdT_sb", 1)
        kv_ps, state_ready = Signal("kv_ps", 1), Signal("state_ready", 1)
        go_ps, go_sq, gmean_ps, grms = Signal("go_ps", 1), Signal("go_sq", 1), Signal("gmean_ps", 1), Signal("grms", 1)
        brA_ready = Signal("brA_ready", 1)
        lam_abs, lam_exp, lam_ready = Signal("lam_abs", 1), Signal("lam_exp", 1), Signal("lam_ready", 1)
        pad_ready, xc_ready = Signal("pad_ready", 1), Signal("xc_ready", 1)
        lru_ps, lru_sig, lru_at = Signal("lru_ps", 2), Signal("lru_sig", 2), Signal("lru_at", 1)
        lru_m, lru_sqrt, brB_ready = Signal("lru_m", 1), Signal("lru_sqrt", 1), Signal("brB_ready", 1)
        att_sq, att_sum, att_sd, att_in = Signal("att_sq", 6), Signal("att_sum", 6), Signal("att_sd", 6), Signal("att_in", 6)
        attT_ps, attT_sb = Signal("attT_ps", 6), Signal("attT_sb", 6)
        sc_ps, sc_sb, sc_max, sc_exp, prob_ready = (Signal(n, STEPS) for n in
                                                    ("sc_ps", "sc_sb", "sc_max", "sc_exp", "prob_ready"))
        probT_ps, probT_sb, ao_ps, ao_sb = (Signal(n, STEPS) for n in ("probT_ps", "probT_sb", "ao_ps", "ao_sb"))
        merged_ready = Signal("merged_ready", 4)
        logit_ps, rt_max, rt_exp = Signal("logit_ps", 1), Signal("rt_max", 1), Signal("rt_exp", 1)
        member_ready, rank_ps = Signal("member_ready", 1), Signal("rank_ps", 1)
        sel_ready, sel_hot, xg_ps, xg_sb = sem("sel_ready"), sem("sel_hot"), sem("xg_ps"), sem("xg_sb")
        gate_ps, gu_ps, silu_ready, h_ready = sem("gate_ps"), sem("gu_ps"), sem("silu_ready"), sem("h_ready")
        hT_ps, hT_sb, selT_ps, selT_sb = sem("hT_ps"), sem("hT_sb"), sem("selT_ps"), sem("selT_sb")
        y_ps, y_sb, mix_ps = sem("y_ps"), sem("y_sb"), sem("mix_ps")
        x_add = [sem(f"x_add{t}") for t in range(NT)]
        slot_done = (gate_ps, gate_ps, gu_ps, gu_ps, y_ps, y_ps)

        block = ctx.enter_context(nc.Block())

        settled = sem("settled")

        def settle(eng):
            eng.sem_inc(settled, 1)

        def uses(slot, l, start, k):
            return l * MIX_USES[slot] + start + k

        @block.sync
        def _(sp):
            sp.dma_start(cst[:, :], const).then_inc(consts_in, 16)
            sp.dma_start(xs[:, :, :], x.rearrange("b (t p) d -> p (b t) d", p=P)).then_inc(x_in, 16)
            sp.dma_start(prm[:, :], par[0]).then_inc(par_in, 16)
            sp.dma_start(g2[:, :], gain2[0]).then_inc(gain2_in, 16)
            sp.dma_start(pos_i[:, :], positions.rearrange("b (t p) -> p (b t)", p=P),
                         allow_slow_non_contiguous=True).then_inc(consts_in, 16)

            with sp.Fori(0, DEPTH) as l:
                sp.wait_ge(pairs_known, l + 1)
                settle(sp)
                start = sp.value_load(pairs_end[0:1, 0:1], min_val=0, max_val=DEPTH * NPASS * PAIRS)

                def mixer_unit(k):
                    slot = k % RING
                    kind, at = MIXER_UNITS[k]
                    if k < RING:
                        sp.wait_ge(slot_done[slot], start + BASE)
                    else:
                        sp.wait_ge(job_done.sem, job_done.at(l, UNIT_JOBS[k - RING] + 1))
                    settle(sp)
                    dst = ring[:, slot, :]
                    if kind == "in":
                        src = w_in[bass.ds(l, 1), :, at:at + 512].rearrange("o (c p) n -> p (o c) n", p=P)
                        dst = dst.rearrange("p (c n) -> p c n", c=DC)
                    elif kind == "branch":
                        src = w_branch[bass.ds(l, 1), at].rearrange("o (c p) n -> p (o c) n", p=P)
                        dst = dst.rearrange("p (c n) -> p c n", c=WC)
                    else:
                        src = w_out[bass.ds(l, 1), at * 512:(at + 1) * 512].rearrange("o (c p) n -> p (o c) n", p=P)
                        dst = dst.rearrange("p (c n) -> p c n", c=WC)
                    sp.dma_start(dst, src).then_inc(loaded[slot], 16)

                for k in range(len(MIXER_UNITS)):
                    mixer_unit(k)

                def expert_weights(slot, it):
                    w = (w_gate, w_up, w_down)[slot // 2]
                    e = 2 * (it % PAIRS) + slot % 2
                    rows = FC if slot in DOWN else DC
                    src = w[bass.ds(l, 1), bass.ds(e, 1)].rearrange("o e (c p) n -> p (o e c) n", p=P)
                    sp.dma_start(ring[:, slot, :].rearrange("p (c n) -> p c n", c=rows), src)\
                        .then_inc(loaded[slot], 16)

                last_unit = [max(k for k in range(len(MIXER_UNITS)) if k % RING == slot) for slot in range(RING)]
                for slot in sorted(range(RING), key=lambda slot: UNIT_JOBS[last_unit[slot]]):
                    sp.wait_ge(job_done.sem, job_done.at(l, UNIT_JOBS[last_unit[slot]] + 1))
                    settle(sp)
                    expert_weights(slot, start)

                def pair(it):
                    for slot in range(RING):
                        sp.wait_ge(slot_done[slot], it + BASE)
                        settle(sp)
                        expert_weights(slot, it)

                with sp.Fori(start + 1, start + PAIRS) as it:
                    pair(it)
                sp.wait_ge(job_done.sem, job_done.at(l, JOBS))
                settle(sp)
                nxt = (l + 1) % DEPTH
                sp.wait_ge(pairs_known, l + 2)
                sp.dma_start(prm[:, :], par[bass.ds(nxt, 1)].rearrange("o p n -> p (o n)")).then_inc(par_in, 16)
                settle(sp)
                end = sp.value_load(pairs_end[0:1, 0:1], min_val=0, max_val=DEPTH * NPASS * PAIRS)
                with sp.If(end > start + PAIRS):
                    with sp.Fori(start + PAIRS, end) as it:
                        pair(it)
                sp.wait_ge(x_add[NT - 1], end + BASE)
                sp.dma_start(g2[:, :], gain2[bass.ds(nxt, 1)].rearrange("o p n -> p (o n)")).then_inc(gain2_in, 16)

            sp.dma_start(out.rearrange("b (t p) d -> p (b t) d", p=P), xs[:, :, :]).then_inc(x_out, 16)
            sp.wait_ge(x_out, 16)
            sp.wait_ge(par_in, 16 * (DEPTH + 1))
            sp.wait_ge(gain2_in, 16 * (DEPTH + 1))

        @block.tensor
        def _(pe):
            mm = nc.tensor.matmul
            for s in (taken[0].sem, taken[1].sem, *x_add, gate_ps, gu_ps, y_ps, selT_ps, xg_ps, xg_sb, mix_ps):
                pe.sem_inc(s, BASE)
            pe.wait_ge(consts_in, 32)

            with pe.Fori(0, DEPTH) as l:
                pe.wait_ge(pairs_known, l + 1)
                settle(pe)
                start = pe.value_load(pairs_end[0:1, 0:1], min_val=0, max_val=DEPTH * NPASS * PAIRS)
                for t in range(NT):
                    pe.wait_ge(x_add[t], start + BASE)
                pe.wait_ge(par_in, 16 * l + 16)

                def weights(k, rows):
                    slot = k % RING
                    pe.wait_ge(loaded[slot], 16 * uses(slot, l, start, k // RING + 1))
                    return ring[:, slot, :].rearrange("p (c n) -> p c n", c=rows)

                def taken_wait(j):
                    pe.wait_ge(taken[j % 2].sem, taken[j % 2].at(l, j // 2 + 1))

                def open_slot(j):
                    pe.wait_ge(taken[j % 2].sem, taken[j % 2].at(l, j // 2))
                    return slotp[j % 2]

                def transposes(j, n):
                    o = open_slot(j)
                    t = j - (J_NORM1, J_NORM2)[n]
                    pe.wait_ge(hn_ready.sem, hn_ready.at(l, NT * n + t + 1))
                    for cc in range(DC):
                        last = nc.tensor.transpose(o[:, cc * P:(cc + 1) * P],
                                                   hn[:, t * D + cc * P:t * D + (cc + 1) * P], ident)
                    last.then_inc(job_done.sem, 1)

                def channel_major(j, k, rhs, rows, col0=0, free=True, middle=None):
                    wv = weights(k, rows)
                    o = open_slot(j)
                    for m in range(4):
                        for cc in range(rows):
                            last = mm(o[:, m * T:(m + 1) * T], wv[:, cc, col0 + m * P:col0 + (m + 1) * P],
                                      rhs[:, cc, :], start=cc == 0, stop=cc == rows - 1)
                        if m == 1 and middle:
                            middle()
                    last.then_inc(job_done.sem, 1)

                def time_major(j, k):
                    wv = weights(k, DC)
                    o = open_slot(j)
                    for t in range(NT):
                        for cc in range(DC):
                            last = mm(o[:, t * 512:(t + 1) * 512], hT[:, cc, t * P:(t + 1) * P], wv[:, cc, :],
                                      start=cc == 0, stop=cc == DC - 1)
                    last.then_inc(job_done.sem, 1)

                for j in (0, 1):
                    transposes(j, 0)
                taken_wait(0)
                taken_wait(1)

                channel_major(J_QK, 0, hT, DC)
                low = q("low").rearrange("p (c r) -> p c r", c=DC)
                for cc in range(DC):
                    last = mm(M0[0:RANK, 512:512 + T], low[:, cc, :], hT[:, cc, :], start=cc == 0, stop=cc == DC - 1)
                last.then_inc(low_ps.sem, 1)
                time_major(J_VA, 1)
                pe.wait_ge(low_sb.sem, low_sb.at(l, 1))
                a = PAR["gate_up"][0]
                for g in range(2):
                    last = mm(M0[:, g * T:(g + 1) * T], prm[0:RANK, a + g * P:a + (g + 1) * P],
                              h0(0, T)[0:RANK, :], start=True, stop=True)
                last.then_inc(z_ps.sem, 1)
                for j, k in ((J_XB, 2), (J_YB, 3)):
                    channel_major(j, k, hT, DC)
                xcv = xc.rearrange("p (c t) -> p c t", c=WC)

                def lru_gates(name, dst):
                    wv = q(name).rearrange("p (c n) -> p c n", c=WC)
                    for cc in range(WC):
                        last = mm(dst[:, cc * T:(cc + 1) * T], wv[:, cc, :], xcv[:, cc, :], start=True, stop=True)
                    last.then_inc(lru_ps.sem, 1)

                pe.wait_ge(xc_ready.sem, xc_ready.at(l, 1))
                lru_gates("w_a", M1)
                channel_major(J_OG, 4, hT, DC)
                pe.wait_ge(z_abs.sem, z_abs.at(l, 1))
                lru_gates("w_x", M0)

                time_major(J_Q, 5)
                pe.wait_ge(gqk_ready.sem, gqk_ready.at(l, 1))
                pe.wait_ge(lru_sig.sem, lru_sig.at(l, 1))
                for hh in range(2):
                    for g in range(2):
                        for t in range(NT):
                            cols = slice(g * T + t * P, g * T + (t + 1) * P)
                            last = mm(M1[:, (hh * 4 + g * 2 + t) * P:(hh * 4 + g * 2 + t + 1) * P],
                                      k_inv[hh * DK:(hh + 1) * DK, cols], q_dec[hh * DK:(hh + 1) * DK, cols],
                                      start=True, stop=True)
                last.then_inc(gsc_ps.sem, 1)
                pe.wait_ge(lru_sig.sem, lru_sig.at(l, 2))
                for i in range(4):
                    last = nc.tensor.transpose(M0[:, i * P:(i + 1) * P], k_dec[:, i * P:(i + 1) * P], ident)
                last.then_inc(kdT_ps.sem, 1)

                time_major(J_Q + 1, 6)
                pe.wait_ge(kdT_sb.sem, kdT_sb.at(l, 1))
                settle(pe)
                for n in (0, 2, 1):
                    b = (n % 2) * CH
                    for g in range(2):
                        col = (512 if n % 2 == 0 else 0) + (n // 2 * 2 + g) * P
                        for hh in range(2):
                            kd = kdT[b:b + CH, (g * 2 + n // 2) * P + hh * DK:(g * 2 + n // 2) * P + (hh + 1) * DK]
                            vv = va[b:b + CH, (n // 2) * 512 + (2 * g + hh) * DV:(n // 2) * 512 + (2 * g + hh + 1) * DV]
                            last = mm(M0[hh * DK:(hh + 1) * DK, col:col + DV], kd, vv, start=True, stop=True)
                last.then_inc(kv_ps.sem, 1)

                time_major(J_Q + 2, 7)
                pe.wait_ge(gsc_sb.sem, gsc_sb.at(l, 1))
                pe.wait_ge(state_ready.sem, state_ready.at(l, 1))
                for hh in range(2):
                    for g in range(2):
                        for t in range(NT):
                            o = M1[:, (hh * 4 + g * 2 + t) * P:(hh * 4 + g * 2 + t + 1) * P]
                            hd = 2 * g + hh
                            last = mm(o, va[:, t * 512 + hd * DV:t * 512 + (hd + 1) * DV],
                                      gsc[:, (hh * 4 + g * 2 + t) * P:(hh * 4 + g * 2 + t + 1) * P],
                                      start=True, stop=False, skip_group_check=True)
                            for n in range(2 * t, 2 * t + 2):
                                if n:
                                    last = mm(M1[:, (hh * 4 + g * 2) * P + n * CH:(hh * 4 + g * 2) * P + (n + 1) * CH],
                                              state[hh * DK:(hh + 1) * DK, (g * 3 + n - 1) * DV:(g * 3 + n) * DV],
                                              q_dec[hh * DK:(hh + 1) * DK, g * T + n * CH:g * T + (n + 1) * CH],
                                              start=False, stop=n == 2 * t + 1, skip_group_check=True)
                last.then_inc(go_ps.sem, 1)

                time_major(J_K, 8)
                pe.wait_ge(go_sq.sem, go_sq.at(l, 1))
                for i in range(2):
                    last = mm(M0[:, i * 512:(i + 1) * 512], c("mean"), gsq[:, i * 512:(i + 1) * 512],
                              start=True, stop=True)
                last.then_inc(gmean_ps.sem, 1)

                def att_transposes(u):
                    dst = (M1, M0)[u % 2]
                    if u == 0:
                        pe.wait_ge(brA_ready.sem, brA_ready.at(l, 1))
                    if u == 1:
                        pe.wait_ge(grms.sem, grms.at(l, 1))
                    if u >= 2:
                        pe.wait_ge(attT_sb.sem, attT_sb.at(l, u - 1))
                    pe.wait_ge(att_in.sem, att_in.at(l, u + 1))
                    for h in range(NH):
                        for t in range(NT):
                            last = nc.tensor.transpose(dst[:, h * T + t * P:h * T + (t + 1) * P],
                                                       qk_raw[u][:, t * 512 + h * P:t * 512 + (h + 1) * P], ident)
                    last.then_inc(attT_ps.sem, 1)

                for u, j in enumerate(range(J_K + 1, J_G)):
                    time_major(j, j - 2)
                    att_transposes(u)
                att_transposes(5)

                def att_scores(s):
                    h, t = s // NT, s % NT
                    wide = (t + 1) * P
                    if s == 0:
                        pe.wait_ge(attT_sb.sem, attT_sb.at(l, 6))
                    if s >= 1:
                        pe.wait_ge(sc_sb.sem, sc_sb.at(l, s))
                    if s >= 2:
                        pe.wait_ge(ao_sb.sem, ao_sb.at(l, s - 1))
                    for p in range(NPAT):
                        last = mm(M0[:, p * wide:(p + 1) * wide],
                                  qk_raw[p][:, h * T + t * P:h * T + (t + 1) * P],
                                  qk_raw[NPAT + p][:, h * T:h * T + wide], start=True, stop=True)
                    last.then_inc(sc_ps.sem, 1)

                def att_prob_transposes(s):
                    t = s % NT
                    pe.wait_ge(prob_ready.sem, prob_ready.at(l, s + 1))
                    if s >= 1:
                        pe.wait_ge(probT_sb.sem, probT_sb.at(l, s))
                    for i in range(NPAT * (t + 1)):
                        last = nc.tensor.transpose(M1[:, i * P:(i + 1) * P], prob[:, i * P:(i + 1) * P], ident)
                    last.then_inc(probT_ps.sem, 1)

                def att_out(s):
                    h, t = s // NT, s % NT
                    pe.wait_ge(probT_sb.sem, probT_sb.at(l, s + 1))
                    pe.wait_ge(sc_sb.sem, sc_sb.at(l, min(s + 2, STEPS)))
                    n = NPAT * (t + 1)
                    for i in range(n):
                        p, kt = i // (t + 1), i % (t + 1)
                        last = mm(M0[:, 896:1024], v_att[p][:, kt * 512 + h * P:kt * 512 + (h + 1) * P],
                                  probT[:, i * P:(i + 1) * P], start=i == 0, stop=i == n - 1, skip_group_check=True)
                    last.then_inc(ao_ps.sem, 1)

                unit = {("g", 0, 0): 14, ("p", 0): 15, ("g", 0, 1): 16, ("g", 1, 0): 17, ("p", 1): 18,
                        ("g", 1, 1): 19, ("g", 2, 0): 20, ("g", 2, 1): 21, ("p", 2): 22}
                for i, (kind, n, half) in enumerate(GATE_JOBS):
                    j = J_G + i
                    middle = (lambda s=i - 2: att_out(s)) if 0 <= i - 2 < STEPS else None
                    if kind == "g":
                        k = unit[kind, n, half]
                        channel_major(j, k, hT, DC, middle=middle)
                    else:
                        if n == 0 and half == 0:
                            pe.wait_ge(brA_ready.sem, brA_ready.at(l, 1))
                        if n == 1 and half == 0:
                            pe.wait_ge(brB_ready.sem, brB_ready.at(l, 1))
                        if n == 2 and half == 0:
                            pe.wait_ge(ao_sb.sem, ao_sb.at(l, STEPS))
                        k = unit[kind, n]
                        channel_major(j, k, br[n].rearrange("p (c t) -> p c t", c=WC), WC,
                                      col0=512 * half, middle=middle)
                    if 0 <= i - 1 < STEPS:
                        att_prob_transposes(i - 1)
                    if i < STEPS:
                        att_scores(i)

                wo = [weights(k, WC) for k in (23, 24)]
                mg = merged.rearrange("p (c t) -> p c t", c=DC)
                pe.wait_ge(merged_ready.sem, merged_ready.at(l, 4))
                for t in range(NT):
                    o = open_slot(J_OUT + t)
                    for half in range(2):
                        for cc in range(DC):
                            last = mm(o[:, half * 512:(half + 1) * 512], mg[:, cc, t * P:(t + 1) * P],
                                      wo[cc // 4][:, cc % 4, half * 512:(half + 1) * 512],
                                      start=cc == 0, stop=cc == DC - 1)
                    last.then_inc(job_done.sem, 1)

                for t in range(NT):
                    transposes(J_NORM2 + t, 1)
                taken_wait(J_NORM2)
                taken_wait(J_NORM2 + 1)
                rw = c("router_w").rearrange("p (c e) -> p c e", c=DC)
                for t in range(NT):
                    for cc in range(DC):
                        last = mm(M0[:, t * NE:(t + 1) * NE], hT[:, cc, t * P:(t + 1) * P], rw[:, cc, :],
                                  start=cc == 0, stop=cc == DC - 1)
                last.then_inc(logit_ps.sem, 1)
                pe.wait_ge(member_ready.sem, member_ready.at(l, 1))
                member = rt(0)
                mm(M1[:, 0:NE], c("before"), member[:, 0:NE], start=True, stop=True)
                mm(M1[:, NE:2 * NE], c("before"), member[:, NE:2 * NE], start=True, stop=False, skip_group_check=True)
                mm(M1[:, NE:2 * NE], ones, member[:, 0:NE], start=False, stop=True, skip_group_check=True)
                mm(M1[:, 512:512 + NE], ones, member[:, 0:NE], start=True, stop=False, skip_group_check=True)
                mm(M1[:, 512:512 + NE], ones, member[:, NE:2 * NE], start=False, stop=True,
                   skip_group_check=True).then_inc(rank_ps.sem, 1)

                G0, G1 = slotp

                def gather(n):
                    pe.wait_ge(sel_ready, n + 1)
                    pe.wait_ge(xg_sb, n + BASE)
                    for cc in range(DC):
                        for t in range(NT):
                            last = mm(G0[:, cc * P:(cc + 1) * P], hn[:, t * D + cc * P:t * D + (cc + 1) * P],
                                      sel[:, t * P:(t + 1) * P], start=t == 0, stop=t == NT - 1)
                    last.then_inc(xg_ps, 1)

                def expert_loaded(slot, it):
                    pe.wait_ge(loaded[slot], 16 * uses(slot, l, it, MIX_USES[slot] + 1))

                gather(start + l)
                pe.wait_ge(pairs_known, l + 2)
                settle(pe)
                end = pe.value_load(pairs_end[0:1, 0:1], min_val=0, max_val=DEPTH * NPASS * PAIRS)
                with pe.Fori(start, end) as it:
                    for t in range(NT):
                        last = nc.tensor.transpose(G1[:, t * P:(t + 1) * P], selw[:, t * P:(t + 1) * P], ident)
                    last.then_inc(selT_ps, 1)
                    pe.wait_ge(xg_sb, it + l + 1 + BASE)
                    pe.wait_ge(x_add[0], it + BASE)
                    for stage, slots in enumerate((GATE, UP)):
                        for cc in range(DC):
                            for i in range(2):
                                if cc == 0:
                                    expert_loaded(slots[i], it)
                                wv = ring[:, slots[i], :].rearrange("p (c n) -> p c n", c=DC)
                                last = mm(M0[i * CAP:(i + 1) * CAP, stage * FF:(stage + 1) * FF],
                                          xgT[:, cc, i * CAP:(i + 1) * CAP], wv[:, cc, :],
                                          start=cc == 0, stop=cc == DC - 1)
                        last.then_inc((gate_ps, gu_ps)[stage], 1)
                    gather(it + l + 1)
                    pe.wait_ge(h_ready, it + 1)
                    pe.wait_ge(x_add[1], it + BASE)
                    for f in range(FC):
                        last = nc.tensor.transpose(M1[:, FF + f * P:FF + (f + 1) * P], hs[:, f * P:(f + 1) * P], ident)
                    last.then_inc(hT_ps, 1)
                    pe.wait_ge(hT_sb, it + 1)
                    pe.wait_ge(selT_sb, it + 1)
                    for half in range(2):
                        for f in range(FC):
                            for i in range(2):
                                if half == 0 and f == 0:
                                    expert_loaded(DOWN[i], it)
                                wv = ring[:, DOWN[i], :].rearrange("p (c n) -> p c n", c=FC)
                                last = mm(G1[i * CAP:(i + 1) * CAP, half * 512:(half + 1) * 512],
                                          hTs[:, f * P + i * CAP:f * P + (i + 1) * CAP],
                                          wv[:, f, half * 512:(half + 1) * 512], start=f == 0, stop=f == FC - 1)
                    last.then_inc(y_ps, 1)
                    pe.wait_ge(y_sb, 2 * it + 2)
                    for t in range(NT):
                        o = (M0, M1)[t]
                        for half in range(2):
                            last = mm(o[:, half * 512:(half + 1) * 512], selT[:, t * P:(t + 1) * P],
                                      ysb[:, half * 512:(half + 1) * 512], start=True, stop=True)
                        last.then_inc(mix_ps, 1)

        @block.scalar
        def _(act):
            A = nc.scalar.activation
            act.wait_ge(setup_act, 1)
            A(sinb[:, :, :], sinb[:, :, :], ACT.Sin).then_inc(rope_ready, 1)
            A(cosb[:, :, :], cosb[:, :, :], ACT.Sin).then_inc(rope_ready, 1)
            act.wait_ge(x_in, 16)

            with act.Fori(0, DEPTH) as l:
                act.wait_ge(pairs_known, l + 1)
                settle(act)
                start = act.value_load(pairs_end[0:1, 0:1], min_val=0, max_val=DEPTH * NPASS * PAIRS)
                for t in range(NT):
                    act.wait_ge(x_add[t], start + BASE)
                act.wait_ge(par_in, 16 * l + 16)

                def done(j):
                    act.wait_ge(job_done.sem, job_done.at(l, j + 1))
                    return slotp[j % 2]

                def norm_stats(n):
                    for t in range(NT):
                        A((gsq, gsc)[t], xs[:, t, :], ACT.Square, accum_out=ss[:, t:t + 1]).then_inc(rms_sq.sem, 1)
                    act.wait_ge(rms_sq.sem, rms_sq.at(l, NT * n + NT))
                    A(sd, ss, ACT.Sqrt, bias=eps, scale=1.0 / D).then_inc(rms_sd.sem, 1)

                norm_stats(0)
                act.wait_ge(lam_abs.sem, lam_abs.at(l, 1))
                A(spz, spz, ACT.Exp, scale=-1.0).then_inc(lam_exp.sem, 1)

                o = done(J_QK)
                A(qk_ch[:, 0:512], o[:, 0:512], ACT.Copy, scale=DK ** -0.5)
                A(qk_ch[:, 512:1024], o[:, 512:1024], ACT.Copy).then_inc(taken[0].sem, 1)
                act.wait_ge(low_ps.sem, low_ps.at(l, 1))
                A(h0(0, T)[0:RANK, :], M0[0:RANK, 512:512 + T], ACT.Copy).then_inc(low_sb.sem, 1)
                o = done(J_VA)
                A(va, o[:, :], ACT.Copy).then_inc(taken[1].sem, 1)
                act.wait_ge(z_abs.sem, z_abs.at(l, 1))
                A(cum, cum, ACT.Exp, scale=-1.0).then_inc(decay_exp.sem, 1)
                act.wait_ge(decay_exp.sem, decay_exp.at(l, 1))
                A(cum, cum, ACT.Ln, bias=one).then_inc(decay_ln.sem, 1)
                o = done(J_XB)
                act.wait_ge(pad_ready.sem, pad_ready.at(l, 1))
                A(xpad[:, :, TAPS - 1:], o[:, :].rearrange("p (c t) -> p c t", c=WC), ACT.Copy)\
                    .then_inc(taken[0].sem, 1)
                act.wait_ge(cum_ready.sem, cum_ready.at(l, 1))
                A(q_dec, cum, ACT.Exp, scale=1.0 / 16)
                A(k_inv, cum, ACT.Exp, scale=-1.0 / 16)
                A(etot, cum.rearrange("p (n t) -> p n t", t=CH)[:, :, CH - 1], ACT.Exp, scale=1.0 / 16)
                A(k_dec, la, ACT.Exp, scale=-1.0 / 16).then_inc(exps_ready.sem, 1)
                o = done(J_YB)
                A(br[1], o[:, :], ACT.Gelu_apprx_tanh).then_inc(taken[1].sem, 1)
                act.wait_ge(lru_ps.sem, lru_ps.at(l, 1))
                for cc in range(WC):
                    w = A(gate_r[:, cc * T:(cc + 1) * T], M1[:, cc * T:(cc + 1) * T], ACT.Sigmoid,
                          bias=q("b_a")[:, cc:cc + 1])
                w.then_inc(lru_sig.sem, 1)
                o = done(J_OG)
                A(og, o[:, :], ACT.Silu).then_inc(taken[0].sem, 1)
                act.wait_ge(lru_ps.sem, lru_ps.at(l, 2))
                for cc in range(WC):
                    w = A(gate_i[:, cc * T:(cc + 1) * T], M0[:, cc * T:(cc + 1) * T], ACT.Sigmoid,
                          bias=q("b_x")[:, cc:cc + 1])
                w.then_inc(lru_sig.sem, 1)
                act.wait_ge(lru_sig.sem, lru_sig.at(l, 2))
                act.wait_ge(lam_ready.sem, lam_ready.at(l, 1))
                for cc in range(WC):
                    A(tanh_y[:, cc * T:(cc + 1) * T], gate_r[:, cc * T:(cc + 1) * T], ACT.Tanh,
                      scale=sp_pos[:, cc:cc + 1])
                for cc in range(WC):
                    w = A(gate_r[:, cc * T:(cc + 1) * T], gate_r[:, cc * T:(cc + 1) * T], ACT.Exp,
                          scale=sp_neg[:, cc:cc + 1])
                w.then_inc(lru_at.sem, 1)
                act.wait_ge(lru_m.sem, lru_m.at(l, 1))
                A(tanh_y, tanh_y, ACT.Sqrt).then_inc(lru_sqrt.sem, 1)

                def take_qk(u):
                    j = J_Q + u
                    o = done(j)
                    if u == 3:
                        act.wait_ge(brB_ready.sem, brB_ready.at(l, 1))
                    A(qk_raw[u], o[:, :], ACT.Copy).then_inc(taken[j % 2].sem, 1)
                    if u == 0:
                        act.wait_ge(gqk_ready.sem, gqk_ready.at(l, 1))
                    else:
                        act.wait_ge(att_sum.sem, att_sum.at(l, u))
                    act.wait_ge(taken[j % 2].sem, taken[j % 2].at(l, j // 2 + 1))
                    A(sq_att, qk_raw[u], ACT.Square).then_inc(att_sq.sem, 1)
                    act.wait_ge(att_sum.sem, att_sum.at(l, u + 1))
                    A(asd, asum, ACT.Sqrt, bias=eps, scale=1.0 / DH).then_inc(att_sd.sem, 1)

                take_qk(0)
                act.wait_ge(kdT_ps.sem, kdT_ps.at(l, 1))
                A(kdT, M0[:, 0:512], ACT.Copy).then_inc(kdT_sb.sem, 1)
                take_qk(1)
                take_qk(2)
                act.wait_ge(go_ps.sem, go_ps.at(l, 1))
                A(gsq, M1[:, :], ACT.Square).then_inc(go_sq.sem, 1)
                take_qk(3)
                act.wait_ge(gmean_ps.sem, gmean_ps.at(l, 1))
                A(gsq, M0[:, :], ACT.Sqrt, bias=eps).then_inc(grms.sem, 1)
                for u in range(6):
                    j = J_K + 1 + u
                    if u < 2:
                        take_qk(4 + u)
                    elif j < J_G:
                        o = done(j)
                        A(v_att[u - 2], o[:, :], ACT.Copy).then_inc(taken[j % 2].sem, 1)
                    act.wait_ge(attT_ps.sem, attT_ps.at(l, u + 1))
                    A(qk_raw[u], (M1, M0)[u % 2][:, :], ACT.Copy).then_inc(attT_sb.sem, 1)

                for i in range(len(GATE_JOBS)):
                    kind, n, half = GATE_JOBS[i]
                    j = J_G + i
                    s = i - 2
                    if 0 <= s < STEPS:
                        h, t = s // NT, s % NT
                        act.wait_ge(ao_ps.sem, ao_ps.at(l, s + 1))
                        A(br[2][:, h * T + t * P:h * T + (t + 1) * P], M0[:, 896:1024], ACT.Copy)\
                            .then_inc(ao_sb.sem, 1)
                    if kind == "g":
                        o = done(j)
                        if n == 0 and half == 1:
                            act.wait_ge(brA_ready.sem, brA_ready.at(l, 1))
                        if n == 1:
                            before = J_G + GATE_JOBS.index(("p", 0, half))
                            act.wait_ge(taken[before % 2].sem, taken[before % 2].at(l, before // 2 + 1))
                        if n == 2:
                            act.wait_ge(merged_ready.sem, merged_ready.at(l, half + 1))
                        A(sig[half], o[:, :], ACT.Sigmoid).then_inc(taken[j % 2].sem, 1)
                    s = i - 1
                    if 0 <= s < STEPS:
                        wide = NPAT * (s % NT + 1) * P
                        act.wait_ge(probT_ps.sem, probT_ps.at(l, s + 1))
                        if s >= 1:
                            act.wait_ge(ao_ps.sem, ao_ps.at(l, s))
                        A(probT[:, 0:wide], M1[:, 0:wide], ACT.Copy).then_inc(probT_sb.sem, 1)
                    s = i
                    if s < STEPS:
                        wide = NPAT * (s % NT + 1) * P
                        act.wait_ge(sc_max.sem, sc_max.at(l, s + 1))
                        if s >= 1:
                            act.wait_ge(probT_ps.sem, probT_ps.at(l, s))
                        A(prob[:, 0:wide], sc[:, 0:wide], ACT.Exp, bias=anegm, scale=ASCALE,
                          accum_out=aden).then_inc(sc_exp.sem, 1)

                act.wait_ge(taken[1].sem, taken[1].at(l, (J_OUT + 1) // 2 + 1))
                act.wait_ge(taken[0].sem, taken[0].at(l, J_OUT // 2 + 1))
                norm_stats(1)
                act.wait_ge(rt_max.sem, rt_max.at(l, 1))
                A(rt(2), rt(1), ACT.Exp).then_inc(rt_exp.sem, 1)

                act.wait_ge(pairs_known, l + 2)
                settle(act)
                end = act.value_load(pairs_end[0:1, 0:1], min_val=0, max_val=DEPTH * NPASS * PAIRS)
                with act.Fori(start, end) as it:
                    act.wait_ge(selT_ps, it + 1 + BASE)
                    act.wait_ge(mix_ps, NT * it + BASE)
                    A(selT, slotp[1][:, 0:NT * P], ACT.Copy).then_inc(selT_sb, 1)
                    act.wait_ge(gate_ps, it + 1 + BASE)
                    A(silu_g, M0[:, 0:FF], ACT.Silu).then_inc(silu_ready, 1)
                    act.wait_ge(hT_ps, it + 1)
                    act.wait_ge(y_ps, it + BASE)
                    A(hTs, M1[:, FF:FF + FC * P], ACT.Copy).then_inc(hT_sb, 1)
                    act.wait_ge(y_ps, it + 1 + BASE)
                    A(ysb[:, 0:512], slotp[1][:, 0:512], ACT.Copy).then_inc(y_sb, 1)

        @block.vector
        def _(dve):
            v = nc.vector
            setup = [0]

            def first(ins):
                setup[0] += 1
                ins.then_inc(setup_step, 1)
                dve.wait_ge(setup_step, setup[0])

            first(v.memset(total_pairs, 0.0))
            v.tensor_copy(pairs_end[0:1, 0:1], total_pairs).then_inc(pairs_known, 1)
            dve.wait_ge(consts_in, 32)
            first(v.tensor_copy(posf, pos_i[:, :]))
            for t in range(NT):
                first(v.tensor_scalar(sinb[:, t, :], c("freq"), posf[:, t:t + 1], None, ALU.mult))
            turns = rope_tmp[:, 0, 0:NT * ROPE].rearrange("p (t r) -> p t r", t=NT)
            first(v.tensor_scalar(turns, sinb[:, :, :], float(np.float32(1 / (2 * np.pi))), None, ALU.mult))
            first(v.tensor_scalar(turns, turns, float(1.5 * 2 ** 23), None, ALU.add))
            first(v.tensor_scalar(turns, turns, float(-1.5 * 2 ** 23), None, ALU.add))
            rest = 2 * np.pi
            for bits in (8, 8, 8, 24):
                scale = 2.0 ** (bits - 1 - np.floor(np.log2(abs(rest))))
                part = np.rint(rest * scale) / scale
                rest -= part
                first(v.scalar_tensor_tensor(out=sinb[:, :, :], in0=turns, scalar=float(-part), in1=sinb[:, :, :],
                                             op0=ALU.mult, op1=ALU.add))
            below_pi = float(np.nextafter(np.float32(np.pi), np.float32(0)))
            first(v.tensor_scalar(sinb[:, :, :], sinb[:, :, :], below_pi, -below_pi, ALU.min, ALU.max))
            first(v.scalar_tensor_tensor(out=cosb[:, :, :], in0=sinb[:, :, :], scalar=-1.0, in1=sinb[:, :, :],
                                         op0=ALU.mult, op1=ALU.min))
            v.tensor_scalar(cosb[:, :, :], cosb[:, :, :], float(np.pi / 2), None, ALU.add).then_inc(setup_act, 1)
            dve.wait_ge(rope_ready, 2)

            with dve.Fori(0, DEPTH) as l:
                dve.wait_ge(pairs_known, l + 1)
                settle(dve)
                start = dve.value_load(pairs_end[0:1, 0:1], min_val=0, max_val=DEPTH * NPASS * PAIRS)
                step = [0]

                def link(ins):
                    step[0] += 1
                    ins.then_inc(dve_step.sem, 1)
                    dve.wait_ge(dve_step.sem, dve_step.at(l, step[0]))

                def done(j):
                    dve.wait_ge(job_done.sem, job_done.at(l, j + 1))
                    return slotp[j % 2]

                def take_done(j):
                    dve.wait_ge(taken[j % 2].sem, taken[j % 2].at(l, j // 2 + 1))

                def normalise(n):
                    dve.wait_ge(rms_sd.sem, rms_sd.at(l, n + 1))
                    link(v.reciprocal(rinv, sd))
                    for t in range(NT):
                        v.tensor_scalar(hn[:, t * D:(t + 1) * D], xs[:, t, :], rinv[:, t:t + 1], None,
                                        ALU.mult).then_inc(hn_ready.sem, 1)

                def take_hT(n, gain):
                    for t in range(NT):
                        j = (J_NORM1, J_NORM2)[n] + t
                        o = done(j)
                        v.tensor_tensor(hT[:, :, t * P:(t + 1) * P], o[:, :].rearrange("p (c t) -> p c t", c=DC),
                                        gain.unsqueeze(2).broadcast_to((P, DC, P)), ALU.mult)\
                            .then_inc(taken[j % 2].sem, 1)

                dve.wait_ge(x_in, 16)
                dve.wait_ge(par_in, 16 * l + 16)
                normalise(0)
                v.memset(xpad[:, :, 0:TAPS - 1], 0.0).then_inc(pad_ready.sem, 1)
                v.scalar_tensor_tensor(out=spz, in0=q("lam"), scalar=-1.0, in1=q("lam"), op0=ALU.mult,
                                       op1=ALU.max).then_inc(lam_abs.sem, 1)
                take_hT(0, q("gain1"))
                dve.wait_ge(lam_exp.sem, lam_exp.at(l, 1))
                link(v.tensor_scalar(sps, spz, 2.0, None, ALU.add))
                link(v.reciprocal(sps, sps))
                link(v.tensor_tensor(sps, sps, spz, ALU.mult))
                link(v.tensor_tensor(sp2, sps, sps, ALU.mult))
                link(v.tensor_scalar(spp, sp2, 1.0 / 17, None, ALU.mult))
                for odd in (15, 13, 11, 9, 7, 5, 3):
                    link(v.scalar_tensor_tensor(out=spp, in0=spp, scalar=1.0 / odd, in1=sp2, op0=ALU.add, op1=ALU.mult))
                link(v.scalar_tensor_tensor(out=spp, in0=spp, scalar=1.0, in1=sps, op0=ALU.add, op1=ALU.mult))
                link(v.tensor_scalar(sps, q("lam"), -1.0, 0.0, ALU.mult, ALU.max))
                link(v.scalar_tensor_tensor(out=spp, in0=spp, scalar=2.0, in1=sps, op0=ALU.mult, op1=ALU.add))
                link(v.tensor_scalar(sp_pos, spp, 8.0, None, ALU.mult))
                v.tensor_scalar(sp_neg, spp, -8.0, None, ALU.mult).then_inc(lam_ready.sem, 1)

                dve.wait_ge(z_ps.sem, z_ps.at(l, 1))
                for g in range(2):
                    link(v.tensor_scalar(la[:, g * T:(g + 1) * T], M0[:, g * T:(g + 1) * T],
                                         q("gate_b")[:, g:g + 1], None, ALU.add))
                v.scalar_tensor_tensor(out=cum, in0=la, scalar=-1.0, in1=la, op0=ALU.mult, op1=ALU.max)\
                    .then_inc(z_abs.sem, 1)
                dve.wait_ge(decay_ln.sem, decay_ln.at(l, 1))
                link(v.scalar_tensor_tensor(out=la, in0=la, scalar=0.0, in1=cum, op0=ALU.min, op1=ALU.subtract))
                link(v.tensor_tensor_scan(cum, c("reset"), la, 0.0, ALU.mult, ALU.add))
                cumv = cum.rearrange("p (n t) -> p n t", t=CH)
                v.tensor_tensor(la.rearrange("p (n t) -> p n t", t=CH), cumv,
                                cumv[:, :, CH - 1:CH].broadcast_to((P, NT * T // CH, CH)), ALU.subtract)\
                    .then_inc(cum_ready.sem, 1)

                take_done(J_XB)
                for cc in range(WC):
                    o = xc[:, cc * T:(cc + 1) * T]
                    link(v.tensor_scalar(o, xpad[:, cc, 0:T], q("conv_w")[:, cc:cc + 1],
                                         q("conv_b")[:, cc:cc + 1], ALU.mult, ALU.add))
                    for k in range(1, TAPS):
                        w = v.scalar_tensor_tensor(out=o, in0=xpad[:, cc, k:k + T],
                                                   scalar=q("conv_w")[:, k * WC + cc:k * WC + cc + 1],
                                                   in1=o, op0=ALU.mult, op1=ALU.add)
                        if (cc, k) != (WC - 1, TAPS - 1):
                            link(w)
                w.then_inc(xc_ready.sem, 1)

                dve.wait_ge(exps_ready.sem, exps_ready.at(l, 1))
                take_done(J_QK)
                v.tensor_tensor(k_dec, k_dec, qk_ch[:, 512:1024], ALU.mult)
                v.tensor_tensor(k_inv, k_inv, qk_ch[:, 512:1024], ALU.mult)
                v.tensor_tensor(q_dec, q_dec, qk_ch[:, 0:512], ALU.mult).then_inc(gqk_ready.sem, 1)

                dve.wait_ge(lru_at.sem, lru_at.at(l, 1))
                link(v.tensor_tensor(a_sq, gate_r, gate_r, ALU.mult))
                v.scalar_tensor_tensor(out=tanh_y, in0=a_sq, scalar=1.0, in1=tanh_y, op0=ALU.add,
                                       op1=ALU.mult).then_inc(lru_m.sem, 1)
                dve.wait_ge(xc_ready.sem, xc_ready.at(l, 1))
                link(v.tensor_tensor(gate_i, gate_i, xc, ALU.mult))
                dve.wait_ge(lru_sqrt.sem, lru_sqrt.at(l, 1))
                link(v.tensor_tensor(gate_i, gate_i, tanh_y, ALU.mult))
                for cc in range(WC):
                    s = slice(cc * T, (cc + 1) * T)
                    w = v.tensor_tensor_scan(xc[:, s], gate_r[:, s], gate_i[:, s], 0.0, ALU.mult, ALU.add)
                link(w)
                take_done(J_YB)
                v.tensor_tensor(br[1], br[1], xc, ALU.mult).then_inc(brB_ready.sem, 1)

                def qk_sum(u):
                    dve.wait_ge(att_sq.sem, att_sq.at(l, u + 1))
                    v.tensor_reduce(asum, sq_att.rearrange("p (g d) -> p g d", d=DH), AX.X, ALU.add)\
                        .then_inc(att_sum.sem, 1)

                def qk_norm(u):
                    dve.wait_ge(att_sd.sem, att_sd.at(l, u + 1))
                    link(v.reciprocal(arinv, asd))
                    raw = qk_raw[u].rearrange("p (g d) -> p g d", d=DH)
                    link(v.tensor_tensor(raw, raw, arinv.unsqueeze(2).broadcast_to((P, NT * NH, DH)), ALU.mult))
                    gain = q("q_gain" if u < NPAT else "k_gain").unsqueeze(1).broadcast_to((P, NT * NH, DH))
                    link(v.tensor_tensor(raw, raw, gain, ALU.mult))
                    x1 = raw[:, :, 0:ROPE].rearrange("p (t h) d -> p t h d", t=NT)
                    x2 = raw[:, :, ROPE:2 * ROPE].rearrange("p (t h) d -> p t h d", t=NT)
                    cs = cosb[:, :, :].unsqueeze(2).broadcast_to((P, NT, NH, ROPE))
                    sn = sinb[:, :, :].unsqueeze(2).broadcast_to((P, NT, NH, ROPE))
                    tmp = [rope_tmp[:, i, :].rearrange("p (t h d) -> p t h d", t=NT, h=NH) for i in range(4)]
                    v.tensor_tensor(tmp[0], x1, cs, ALU.mult)
                    v.tensor_tensor(tmp[1], x2, sn, ALU.mult)
                    v.tensor_tensor(tmp[2], x2, cs, ALU.mult)
                    link(v.tensor_tensor(tmp[3], x1, sn, ALU.mult))
                    v.tensor_tensor(x1, tmp[0], tmp[1], ALU.subtract)
                    v.tensor_tensor(x2, tmp[2], tmp[3], ALU.add).then_inc(att_in.sem, 1)

                qk_sum(0)
                qk_norm(0)
                dve.wait_ge(gsc_ps.sem, gsc_ps.at(l, 1))
                mask = c("gla_mask").unsqueeze(1).broadcast_to((P, 4, P))
                for i in range(2):
                    w = v.tensor_tensor(gsc[:, i * 512:(i + 1) * 512].rearrange("p (n q) -> p n q", n=4),
                                        M1[:, i * 512:(i + 1) * 512].rearrange("p (n q) -> p n q", n=4),
                                        mask, ALU.mult)
                w.then_inc(gsc_sb.sem, 1)
                qk_sum(1)
                qk_norm(1)
                dve.wait_ge(kv_ps.sem, kv_ps.at(l, 1))
                for g in range(2):
                    st = [state[:, (g * 3 + n) * DV:(g * 3 + n + 1) * DV] for n in range(3)]
                    link(v.tensor_copy(st[0], M0[:, 512 + g * P:512 + (g + 1) * P]))
                    link(v.scalar_tensor_tensor(out=st[1], in0=st[0], scalar=etot[:, g * 4 + 1:g * 4 + 2],
                                                in1=M0[:, g * P:(g + 1) * P], op0=ALU.mult, op1=ALU.add))
                    w = v.scalar_tensor_tensor(out=st[2], in0=st[1], scalar=etot[:, g * 4 + 2:g * 4 + 3],
                                               in1=M0[:, 768 + g * P:768 + (g + 1) * P], op0=ALU.mult, op1=ALU.add)
                w.then_inc(state_ready.sem, 1)
                qk_sum(2)
                qk_norm(2)
                qk_sum(3)
                qk_norm(3)
                dve.wait_ge(grms.sem, grms.at(l, 1))
                take_done(J_OG)
                link(v.reciprocal(gsq, gsq))
                link(v.scalar_tensor_tensor(out=gsq, in0=M1[:, :], scalar=q("out_gain"), in1=gsq,
                                            op0=ALU.mult, op1=ALU.mult))
                for hh in range(2):
                    w = v.tensor_tensor(br[0].rearrange("p (g h t) -> p g h t", g=2, h=2)[:, :, hh, :],
                                        gsq[:, hh * 512:(hh + 1) * 512].rearrange("p (g t) -> p g t", g=2),
                                        og.rearrange("p (g h t) -> p g h t", g=2, h=2)[:, :, hh, :], ALU.mult)
                w.then_inc(brA_ready.sem, 1)
                for u in (4, 5):
                    qk_sum(u)
                    qk_norm(u)

                for i in range(len(GATE_JOBS)):
                    kind, n, half = GATE_JOBS[i]
                    j = J_G + i
                    if kind == "p":
                        o = done(j)
                        take_done(J_G + GATE_JOBS.index(("g", n, half)))
                        mg = merged[:, half * BLK:(half + 1) * BLK]
                        if n == 0:
                            v.tensor_tensor(mg, sig[half], o[:, :], ALU.mult).then_inc(taken[j % 2].sem, 1)
                        else:
                            v.tensor_tensor(sig[half], sig[half], o[:, :], ALU.mult).then_inc(taken[j % 2].sem, 1)
                            take_done(j)
                            if n > 1:
                                dve.wait_ge(merged_ready.sem, merged_ready.at(l, half + 1))
                            v.tensor_tensor(mg, mg, sig[half], ALU.add).then_inc(merged_ready.sem, 1)
                    if i < STEPS:
                        s, t = i, i % NT
                        wide = NPAT * (t + 1) * P
                        dve.wait_ge(sc_ps.sem, sc_ps.at(l, s + 1))
                        if s >= 1:
                            dve.wait_ge(sc_exp.sem, sc_exp.at(l, s))
                        v.tensor_tensor(sc[:, 0:wide], M0[:, 0:wide], c("band1" if t else "band0"), ALU.add)\
                            .then_inc(sc_sb.sem, 1)
                        dve.wait_ge(sc_sb.sem, sc_sb.at(l, s + 1))
                        link(v.tensor_reduce(amax, sc[:, 0:wide], AX.X, ALU.max))
                        v.tensor_scalar(anegm, amax, -ASCALE, None, ALU.mult).then_inc(sc_max.sem, 1)
                        dve.wait_ge(sc_exp.sem, sc_exp.at(l, s + 1))
                        link(v.reciprocal(arden, aden))
                        v.tensor_scalar(prob[:, 0:wide], prob[:, 0:wide], arden, None, ALU.mult)\
                            .then_inc(prob_ready.sem, 1)

                for t in range(NT):
                    j = J_OUT + t
                    o = done(j)
                    v.tensor_tensor(xs[:, t, :], xs[:, t, :], o[:, :], ALU.add).then_inc(taken[j % 2].sem, 1)
                take_done(J_OUT)
                take_done(J_OUT + 1)
                normalise(1)
                dve.wait_ge(gain2_in, 16 * l + 16)
                take_hT(1, g2[:, :])

                def e16(i):
                    return rt(i).rearrange("p (t e) -> p t e", t=NT)

                def e4(i, n=NT * NG):
                    return rt(i, n).rearrange("p (t g) -> p t g", t=NT)

                def per_tile(ap):
                    return ap.unsqueeze(2).broadcast_to((P, NT, NE))

                member, logit, ex, top1, top2 = (rt(i) for i in range(5))
                red = [blk(5, off=512 + 8 * i, width=NT) for i in range(8)]
                dve.wait_ge(logit_ps.sem, logit_ps.at(l, 1))
                link(v.tensor_tensor(e16(1), M0[:, 0:NT * NE].rearrange("p (t e) -> p t e", t=NT),
                                     c("router_b").unsqueeze(1).broadcast_to((P, NT, NE)), ALU.add))
                link(v.tensor_reduce(red[0], e16(1), AX.X, ALU.max))
                v.tensor_tensor(e16(1), e16(1), per_tile(red[0]), ALU.subtract).then_inc(rt_max.sem, 1)
                dve.wait_ge(rt_exp.sem, rt_exp.at(l, 1))
                link(v.tensor_reduce(red[1], e16(2), AX.X, ALU.add))
                link(v.reciprocal(red[2], red[1]))
                link(v.tensor_tensor(e16(2), e16(2), per_tile(red[2]), ALU.mult))
                ev = ex.rearrange("p (g e) -> p g e", e=NE // NG)
                hi1, lo1, hi2, lo2, m1, m2, gs, gsel = (blk(5, off=608 + 8 * i, width=8) for i in range(8))
                v.tensor_tensor(hi1, ev[:, :, 0], ev[:, :, 1], ALU.max)
                v.tensor_tensor(lo1, ev[:, :, 0], ev[:, :, 1], ALU.min)
                v.tensor_tensor(hi2, ev[:, :, 2], ev[:, :, 3], ALU.max)
                link(v.tensor_tensor(lo2, ev[:, :, 2], ev[:, :, 3], ALU.min))
                v.tensor_tensor(m1, hi1, hi2, ALU.max)
                v.tensor_tensor(m2, hi1, hi2, ALU.min)
                link(v.tensor_tensor(lo1, lo1, lo2, ALU.max))
                link(v.tensor_tensor(m2, m2, lo1, ALU.max))
                link(v.tensor_tensor(gs, m1, m2, ALU.add))

                def first_max(dst, src, keys, top, shape):
                    key = blk(5, off=672, width=shape[1] * shape[2]).rearrange("p (t e) -> p t e", t=NT)
                    kt = blk(5, off=712, width=NT)
                    link(v.tensor_reduce(top, src, AX.X, ALU.max))
                    link(v.tensor_tensor(key, src, top.unsqueeze(2).broadcast_to(shape), ALU.is_equal))
                    link(v.tensor_tensor(key, key, keys.unsqueeze(1).broadcast_to(shape), ALU.mult))
                    link(v.tensor_reduce(kt, key, AX.X, ALU.max))
                    link(v.tensor_tensor(dst, key, kt.unsqueeze(2).broadcast_to(shape), ALU.is_equal))

                gsv = gs.rearrange("p (t g) -> p t g", t=NT)
                gselv = gsel.rearrange("p (t g) -> p t g", t=NT)
                first_max(gselv, gsv, c("key4"), red[3], (P, NT, NG))
                gb = gsel.unsqueeze(2).broadcast_to((P, NT * NG, NE // NG))
                link(v.tensor_tensor(ev, ev, gb, ALU.mult))
                link(v.tensor_tensor(ev, ev, gb, ALU.add))
                link(v.tensor_scalar(ev, ev, -1.0, None, ALU.add))
                first_max(e16(3), e16(2), c("key16"), red[4], (P, NT, NE))
                link(v.scalar_tensor_tensor(out=ex, in0=top1, scalar=-4.0, in1=ex, op0=ALU.mult, op1=ALU.add))
                first_max(e16(4), e16(2), c("key16"), red[5], (P, NT, NE))
                link(v.tensor_tensor(red[6], red[4], red[5], ALU.add))
                link(v.reciprocal(red[6], red[6]))
                v.tensor_tensor(red[4], red[4], red[6], ALU.mult)
                v.tensor_tensor(red[5], red[5], red[6], ALU.mult)
                v.tensor_tensor(member, top1, top2, ALU.add).then_inc(member_ready.sem, 1)
                dve.wait_ge(member_ready.sem, member_ready.at(l, 1))
                link(v.tensor_tensor(e16(3), e16(3), per_tile(red[4]), ALU.mult))
                link(v.tensor_tensor(e16(4), e16(4), per_tile(red[5]), ALU.mult))
                link(v.tensor_tensor(gw2, e16(3).rearrange("p t e -> p e t"), e16(4).rearrange("p t e -> p e t"),
                                     ALU.add))
                dve.wait_ge(rank_ps.sem, rank_ps.at(l, 1))
                link(v.scalar_tensor_tensor(out=logit, in0=M1[:, 0:NT * NE], scalar=1.0, in1=member,
                                            op0=ALU.add, op1=ALU.mult))
                link(v.tensor_scalar(rank2, e16(1).rearrange("p t e -> p e t"), -1.0, None, ALU.add))
                link(v.tensor_reduce(mxc, M1[0:1, 512:512 + NE], AX.X, ALU.max))
                link(v.tensor_scalar(cmp4, c("caps")[0:1, :], mxc, None, ALU.is_lt))
                link(v.tensor_reduce(npass, cmp4, AX.X, ALU.add))
                link(v.scalar_tensor_tensor(out=total_pairs, in0=npass, scalar=float(PAIRS), in1=total_pairs,
                                            op0=ALU.mult, op1=ALU.add))
                v.tensor_copy(pairs_end[0:1, 0:1], total_pairs).then_inc(pairs_known, 1)

                def select(n, it):
                    e = 2 * (it % PAIRS)
                    base = nc.s_assert_within((it - start) // PAIRS * CAP, 0, T,
                                              skip_runtime_bounds_check_because="npass is at most T / CAP")
                    for i in range(2):
                        sv = sel.rearrange("p (t i s) -> p i t s", t=NT, i=2)[:, i]
                        w = v.tensor_tensor(sv, c("iota")[:, bass.ds(base, CAP)].unsqueeze(1).broadcast_to((P, NT, CAP)),
                                            rank2[:, bass.ds(e + i, 1), :].rearrange("p o t -> p (o t)").unsqueeze(2)
                                            .broadcast_to((P, NT, CAP)), ALU.is_equal)
                    w.then_inc(sel_hot, 1)
                    dve.wait_ge(sel_hot, n + 1)
                    for i in range(2):
                        w = v.tensor_tensor(selw.rearrange("p (t i s) -> p i t s", t=NT, i=2)[:, i],
                                            sel.rearrange("p (t i s) -> p i t s", t=NT, i=2)[:, i],
                                            gw2[:, bass.ds(e + i, 1), :].rearrange("p o t -> p (o t)").unsqueeze(2)
                                            .broadcast_to((P, NT, CAP)), ALU.mult)
                    w.then_inc(sel_ready, 1)

                def take_gather(n):
                    dve.wait_ge(xg_ps, n + 1 + BASE)
                    v.tensor_tensor(xgT, slotp[0][:, :].rearrange("p (c s) -> p c s", c=DC),
                                    g2[:, :].unsqueeze(2).broadcast_to((P, DC, P)), ALU.mult).then_inc(xg_sb, 1)

                dve.wait_ge(pairs_known, l + 2)
                settle(dve)
                end = dve.value_load(pairs_end[0:1, 0:1], min_val=0, max_val=DEPTH * NPASS * PAIRS)
                select(start + l, start)
                take_gather(start + l)
                with dve.Fori(start, end) as it:
                    dve.wait_ge(selT_ps, it + 1 + BASE)
                    dve.wait_ge(xg_ps, it + l + 1 + BASE)
                    select(it + l + 1, it + 1)
                    dve.wait_ge(silu_ready, it + 1)
                    dve.wait_ge(gu_ps, it + 1 + BASE)
                    v.tensor_tensor(hs, silu_g, M0[:, FF:2 * FF], ALU.mult).then_inc(h_ready, 1)
                    take_gather(it + l + 1)
                    dve.wait_ge(y_ps, it + 1 + BASE)
                    v.tensor_copy(ysb[:, 512:1024], slotp[1][:, 512:1024]).then_inc(y_sb, 1)
                    for t in range(NT):
                        dve.wait_ge(mix_ps, NT * it + t + 1 + BASE)
                        v.tensor_tensor(xs[:, t, :], xs[:, t, :], (M0, M1)[t][:, :], ALU.add).then_inc(x_add[t], 1)
                assert step[0] == dve_step.per, step[0]


def constants(router_w, router_b):
    k = np.zeros((P, NCONST), np.float32)

    def put(name, value):
        a, b = CONST[name]
        k[:, a:b] = value

    i, j = np.arange(P)[:, None], np.arange(P)[None, :]
    put("ident", i == j)
    put("mean", 1.0 / P)
    put("ones", 1.0)
    put("before", i < j)
    put("gla_mask", (i // CH == j // CH) & (i <= j))
    put("reset", (np.arange(NT * T) % CH != 0)[None, :])
    for t in range(NT):
        wide = (t + 1) * P
        dist = t * P + np.arange(P)[:, None] - np.arange(wide)[None, :]
        band = [np.where((dist >= 0) & (dist % dil == 0) & (dist // dil <= window // dil), 0.0, -1e30)
                for window, dil in PATTERNS]
        put(f"band{t}", np.concatenate(band, 1))
    put("iota", np.arange(T + CAP)[None, :])
    put("caps", (CAP * np.arange(NPASS))[None, :])
    put("key4", (NG - np.arange(NG))[None, :])
    put("key16", (NE - np.arange(NE))[None, :])
    put("freq", (THETA ** (-np.arange(ROPE) / ROPE))[None, :])
    put("eps", EPS)
    put("one", 1.0)
    put("router_w", router_w.reshape(DC, P, NE).transpose(1, 0, 2).reshape(P, -1))
    put("router_b", router_b[None, :])
    return k


def parameters(a):
    k = np.zeros((DEPTH, P, NPAR), np.float32)
    for l in range(DEPTH):
        def put(name, value, rows=P):
            s, e = PAR[name]
            k[l, 0:rows, s:e] = value

        def cols(v):
            return v.reshape(-1, P).T

        def blocks(w):
            o = np.zeros((P, WC, P), np.float32)
            for n in range(2 * WC):
                b = (n % 2) * 64
                o[b:b + 64, n // 2, b:b + 64] = w[n]
            return o.reshape(P, -1)

        put("gain1", cols(a["norm1_gain"][l]))
        put("gate_b", cols(a["gla_gate_bias"][l]))
        put("out_gain", cols(a["gla_out_gain"][l]))
        put("conv_w", a["lru_conv_w"][l].reshape(TAPS, WC, P).transpose(2, 0, 1).reshape(P, -1))
        put("conv_b", cols(a["lru_conv_b"][l]))
        put("b_a", cols(a["lru_b_a"][l]))
        put("b_x", cols(a["lru_b_x"][l]))
        put("lam", cols(a["lru_lambda"][l]))
        put("w_a", blocks(a["lru_w_a"][l]))
        put("w_x", blocks(a["lru_w_x"][l]))
        put("q_gain", a["q_norm_gain"][l][None, :])
        put("k_gain", a["k_norm_gain"][l][None, :])
        put("low", a["w_in"][l][:, C_LOW:C_LOW + RANK].reshape(DC, P, RANK).transpose(1, 0, 2).reshape(P, -1))
        put("gate_up", a["gla_gate_up"][l], RANK)
    return k


def kernel(**inputs):
    import concourse.bacc as _bacc
    from concourse.bass_utils import run_bass_kernel_spmd as _run

    a = {name: np.ascontiguousarray(v) for name, v in inputs.items()}
    arrays = {
        "x": a["x"], "positions": a["positions"],
        "const": constants(a["router_w"], a["router_b"]), "par": parameters(a),
        "gain2": np.ascontiguousarray(a["norm2_gain"].reshape(DEPTH, DC, P).transpose(0, 2, 1)),
    }
    for name in ("w_in", "w_branch", "w_out", "w_gate", "w_up", "w_down"):
        arrays[name] = a[name]
    nc = _bacc.Bacc("TRN2", target_bir_lowering=False, num_devices=1)
    args = [nc.dram_tensor(f"in_{n}", v.shape, mybir.dt.from_np(v.dtype), kind="ExternalInput").ap()
            for n, v in arrays.items()]
    out = nc.dram_tensor("out_x", a["x"].shape, F32, kind="ExternalOutput").ap()
    build(nc, *args, out)
    r = _run(nc, [{f"in_{n}": v for n, v in arrays.items()}], core_ids=[0])
    return r.results[0]["out_x"]
```

```python
from contextlib import ExitStack

import numpy as np
import concourse.bass as bass
from concourse import mybir

F32 = mybir.dt.float32
F32R = mybir.dt.float32r
I32 = mybir.dt.int32
ALU = mybir.AluOpType
ACT = mybir.ActivationFunctionType
AX = mybir.AxisListType

P = 128
D = 1024
T = 256
NT = T // P
DC = D // P
DEPTH = 2
EPS = 1e-6
HG, DK, DV, CH = 4, 64, 128, 64
RANK = 16
W = 512
WC = W // P
TAPS = 4
NPAT, NH, DH = 3, 4, 128
PATTERNS = ((128, 1), (512, 4), (2048, 16))
ROPE = 16
THETA = 500000.0
ASCALE = float(DH) ** -0.5
NE, NG, FF = 16, 4, 512
FC = FF // P
CAP = 64
PAIRS = NE // 2
NPASS = T // CAP
UNIT = 4096
BLK = 1024
RING = 8
MIX_RING = 4
BASE = 1

C_QK, C_VA, C_OG, C_LOW = 0, 512, 1024, 1536
C_XB = C_LOW + RANK
C_YB = C_XB + W
C_Q = C_YB + W
C_K = C_Q + NPAT * 512
C_V = C_K + NPAT * 512
C_G = C_V + NPAT * 512

TIME_MAJOR = {C_VA} | {a + 512 * p for a in (C_Q, C_K, C_V) for p in range(NPAT)}

MIXER_UNITS = ([("in", C_QK), ("in", C_VA), ("in", C_XB), ("in", C_YB), ("in", C_OG)]
               + [("in", C_Q + 512 * p) for p in range(NPAT)]
               + [("in", C_K + 512 * p) for p in range(NPAT)]
               + [("in", C_V + 512 * p) for p in range(NPAT)]
               + [("in", C_G), ("branch", 0), ("in", C_G + 512),
                  ("in", C_G + 1024), ("branch", 1), ("in", C_G + 1536),
                  ("in", C_G + 2048), ("in", C_G + 2560), ("branch", 2),
                  ("out", 0), ("out", 1)])
MIX_USES = [len(MIXER_UNITS[s:: MIX_RING]) if s < MIX_RING else 0 for s in range(RING)]
UNIT_JOBS = list(range(2, 16)) + [16, 19, 18, 20, 23, 22, 24, 25, 27, 29, 29]
SPLIT_UNITS = [k for k, (kind, _) in enumerate(MIXER_UNITS) if kind == "in"]
SPLIT_JOBS = [UNIT_JOBS[k] for k in SPLIT_UNITS]
SPLITS = len(SPLIT_UNITS)
QUARTERS = 4
QUARTER = UNIT // QUARTERS
GATE, UP, DOWN, GATE_ODD = (0, 1), (2, 3), (4, 5), (6, 7)

J_NORM1, J_QK, J_VA, J_XB, J_YB, J_OG, J_Q, J_K, J_V, J_G = 0, 2, 3, 4, 5, 6, 7, 10, 13, 16
GATE_JOBS = (("g", 0, 0), ("p", 0, 0), ("g", 0, 1), ("p", 0, 1),
             ("g", 1, 0), ("p", 1, 0), ("g", 1, 1), ("p", 1, 1),
             ("g", 2, 0), ("g", 2, 1), ("p", 2, 0), ("p", 2, 1))
J_OUT = J_G + len(GATE_JOBS)
J_NORM2 = J_OUT + NT
JOBS = J_NORM2 + NT
STEPS = NH * NT


def columns(widths):
    out, at = {}, 0
    for name, width in widths:
        out[name] = (at, at + width)
        at += width
    return out, at


CONST, NCONST = columns([
    ("ident", P), ("mean", P), ("ones", P), ("before", P), ("gla_mask", P),
    ("band", NPAT * T), ("iota", T + CAP), ("caps", NPASS), ("key4", NG), ("key16", NE),
    ("freq", ROPE), ("eps", 1), ("one", 1), ("router_w", DC * NE), ("router_b", NE)])
PAR, NPAR = columns([
    ("gain1", DC), ("gate_b", 2), ("out_gain", 1), ("conv_w", TAPS * WC), ("conv_b", WC), ("b_a", WC),
    ("b_x", WC), ("lam", WC), ("w_a", WC * P), ("w_x", WC * P), ("q_gain", P), ("k_gain", P),
    ("low", DC * RANK), ("gate_up", 2 * P)])


def build(nc, x, positions, const, par, gain2, w_in, w_branch, w_out, w_gate, w_up, w_down, out):
    with ExitStack() as ctx:
        def sb(name, shape, dt=F32):
            return ctx.enter_context(nc.sbuf_tensor(name, shape, dt))

        class Signal:

            def __init__(self, name, per, base=0):
                self.sem = ctx.enter_context(nc.semaphore(name))
                self.per = per
                self.base = base

            def at(self, l, k):
                return l * self.per + k + self.base

        def sem(name):
            return ctx.enter_context(nc.semaphore(name))

        ring = sb("ring", [P, MIX_RING, UNIT])
        with nc.sbuf_tensor("w_hi", [P, QUARTERS, QUARTER], F32R) as w_hi, \
                nc.sbuf_tensor("w_lo", [P, QUARTERS, QUARTER], F32R) as w_lo:
            pass
        ring_down = sb("ring_down", [P, len(DOWN), UNIT])
        arena = sb("arena", [P, 16 * BLK])
        hn = sb("hn", [P, NT * D])
        hT_hi = sb("hT_hi", [P, DC, T], F32R)
        hT_lo = sb("hT_lo", [P, DC, T], F32R)
        xs = sb("xs", [P, NT, D])
        cst = sb("cst", [P, NCONST])
        prm = sb("prm", [P, NPAR])
        g2 = sb("g2", [P, DC])
        cosb = sb("cosb", [P, NT, ROPE])
        sinb = sb("sinb", [P, NT, ROPE])
        small = sb("small", [P, 96])
        pairs_end = sb("pairs_end", [1, 1], I32)
        pos_i = sb("pos_i", [P, NT], I32)

        slotp = [ctx.enter_context(nc.psum_tensor(f"slot{i}", [P, 1024], F32)) for i in range(2)]
        M0 = ctx.enter_context(nc.psum_tensor("M0", [P, 1024], F32))
        M1 = ctx.enter_context(nc.psum_tensor("M1", [P, 1024], F32))

        def c(name):
            a, b = CONST[name]
            return cst[:, a:b]

        def q(name):
            a, b = PAR[name]
            return prm[:, a:b]

        def blk(i, n=1, off=0, width=None):
            a = i * BLK + off
            return arena[:, a:a + (width or n * BLK)]

        def h0(a, b):
            return hn[:, a:b]

        ident, ones = c("ident"), c("ones")
        eps, one = c("eps"), c("one")

        def slot_mem(slot):
            if slot in GATE_ODD:
                return blk(8 + 4 * GATE_ODD.index(slot), 4)
            return ring_down[:, DOWN.index(slot), :] if slot in DOWN else ring[:, slot, :]

        hT = blk(0, 2).rearrange("p (c t) -> p c t", c=DC)
        diag = blk(2, width=NT * P)
        rope_tmp = blk(8, width=4 * P).rearrange("p (i r) -> p i r", i=4)
        qk_raw = [blk(u) for u in range(2 * NPAT)]
        xc, gate_r, tanh_y, gate_i = blk(3), blk(4), blk(5), blk(6)
        xpad = arena[:, 7 * BLK:7 * BLK + WC * (T + TAPS - 1)].rearrange("p (c t) -> p c t", c=WC)
        a_sq = arena[:, 7 * BLK:8 * BLK]
        k_dec = blk(8, off=512, width=512)
        kdT = k_dec
        br = [blk(9), blk(10), blk(11)]
        qk_ch, sq_att = blk(11), blk(11)
        va, og = blk(12), blk(13)
        gsc, gsq = blk(14), blk(15)
        la, cum = h0(0, 512), h0(512, 1024)
        q_dec, k_inv = h0(1024, 1536), h0(1536, 2048)
        state = h0(0, 768)
        v_att = [blk(6), blk(7), blk(8)]
        merged = blk(12, 2)
        sig = [blk(14), blk(15)]
        sc = h0(0, 768)
        prob = h0(1024, 1792)
        wa0 = PAR["w_a"][0]
        probT = prm[:, wa0:wa0 + 768]
        xgT = blk(0).rearrange("p (c s) -> p c s", c=DC)
        sel = blk(1, width=256)
        selw = blk(1, off=256, width=256)
        selT = blk(1, off=512, width=256)
        silu_g = blk(2, width=FF)
        hs = blk(2, off=FF, width=FF)
        hTs = blk(3, width=FC * P)
        ysb = blk(4)
        rank2 = blk(6, width=NE * NT).rearrange("p (e t) -> p e t", e=NE)
        gw2 = blk(6, off=64, width=NE * NT).rearrange("p (e t) -> p e t", e=NE)

        def rt(i, n=NT * NE):
            return blk(5, off=32 * i, width=n)

        ss, sd, rinv = small[:, 0:2], small[:, 2:4], small[:, 4:6]
        etot = small[:, 6:14]
        asum, arinv = small[:, 14:22], small[:, 30:38]
        asd = (small[:, 22:30], small[:, 76:84])
        amax, anegm, aden, arden = (small[:, 38 + i:39 + i] for i in range(4))
        posf = small[:, 42:44]
        spz, sps, sp2, spp, sp_neg, sp_pos = (small[:, 44 + 4 * i:48 + 4 * i] for i in range(6))
        total_pairs = small[0:1, 68:69]
        npass = small[0:1, 69:70]
        cmp4 = small[0:1, 70:74]
        mxc = small[0:1, 74:75]

        loaded = [sem(f"loaded{s}") for s in range(RING)]
        consts_in, x_in, x_out = sem("consts_in"), sem("x_in"), sem("x_out")
        par_in, gain2_in = sem("par_in"), sem("gain2_in")
        setup_step, setup_act, rope_ready = sem("setup_step"), sem("setup_act"), sem("rope_ready")
        pairs_known = sem("pairs_known")
        job_done = Signal("job_done", JOBS)
        hi_ready, lo_ready = Signal("hi_ready", QUARTERS * SPLITS), Signal("lo_ready", QUARTERS * SPLITS)
        quarter_used = Signal("quarter_used", (QUARTERS - 1) * SPLITS)
        hT_hi_ready, hT_lo_ready = Signal("hT_hi_ready", NT), Signal("hT_lo_ready", NT)
        taken = [Signal(f"taken{i}", JOBS // 2, BASE) for i in range(2)]
        dve_step = Signal("dve_step", 124)
        rms_sq, rms_sd, diag_ready = (Signal(n, 2 * NT) for n in ("rms_sq", "rms_sd", "diag_ready"))
        low_ps, low_sb, z_ps = Signal("low_ps", 1), Signal("low_sb", 1), Signal("z_ps", 1)
        z_abs, decay_exp, decay_ln = Signal("z_abs", 1), Signal("decay_exp", 1), Signal("decay_ln", 1)
        cum_ready, exps_ready, gqk_ready = Signal("cum_ready", 1), Signal("exps_ready", 1), Signal("gqk_ready", 1)
        gsc_ps, gsc_sb = Signal("gsc_ps", 1), Signal("gsc_sb", 1)
        kdT_ps, kdT_sb = Signal("kdT_ps", 1), Signal("kdT_sb", 1)
        kv_ps, state_ready = Signal("kv_ps", 1), Signal("state_ready", 1)
        go_ps, go_sq, gmean_ps, grms = Signal("go_ps", 1), Signal("go_sq", 1), Signal("gmean_ps", 1), Signal("grms", 1)
        brA_ready = Signal("brA_ready", 1)
        lam_abs, lam_exp, lam_ready = Signal("lam_abs", 1), Signal("lam_exp", 1), Signal("lam_ready", 1)
        pad_ready, xc_ready = Signal("pad_ready", 1), Signal("xc_ready", 1)
        lru_ps, lru_sig, lru_at = Signal("lru_ps", 2), Signal("lru_sig", 2), Signal("lru_at", 1)
        lru_m, lru_sqrt, brB_ready = Signal("lru_m", 1), Signal("lru_sqrt", 1), Signal("brB_ready", 1)
        att_sq, att_sd, att_in = Signal("att_sq", 6), Signal("att_sd", 6), Signal("att_in", 6)
        attT_ps, attT_sb = Signal("attT_ps", 6), Signal("attT_sb", 6)
        sc_ps, sc_sb, sc_max, sc_exp, prob_ready = (Signal(n, STEPS) for n in
                                                    ("sc_ps", "sc_sb", "sc_max", "sc_exp", "prob_ready"))
        probT_ps, probT_sb, ao_ps, ao_sb = (Signal(n, STEPS) for n in ("probT_ps", "probT_sb", "ao_ps", "ao_sb"))
        merged_ready = Signal("merged_ready", 4)
        logit_ps, rt_max, rt_exp = Signal("logit_ps", 1), Signal("rt_max", 1), Signal("rt_exp", 1)
        member_ready, rank_ps = Signal("member_ready", 1), Signal("rank_ps", 1)
        sel_ready, sel_hot, xg_ps, xg_sb = sem("sel_ready"), sem("sel_hot"), sem("xg_ps"), sem("xg_sb")
        gate_ps, gu_ps, silu_ready, h_ready = sem("gate_ps"), sem("gu_ps"), sem("silu_ready"), sem("h_ready")
        hT_ps, hT_sb, selT_ps, selT_sb = sem("hT_ps"), sem("hT_sb"), sem("selT_ps"), sem("selT_sb")
        y_ps, y_sb, mix_ps = sem("y_ps"), sem("y_sb"), sem("mix_ps")
        x_add = [sem(f"x_add{t}") for t in range(NT)]
        slot_done = (gate_ps, gate_ps, gu_ps, gu_ps, y_ps, y_ps, gate_ps, gate_ps)

        block = ctx.enter_context(nc.Block())

        settled = sem("settled")

        def settle(eng):
            eng.sem_inc(settled, 1)

        def arrivals(slot, l, start, k):
            return 16 * (l * MIX_USES[slot] + k) + start * (8 if slot in GATE else 16)

        def expert_arrivals(slot, l, it):
            if slot in GATE:
                return 16 * (l + 1) * MIX_USES[slot] + 8 * it + 16
            if slot in GATE_ODD:
                return 8 * it + 8
            return 16 * (l + 1) * MIX_USES[slot] + 16 * (it + 1)

        def quarter_of(weights, m, qt):
            if MIXER_UNITS[SPLIT_UNITS[m]][1] in TIME_MAJOR:
                return weights[:, qt * QUARTER:(qt + 1) * QUARTER]
            return weights.rearrange("p (c n) -> p c n", c=DC)[:, :, qt * P:(qt + 1) * P]

        def quarter_part(part, m, qt):
            a = part[:, qt, :]
            return a if MIXER_UNITS[SPLIT_UNITS[m]][1] in TIME_MAJOR else a.rearrange("p (c n) -> p c n", c=DC)

        @block.sync
        def _(sp):
            sp.dma_start(pos_i[:, :], positions.rearrange("b (t p) -> p (b t)", p=P),
                         allow_slow_non_contiguous=True).then_inc(consts_in, 16)
            sp.dma_start(cst[:, :], const).then_inc(consts_in, 16)
            sp.dma_start(xs[:, :, :], x.rearrange("b (t p) d -> p (b t) d", p=P)).then_inc(x_in, 16)
            sp.dma_start(prm[:, :], par[0]).then_inc(par_in, 16)

            with sp.Fori(0, DEPTH) as l:
                sp.wait_ge(pairs_known, l + 1)
                settle(sp)
                start = sp.value_load(pairs_end[0:1, 0:1], min_val=0, max_val=DEPTH * NPASS * PAIRS)

                def unit_used(k):
                    if k in SPLIT_UNITS:
                        sp.wait_ge(lo_ready.sem, lo_ready.at(l, QUARTERS * (SPLIT_UNITS.index(k) + 1)))
                    else:
                        sp.wait_ge(job_done.sem, job_done.at(l, UNIT_JOBS[k] + 1))

                def mixer_unit(k):
                    slot = k % MIX_RING
                    kind, at = MIXER_UNITS[k]
                    if k < MIX_RING:
                        sp.wait_ge(slot_done[slot], start + BASE)
                    else:
                        unit_used(k - MIX_RING)
                    settle(sp)
                    dst = ring[:, slot, :]
                    if kind == "in":
                        src = w_in[bass.ds(l, 1), :, at:at + 512].rearrange("o (c p) n -> p (o c) n", p=P)
                        dst = dst.rearrange("p (c n) -> p c n", c=DC)
                    elif kind == "branch":
                        src = w_branch[bass.ds(l, 1), at].rearrange("o (c p) n -> p (o c) n", p=P)
                        dst = dst.rearrange("p (c n) -> p c n", c=WC)
                    else:
                        src = w_out[bass.ds(l, 1), at * 512:(at + 1) * 512].rearrange("o (c p) n -> p (o c) n", p=P)
                        dst = dst.rearrange("p (c n) -> p c n", c=WC)
                    sp.dma_start(dst, src).then_inc(loaded[slot], 16)

                for k in range(len(MIXER_UNITS)):
                    mixer_unit(k)
                    if k == MIX_RING - 1:
                        sp.wait_ge(x_add[NT - 1], start + BASE)
                        settle(sp)
                        sp.dma_start(g2[:, :], gain2[bass.ds(l, 1)].rearrange("o p n -> p (o n)"))\
                            .then_inc(gain2_in, 16)

                def expert_weights(slot, it):
                    w = (w_gate, w_up, w_down, w_gate)[slot // 2]
                    e = 2 * (it % PAIRS) + slot % 2
                    rows = FC if slot in DOWN else DC
                    src = w[bass.ds(l, 1), bass.ds(e, 1)].rearrange("o e (c p) n -> p (o e c) n", p=P)
                    sp.dma_start(slot_mem(slot).rearrange("p (c n) -> p c n", c=rows), src)\
                        .then_inc(loaded[slot], 16)

                last_unit = [max(k for k in range(len(MIXER_UNITS)) if k % MIX_RING == slot) for slot in range(MIX_RING)]
                for slot in DOWN:
                    sp.wait_ge(job_done.sem, job_done.at(l, SPLIT_JOBS[-1] + 1))
                    settle(sp)
                    expert_weights(slot, start)
                for slot in sorted(range(MIX_RING), key=lambda slot: UNIT_JOBS[last_unit[slot]]):
                    unit_used(last_unit[slot])
                    settle(sp)
                    expert_weights(slot, start)

                sp.wait_ge(job_done.sem, job_done.at(l, J_OUT + NT))
                settle(sp)
                for slot in GATE_ODD:
                    expert_weights(slot, start + 1)

                def refill(slots, it):
                    for slot in slots:
                        sp.wait_ge(slot_done[slot], it + BASE)
                        settle(sp)
                        expert_weights(slot, it)

                def refill_gate(slots, it):
                    for slot in slots:
                        sp.wait_ge(gate_ps, it - 1 + BASE)
                        settle(sp)
                        expert_weights(slot, it)

                with sp.Fori(start + 2, start + PAIRS, 2) as it:
                    refill(UP + DOWN, it - 1)
                    refill_gate(GATE, it)
                    refill(UP + DOWN, it)
                    refill_gate(GATE_ODD, it + 1)
                refill(UP + DOWN, start + PAIRS - 1)
                sp.wait_ge(job_done.sem, job_done.at(l, JOBS))
                settle(sp)
                nxt = (l + 1) % DEPTH
                sp.wait_ge(pairs_known, l + 2)
                sp.dma_start(prm[:, :], par[bass.ds(nxt, 1)].rearrange("o p n -> p (o n)")).then_inc(par_in, 16)
                settle(sp)
                end = sp.value_load(pairs_end[0:1, 0:1], min_val=0, max_val=DEPTH * NPASS * PAIRS)
                with sp.If(end > start + PAIRS):
                    with sp.Fori(start + PAIRS, end, 2) as it:
                        refill_gate(GATE, it)
                        refill(UP + DOWN, it)
                        refill_gate(GATE_ODD, it + 1)
                        refill(UP + DOWN, it + 1)

            total = sp.value_load(pairs_end[0:1, 0:1], min_val=0, max_val=DEPTH * NPASS * PAIRS)
            for t in range(NT):
                sp.wait_ge(x_add[t], total + BASE)
                settle(sp)
                sp.dma_start(out.rearrange("b (t p) d -> p (b t) d", p=P)[:, t, :], xs[:, t, :]).then_inc(x_out, 16)
            sp.wait_ge(x_out, 16 * NT)
            sp.wait_ge(par_in, 16 * (DEPTH + 1))
            sp.wait_ge(gain2_in, 16 * DEPTH)

        @block.tensor
        def _(pe):
            mm = nc.tensor.matmul
            for s in (taken[0].sem, taken[1].sem, *x_add, gate_ps, gu_ps, y_ps, selT_ps, xg_ps, xg_sb, mix_ps):
                pe.sem_inc(s, BASE)
            pe.wait_ge(consts_in, 32)

            with pe.Fori(0, DEPTH) as l:
                pe.wait_ge(pairs_known, l + 1)
                settle(pe)
                start = pe.value_load(pairs_end[0:1, 0:1], min_val=0, max_val=DEPTH * NPASS * PAIRS)
                for t in range(NT):
                    pe.wait_ge(x_add[t], start + BASE)
                pe.wait_ge(par_in, 16 * l + 16)

                def weights(k, rows):
                    slot = k % MIX_RING
                    pe.wait_ge(loaded[slot], arrivals(slot, l, start, k // MIX_RING + 1))
                    return ring[:, slot, :].rearrange("p (c n) -> p c n", c=rows)

                def taken_wait(j):
                    pe.wait_ge(taken[j % 2].sem, taken[j % 2].at(l, j // 2 + 1))

                def open_slot(j):
                    pe.wait_ge(taken[j % 2].sem, taken[j % 2].at(l, j // 2))
                    return slotp[j % 2]

                def transposes(j, n):
                    o = open_slot(j)
                    t = j - (J_NORM1, J_NORM2)[n]
                    pe.wait_ge(diag_ready.sem, diag_ready.at(l, NT * n + t + 1))
                    for cc in range(DC):
                        last = mm(o[:, cc * P:(cc + 1) * P], xs[:, t, cc * P:(cc + 1) * P],
                                  diag[:, t * P:(t + 1) * P], start=True, stop=True)
                    last.then_inc(job_done.sem, 1)

                PARTS = ((w_hi, hT_hi), (w_hi, hT_lo), (w_lo, hT_hi))

                def quarter_done(qt, last):
                    last.then_inc(quarter_used.sem if qt < QUARTERS - 1 else job_done.sem, 1)

                def channel_major(j, middle=None):
                    m = SPLIT_JOBS.index(j)
                    o = open_slot(j)
                    for qt in range(QUARTERS):
                        pe.wait_ge(lo_ready.sem, lo_ready.at(l, QUARTERS * m + qt + 1))
                        for cc in range(DC):
                            for i, (w, h) in enumerate(PARTS):
                                last = mm(o[:, qt * T:(qt + 1) * T], quarter_part(w, m, qt)[:, cc, :], h[:, cc, :],
                                          start=cc == i == 0, stop=cc == DC - 1 and i == 2)
                        quarter_done(qt, last)
                        if qt == 1 and middle:
                            middle()

                def time_major(j):
                    m = SPLIT_JOBS.index(j)
                    o = open_slot(j)
                    for qt in range(QUARTERS):
                        pe.wait_ge(lo_ready.sem, lo_ready.at(l, QUARTERS * m + qt + 1))
                        for t in range(NT):
                            for cc in range(2 * qt, 2 * qt + 2):
                                for i, (w, h) in enumerate(PARTS):
                                    last = mm(o[:, t * 512:(t + 1) * 512], h[:, cc, t * P:(t + 1) * P],
                                              w[:, qt, (cc % 2) * 512:(cc % 2 + 1) * 512],
                                              start=cc == i == 0, stop=cc == DC - 1 and i == 2)
                        quarter_done(qt, last)

                def branch_major(j, k, rhs, col0, middle=None):
                    wv = weights(k, WC)
                    o = open_slot(j)
                    for m in range(4):
                        for cc in range(WC):
                            last = mm(o[:, m * T:(m + 1) * T], wv[:, cc, col0 + m * P:col0 + (m + 1) * P],
                                      rhs[:, cc, :], start=cc == 0, stop=cc == WC - 1)
                        if m == 1 and middle:
                            middle()
                    last.then_inc(job_done.sem, 1)

                for j in (0, 1):
                    transposes(j, 0)
                taken_wait(0)
                taken_wait(1)

                low = q("low").rearrange("p (c r) -> p c r", c=DC)
                for cc in range(DC):
                    last = mm(M0[0:RANK, 512:512 + T], low[:, cc, :], hT[:, cc, :], start=cc == 0, stop=cc == DC - 1)
                last.then_inc(low_ps.sem, 1)
                pe.wait_ge(hT_lo_ready.sem, hT_lo_ready.at(l, NT))
                channel_major(J_QK)
                pe.wait_ge(low_sb.sem, low_sb.at(l, 1))
                a = PAR["gate_up"][0]
                for g in range(2):
                    last = mm(M0[:, g * T:(g + 1) * T], prm[0:RANK, a + g * P:a + (g + 1) * P],
                              h0(0, T)[0:RANK, :], start=True, stop=True)
                last.then_inc(z_ps.sem, 1)
                time_major(J_VA)
                for j in (J_XB, J_YB):
                    channel_major(j)
                xcv = xc.rearrange("p (c t) -> p c t", c=WC)

                def lru_gates(name, dst):
                    wv = q(name).rearrange("p (c n) -> p c n", c=WC)
                    for cc in range(WC):
                        last = mm(dst[:, cc * T:(cc + 1) * T], wv[:, cc, :], xcv[:, cc, :], start=True, stop=True)
                    last.then_inc(lru_ps.sem, 1)

                channel_major(J_OG)
                pe.wait_ge(xc_ready.sem, xc_ready.at(l, 1))
                lru_gates("w_a", M1)
                pe.wait_ge(z_abs.sem, z_abs.at(l, 1))
                lru_gates("w_x", M0)

                time_major(J_Q)
                pe.wait_ge(gqk_ready.sem, gqk_ready.at(l, 1))
                pe.wait_ge(lru_sig.sem, lru_sig.at(l, 1))
                for hh in range(2):
                    for g in range(2):
                        for t in range(NT):
                            cols = slice(g * T + t * P, g * T + (t + 1) * P)
                            last = mm(M1[:, (hh * 4 + g * 2 + t) * P:(hh * 4 + g * 2 + t + 1) * P],
                                      k_inv[hh * DK:(hh + 1) * DK, cols], q_dec[hh * DK:(hh + 1) * DK, cols],
                                      start=True, stop=True)
                last.then_inc(gsc_ps.sem, 1)
                pe.wait_ge(lru_sig.sem, lru_sig.at(l, 2))
                for i in range(4):
                    last = nc.tensor.transpose(M0[:, i * P:(i + 1) * P], k_dec[:, i * P:(i + 1) * P], ident)
                last.then_inc(kdT_ps.sem, 1)

                time_major(J_Q + 1)
                pe.wait_ge(kdT_sb.sem, kdT_sb.at(l, 1))
                settle(pe)
                for n in (0, 2, 1):
                    b = (n % 2) * CH
                    for g in range(2):
                        col = (512 if n % 2 == 0 else 0) + (n // 2 * 2 + g) * P
                        for hh in range(2):
                            kd = kdT[b:b + CH, (g * 2 + n // 2) * P + hh * DK:(g * 2 + n // 2) * P + (hh + 1) * DK]
                            vv = va[b:b + CH, (n // 2) * 512 + (2 * g + hh) * DV:(n // 2) * 512 + (2 * g + hh + 1) * DV]
                            last = mm(M0[hh * DK:(hh + 1) * DK, col:col + DV], kd, vv, start=True, stop=True)
                last.then_inc(kv_ps.sem, 1)

                time_major(J_Q + 2)
                pe.wait_ge(gsc_sb.sem, gsc_sb.at(l, 1))
                pe.wait_ge(state_ready.sem, state_ready.at(l, 1))
                for hh in range(2):
                    for g in range(2):
                        for t in range(NT):
                            o = M1[:, (hh * 4 + g * 2 + t) * P:(hh * 4 + g * 2 + t + 1) * P]
                            hd = 2 * g + hh
                            last = mm(o, va[:, t * 512 + hd * DV:t * 512 + (hd + 1) * DV],
                                      gsc[:, (hh * 4 + g * 2 + t) * P:(hh * 4 + g * 2 + t + 1) * P],
                                      start=True, stop=False, skip_group_check=True)
                            for n in range(2 * t, 2 * t + 2):
                                if n:
                                    last = mm(M1[:, (hh * 4 + g * 2) * P + n * CH:(hh * 4 + g * 2) * P + (n + 1) * CH],
                                              state[hh * DK:(hh + 1) * DK, (g * 3 + n - 1) * DV:(g * 3 + n) * DV],
                                              q_dec[hh * DK:(hh + 1) * DK, g * T + n * CH:g * T + (n + 1) * CH],
                                              start=False, stop=n == 2 * t + 1, skip_group_check=True)
                last.then_inc(go_ps.sem, 1)

                time_major(J_K)
                pe.wait_ge(go_sq.sem, go_sq.at(l, 1))
                for i in range(2):
                    last = mm(M0[:, i * 512:(i + 1) * 512], c("mean"), gsq[:, i * 512:(i + 1) * 512],
                              start=True, stop=True)
                last.then_inc(gmean_ps.sem, 1)

                def att_transposes(u):
                    dst = (M1, M0)[u % 2]
                    if u == 0:
                        pe.wait_ge(brA_ready.sem, brA_ready.at(l, 1))
                    if u == 1:
                        pe.wait_ge(grms.sem, grms.at(l, 1))
                    if u >= 2:
                        pe.wait_ge(attT_sb.sem, attT_sb.at(l, u - 1))
                    pe.wait_ge(att_in.sem, att_in.at(l, u + 1))
                    for h in range(NH):
                        for t in range(NT):
                            last = nc.tensor.transpose(dst[:, h * T + t * P:h * T + (t + 1) * P],
                                                       qk_raw[u][:, t * 512 + h * P:t * 512 + (h + 1) * P], ident)
                    last.then_inc(attT_ps.sem, 1)

                for u, j in enumerate(range(J_K + 1, J_G)):
                    time_major(j)
                    att_transposes(u)
                att_transposes(5)

                def att_scores(s):
                    h, t = s // NT, s % NT
                    wide = (t + 1) * P
                    if s == 0:
                        pe.wait_ge(attT_sb.sem, attT_sb.at(l, 6))
                    if s >= 1:
                        pe.wait_ge(sc_sb.sem, sc_sb.at(l, s))
                    if s >= 2:
                        pe.wait_ge(ao_sb.sem, ao_sb.at(l, s - 1))
                    for p in range(NPAT):
                        last = mm(M0[:, p * wide:(p + 1) * wide],
                                  qk_raw[p][:, h * T + t * P:h * T + (t + 1) * P],
                                  qk_raw[NPAT + p][:, h * T:h * T + wide], start=True, stop=True)
                    last.then_inc(sc_ps.sem, 1)

                def att_prob_transposes(s):
                    t = s % NT
                    pe.wait_ge(prob_ready.sem, prob_ready.at(l, s + 1))
                    if s >= 1:
                        pe.wait_ge(probT_sb.sem, probT_sb.at(l, s))
                    for i in range(NPAT * (t + 1)):
                        last = nc.tensor.transpose(M1[:, i * P:(i + 1) * P], prob[:, i * P:(i + 1) * P], ident)
                    last.then_inc(probT_ps.sem, 1)

                def att_out(s):
                    h, t = s // NT, s % NT
                    pe.wait_ge(probT_sb.sem, probT_sb.at(l, s + 1))
                    pe.wait_ge(sc_sb.sem, sc_sb.at(l, min(s + 2, STEPS)))
                    n = NPAT * (t + 1)
                    for i in range(n):
                        p, kt = i // (t + 1), i % (t + 1)
                        last = mm(M0[:, 896:1024], v_att[p][:, kt * 512 + h * P:kt * 512 + (h + 1) * P],
                                  probT[:, i * P:(i + 1) * P], start=i == 0, stop=i == n - 1, skip_group_check=True)
                    last.then_inc(ao_ps.sem, 1)

                for i, (kind, n, half) in enumerate(GATE_JOBS):
                    j = J_G + i
                    middle = (lambda s=i - 2: att_out(s)) if 0 <= i - 2 < STEPS else None
                    if kind == "g":
                        channel_major(j, middle=middle)
                    else:
                        if n == 0 and half == 0:
                            pe.wait_ge(brA_ready.sem, brA_ready.at(l, 1))
                        if n == 1 and half == 0:
                            pe.wait_ge(brB_ready.sem, brB_ready.at(l, 1))
                        if n == 2 and half == 0:
                            pe.wait_ge(ao_sb.sem, ao_sb.at(l, STEPS))
                        branch_major(j, MIXER_UNITS.index(("branch", n)),
                                     br[n].rearrange("p (c t) -> p c t", c=WC), 512 * half, middle=middle)
                    if 0 <= i - 1 < STEPS:
                        att_prob_transposes(i - 1)
                    if i < STEPS:
                        att_scores(i)

                wo = [weights(k, WC) for k in (23, 24)]
                mg = merged.rearrange("p (c t) -> p c t", c=DC)
                for t in range(NT):
                    o = open_slot(J_OUT + t)
                    for first in (0, WC):
                        if t == 0:
                            pe.wait_ge(merged_ready.sem, merged_ready.at(l, 3 if first == 0 else 4))
                        for half in range(2):
                            for cc in range(first, first + WC):
                                last = mm(o[:, half * 512:(half + 1) * 512], mg[:, cc, t * P:(t + 1) * P],
                                          wo[cc // WC][:, cc % WC, half * 512:(half + 1) * 512],
                                          start=cc == 0, stop=cc == DC - 1)
                    last.then_inc(job_done.sem, 1)

                for t in range(NT):
                    transposes(J_NORM2 + t, 1)
                rw = c("router_w").rearrange("p (c e) -> p c e", c=DC)
                for t in range(NT):
                    taken_wait(J_NORM2 + t)
                    for cc in range(DC):
                        last = mm(M0[:, t * NE:(t + 1) * NE], hT[:, cc, t * P:(t + 1) * P], rw[:, cc, :],
                                  start=cc == 0, stop=cc == DC - 1)
                last.then_inc(logit_ps.sem, 1)
                pe.wait_ge(member_ready.sem, member_ready.at(l, 1))
                member = rt(0)
                mm(M1[:, 0:NE], c("before"), member[:, 0:NE], start=True, stop=True)
                mm(M1[:, NE:2 * NE], c("before"), member[:, NE:2 * NE], start=True, stop=False, skip_group_check=True)
                mm(M1[:, NE:2 * NE], ones, member[:, 0:NE], start=False, stop=True, skip_group_check=True)
                mm(M1[:, 512:512 + NE], ones, member[:, 0:NE], start=True, stop=False, skip_group_check=True)
                mm(M1[:, 512:512 + NE], ones, member[:, NE:2 * NE], start=False, stop=True,
                   skip_group_check=True).then_inc(rank_ps.sem, 1)

                G0, G1 = slotp

                def gather(n, chunks=range(DC)):
                    if chunks[0] == 0:
                        pe.wait_ge(sel_hot, n + 1)
                        pe.wait_ge(xg_sb, n + BASE)
                    for cc in chunks:
                        for t in range(NT):
                            last = mm(G0[:, cc * P:(cc + 1) * P], hn[:, t * D + cc * P:t * D + (cc + 1) * P],
                                      sel[:, t * P:(t + 1) * P], start=t == 0, stop=t == NT - 1)
                    if chunks[-1] == DC - 1:
                        last.then_inc(xg_ps, 1)

                def expert_loaded(slot, it):
                    pe.wait_ge(loaded[slot], expert_arrivals(slot, l, it))

                gather(start + l)
                pe.wait_ge(pairs_known, l + 2)
                settle(pe)
                end = pe.value_load(pairs_end[0:1, 0:1], min_val=0, max_val=DEPTH * NPASS * PAIRS)
                def pair(it, odd):
                    pe.wait_ge(sel_ready, it + l + 1)
                    for t in range(NT):
                        last = nc.tensor.transpose(G1[:, t * P:(t + 1) * P], selw[:, t * P:(t + 1) * P], ident)
                    last.then_inc(selT_ps, 1)
                    pe.wait_ge(xg_sb, it + l + 1 + BASE)
                    pe.wait_ge(x_add[0], it + BASE)
                    for stage, slots in enumerate((GATE_ODD if odd else GATE, UP)):
                        for cc in range(DC):
                            for i in range(2):
                                if cc == 0:
                                    expert_loaded(slots[i], it)
                                wv = slot_mem(slots[i]).rearrange("p (c n) -> p c n", c=DC)
                                last = mm(M0[i * CAP:(i + 1) * CAP, stage * FF:(stage + 1) * FF],
                                          xgT[:, cc, i * CAP:(i + 1) * CAP], wv[:, cc, :],
                                          start=cc == 0, stop=cc == DC - 1)
                        last.then_inc((gate_ps, gu_ps)[stage], 1)
                    gather(it + l + 1, range(0, 4))
                    pe.wait_ge(h_ready, it + 1)
                    pe.wait_ge(x_add[1], it + BASE)
                    for f in range(FC):
                        last = nc.tensor.transpose(M1[:, FF + f * P:FF + (f + 1) * P], hs[:, f * P:(f + 1) * P], ident)
                    last.then_inc(hT_ps, 1)
                    gather(it + l + 1, range(4, 6))
                    pe.wait_ge(hT_sb, it + 1)
                    pe.wait_ge(selT_sb, it + 1)
                    for half in range(2):
                        for f in range(FC):
                            for i in range(2):
                                if half == 0 and f == 0:
                                    expert_loaded(DOWN[i], it)
                                wv = slot_mem(DOWN[i]).rearrange("p (c n) -> p c n", c=FC)
                                last = mm(G1[i * CAP:(i + 1) * CAP, half * 512:(half + 1) * 512],
                                          hTs[:, f * P + i * CAP:f * P + (i + 1) * CAP],
                                          wv[:, f, half * 512:(half + 1) * 512], start=f == 0, stop=f == FC - 1)
                    last.then_inc(y_ps, 1)
                    gather(it + l + 1, range(6, DC))
                    pe.wait_ge(y_sb, 2 * it + 2)
                    for t in range(NT):
                        o = (M0, M1)[t]
                        for half in range(2):
                            last = mm(o[:, half * 512:(half + 1) * 512], selT[:, t * P:(t + 1) * P],
                                      ysb[:, half * 512:(half + 1) * 512], start=True, stop=True)
                        last.then_inc(mix_ps, 1)

                with pe.Fori(start, end, 2) as it:
                    pair(it, False)
                    pair(it + 1, True)

        @block.scalar
        def _(act):
            A = nc.scalar.activation
            act.wait_ge(setup_act, 1)
            A(sinb[:, :, :], sinb[:, :, :], ACT.Sin).then_inc(rope_ready, 1)
            A(cosb[:, :, :], cosb[:, :, :], ACT.Sin).then_inc(rope_ready, 1)
            act.wait_ge(x_in, 16)

            with act.Fori(0, DEPTH) as l:
                act.wait_ge(pairs_known, l + 1)
                settle(act)
                start = act.value_load(pairs_end[0:1, 0:1], min_val=0, max_val=DEPTH * NPASS * PAIRS)

                def high_part(m, qt):
                    k = SPLIT_UNITS[m]
                    slot = k % MIX_RING
                    if qt == 0:
                        act.wait_ge(loaded[slot], arrivals(slot, l, start, k // MIX_RING + 1))
                    if m:
                        if qt < QUARTERS - 1:
                            act.wait_ge(quarter_used.sem, quarter_used.at(l, (QUARTERS - 1) * (m - 1) + qt + 1))
                        else:
                            act.wait_ge(job_done.sem, job_done.at(l, SPLIT_JOBS[m - 1] + 1))
                    A(quarter_part(w_hi, m, qt), quarter_of(ring[:, slot, :], m, qt), ACT.Copy)\
                        .then_inc(hi_ready.sem, 1)

                def done(j):
                    if j in SPLIT_JOBS[:-1]:
                        for qt in range(QUARTERS - 1):
                            high_part(SPLIT_JOBS.index(j) + 1, qt)
                    act.wait_ge(job_done.sem, job_done.at(l, j + 1))
                    return slotp[j % 2]

                def last_quarter(j):
                    if j in SPLIT_JOBS[:-1]:
                        high_part(SPLIT_JOBS.index(j) + 1, QUARTERS - 1)

                def norm_stats(n, t):
                    A(blk(3 + t), xs[:, t, :], ACT.Square, accum_out=ss[:, t:t + 1]).then_inc(rms_sq.sem, 1)
                    act.wait_ge(rms_sq.sem, rms_sq.at(l, NT * n + t + 1))
                    A(sd[:, t:t + 1], ss[:, t:t + 1], ACT.Sqrt, bias=eps, scale=1.0 / D).then_inc(rms_sd.sem, 1)

                for t in range(NT):
                    act.wait_ge(x_add[t], start + BASE)
                    norm_stats(0, t)
                act.wait_ge(par_in, 16 * l + 16)
                act.wait_ge(lam_abs.sem, lam_abs.at(l, 1))
                A(spz, spz, ACT.Exp, scale=-1.0).then_inc(lam_exp.sem, 1)
                for qt in range(QUARTERS):
                    high_part(0, qt)
                for t in range(NT):
                    act.wait_ge(taken[t].sem, taken[t].at(l, 1))
                    A(hT_hi[:, :, t * P:(t + 1) * P], hT[:, :, t * P:(t + 1) * P], ACT.Copy).then_inc(hT_hi_ready.sem, 1)

                act.wait_ge(low_ps.sem, low_ps.at(l, 1))
                A(h0(0, T)[0:RANK, :], M0[0:RANK, 512:512 + T], ACT.Copy).then_inc(low_sb.sem, 1)
                o = done(J_QK)
                A(qk_ch[:, 0:512], o[:, 0:512], ACT.Copy, scale=DK ** -0.5)
                A(qk_ch[:, 512:1024], o[:, 512:1024], ACT.Copy).then_inc(taken[0].sem, 1)
                last_quarter(J_QK)
                act.wait_ge(z_abs.sem, z_abs.at(l, 1))
                A(cum, cum, ACT.Exp, scale=-1.0).then_inc(decay_exp.sem, 1)
                act.wait_ge(decay_exp.sem, decay_exp.at(l, 1))
                A(cum, cum, ACT.Ln, bias=one).then_inc(decay_ln.sem, 1)
                o = done(J_VA)
                A(va, o[:, :], ACT.Copy).then_inc(taken[1].sem, 1)
                last_quarter(J_VA)
                act.wait_ge(cum_ready.sem, cum_ready.at(l, 1))
                A(q_dec, cum, ACT.Exp, scale=1.0 / 16)
                A(k_inv, cum, ACT.Exp, scale=-1.0 / 16)
                A(etot, cum.rearrange("p (n t) -> p n t", t=CH)[:, :, CH - 1], ACT.Exp, scale=1.0 / 16)
                A(k_dec, la, ACT.Exp, scale=-1.0 / 16).then_inc(exps_ready.sem, 1)
                o = done(J_XB)
                act.wait_ge(pad_ready.sem, pad_ready.at(l, 1))
                A(xpad[:, :, TAPS - 1:], o[:, :].rearrange("p (c t) -> p c t", c=WC), ACT.Copy)\
                    .then_inc(taken[0].sem, 1)
                last_quarter(J_XB)
                o = done(J_YB)
                A(br[1], o[:, :], ACT.Gelu_apprx_tanh).then_inc(taken[1].sem, 1)
                last_quarter(J_YB)
                o = done(J_OG)
                A(og, o[:, :], ACT.Silu).then_inc(taken[0].sem, 1)
                last_quarter(J_OG)
                act.wait_ge(lru_ps.sem, lru_ps.at(l, 1))
                for cc in range(WC):
                    w = A(gate_r[:, cc * T:(cc + 1) * T], M1[:, cc * T:(cc + 1) * T], ACT.Sigmoid,
                          bias=q("b_a")[:, cc:cc + 1])
                w.then_inc(lru_sig.sem, 1)
                act.wait_ge(lru_ps.sem, lru_ps.at(l, 2))
                for cc in range(WC):
                    w = A(gate_i[:, cc * T:(cc + 1) * T], M0[:, cc * T:(cc + 1) * T], ACT.Sigmoid,
                          bias=q("b_x")[:, cc:cc + 1])
                w.then_inc(lru_sig.sem, 1)
                act.wait_ge(lru_sig.sem, lru_sig.at(l, 2))
                act.wait_ge(lam_ready.sem, lam_ready.at(l, 1))
                for cc in range(WC):
                    A(tanh_y[:, cc * T:(cc + 1) * T], gate_r[:, cc * T:(cc + 1) * T], ACT.Tanh,
                      scale=sp_pos[:, cc:cc + 1])
                for cc in range(WC):
                    w = A(gate_r[:, cc * T:(cc + 1) * T], gate_r[:, cc * T:(cc + 1) * T], ACT.Exp,
                          scale=sp_neg[:, cc:cc + 1])
                w.then_inc(lru_at.sem, 1)
                act.wait_ge(lru_m.sem, lru_m.at(l, 1))
                A(tanh_y, tanh_y, ACT.Sqrt).then_inc(lru_sqrt.sem, 1)

                def take_qk(u):
                    j = J_Q + u
                    o = done(j)
                    if u == 3:
                        act.wait_ge(brB_ready.sem, brB_ready.at(l, 1))
                    A(qk_raw[u], o[:, :], ACT.Copy).then_inc(taken[j % 2].sem, 1)
                    last_quarter(j)

                def qk_stats(u):
                    j = J_Q + u
                    if u == 0:
                        act.wait_ge(gqk_ready.sem, gqk_ready.at(l, 1))
                    if u >= 2:
                        act.wait_ge(att_in.sem, att_in.at(l, u - 1))
                    act.wait_ge(taken[j % 2].sem, taken[j % 2].at(l, j // 2 + 1))
                    for g in range(NT * NH):
                        s = slice(g * DH, (g + 1) * DH)
                        w = A(sq_att[:, s], qk_raw[u][:, s], ACT.Square, accum_out=asum[:, g:g + 1])
                    w.then_inc(att_sq.sem, 1)
                    act.wait_ge(att_sq.sem, att_sq.at(l, u + 1))
                    A(asd[u % 2], asum, ACT.Sqrt, bias=eps, scale=1.0 / DH).then_inc(att_sd.sem, 1)

                take_qk(0)
                qk_stats(0)
                act.wait_ge(kdT_ps.sem, kdT_ps.at(l, 1))
                A(kdT, M0[:, 0:512], ACT.Copy).then_inc(kdT_sb.sem, 1)
                take_qk(1)
                qk_stats(1)
                take_qk(2)
                qk_stats(2)
                act.wait_ge(go_ps.sem, go_ps.at(l, 1))
                A(gsq, M1[:, :], ACT.Square).then_inc(go_sq.sem, 1)
                take_qk(3)
                act.wait_ge(gmean_ps.sem, gmean_ps.at(l, 1))
                A(gsq, M0[:, :], ACT.Sqrt, bias=eps).then_inc(grms.sem, 1)
                qk_stats(3)
                for u in range(6):
                    j = J_K + 1 + u
                    if u < 2:
                        take_qk(4 + u)
                        qk_stats(4 + u)
                    elif j < J_G:
                        o = done(j)
                        if u == 4:
                            act.wait_ge(att_in.sem, att_in.at(l, 6))
                        A(v_att[u - 2], o[:, :], ACT.Copy).then_inc(taken[j % 2].sem, 1)
                        last_quarter(j)
                    act.wait_ge(attT_ps.sem, attT_ps.at(l, u + 1))
                    A(qk_raw[u], (M1, M0)[u % 2][:, :], ACT.Copy).then_inc(attT_sb.sem, 1)

                for i in range(len(GATE_JOBS)):
                    kind, n, half = GATE_JOBS[i]
                    j = J_G + i
                    s = i - 2
                    if 0 <= s < STEPS:
                        h, t = s // NT, s % NT
                        act.wait_ge(ao_ps.sem, ao_ps.at(l, s + 1))
                        A(br[2][:, h * T + t * P:h * T + (t + 1) * P], M0[:, 896:1024], ACT.Copy)\
                            .then_inc(ao_sb.sem, 1)
                    if kind == "g":
                        o = done(j)
                        if n == 0 and half == 1:
                            act.wait_ge(brA_ready.sem, brA_ready.at(l, 1))
                        if n == 1:
                            before = J_G + GATE_JOBS.index(("p", 0, half))
                            act.wait_ge(taken[before % 2].sem, taken[before % 2].at(l, before // 2 + 1))
                        if n == 2:
                            act.wait_ge(merged_ready.sem, merged_ready.at(l, half + 1))
                        A(sig[half], o[:, :], ACT.Sigmoid).then_inc(taken[j % 2].sem, 1)
                        last_quarter(j)
                    s = i - 1
                    if 0 <= s < STEPS:
                        wide = NPAT * (s % NT + 1) * P
                        act.wait_ge(probT_ps.sem, probT_ps.at(l, s + 1))
                        if s >= 1:
                            act.wait_ge(ao_ps.sem, ao_ps.at(l, s))
                        A(probT[:, 0:wide], M1[:, 0:wide], ACT.Copy).then_inc(probT_sb.sem, 1)
                    s = i
                    if s < STEPS:
                        wide = NPAT * (s % NT + 1) * P
                        act.wait_ge(sc_max.sem, sc_max.at(l, s + 1))
                        if s >= 1:
                            act.wait_ge(probT_ps.sem, probT_ps.at(l, s))
                        A(prob[:, 0:wide], sc[:, 0:wide], ACT.Exp, bias=anegm, scale=ASCALE,
                          accum_out=aden).then_inc(sc_exp.sem, 1)

                for t in range(NT):
                    j = J_OUT + t
                    act.wait_ge(taken[j % 2].sem, taken[j % 2].at(l, j // 2 + 1))
                    norm_stats(1, t)
                act.wait_ge(rt_max.sem, rt_max.at(l, 1))
                A(rt(2), rt(1), ACT.Exp).then_inc(rt_exp.sem, 1)

                act.wait_ge(pairs_known, l + 2)
                settle(act)
                end = act.value_load(pairs_end[0:1, 0:1], min_val=0, max_val=DEPTH * NPASS * PAIRS)
                with act.Fori(start, end) as it:
                    act.wait_ge(selT_ps, it + 1 + BASE)
                    act.wait_ge(mix_ps, NT * it + BASE)
                    A(selT, slotp[1][:, 0:NT * P], ACT.Copy).then_inc(selT_sb, 1)
                    act.wait_ge(gate_ps, it + 1 + BASE)
                    A(silu_g, M0[:, 0:FF], ACT.Silu).then_inc(silu_ready, 1)
                    act.wait_ge(hT_ps, it + 1)
                    act.wait_ge(y_ps, it + BASE)
                    A(hTs, M1[:, FF:FF + FC * P], ACT.Copy).then_inc(hT_sb, 1)
                    act.wait_ge(y_ps, it + 1 + BASE)
                    A(ysb[:, 0:512], slotp[1][:, 0:512], ACT.Copy).then_inc(y_sb, 1)

        @block.vector
        def _(dve):
            v = nc.vector
            setup = [0]

            def first(ins):
                setup[0] += 1
                ins.then_inc(setup_step, 1)
                dve.wait_ge(setup_step, setup[0])

            first(v.memset(total_pairs, 0.0))
            v.tensor_copy(pairs_end[0:1, 0:1], total_pairs).then_inc(pairs_known, 1)
            dve.wait_ge(consts_in, 32)
            first(v.tensor_copy(posf, pos_i[:, :]))
            for t in range(NT):
                first(v.tensor_scalar(sinb[:, t, :], c("freq"), posf[:, t:t + 1], None, ALU.mult))
            turns = rope_tmp[:, 0, 0:NT * ROPE].rearrange("p (t r) -> p t r", t=NT)
            first(v.tensor_scalar(turns, sinb[:, :, :], float(np.float32(1 / (2 * np.pi))), None, ALU.mult))
            first(v.tensor_scalar(turns, turns, float(1.5 * 2 ** 23), None, ALU.add))
            first(v.tensor_scalar(turns, turns, float(-1.5 * 2 ** 23), None, ALU.add))
            rest = 2 * np.pi
            for bits in (8, 8, 8, 24):
                scale = 2.0 ** (bits - 1 - np.floor(np.log2(abs(rest))))
                part = np.rint(rest * scale) / scale
                rest -= part
                first(v.scalar_tensor_tensor(out=sinb[:, :, :], in0=turns, scalar=float(-part), in1=sinb[:, :, :],
                                             op0=ALU.mult, op1=ALU.add))
            below_pi = float(np.nextafter(np.float32(np.pi), np.float32(0)))
            first(v.tensor_scalar(sinb[:, :, :], sinb[:, :, :], below_pi, -below_pi, ALU.min, ALU.max))
            first(v.scalar_tensor_tensor(out=cosb[:, :, :], in0=sinb[:, :, :], scalar=-1.0, in1=sinb[:, :, :],
                                         op0=ALU.mult, op1=ALU.min))
            v.tensor_scalar(cosb[:, :, :], cosb[:, :, :], float(np.pi / 2), None, ALU.add).then_inc(setup_act, 1)
            dve.wait_ge(rope_ready, 2)

            with dve.Fori(0, DEPTH) as l:
                dve.wait_ge(pairs_known, l + 1)
                settle(dve)
                start = dve.value_load(pairs_end[0:1, 0:1], min_val=0, max_val=DEPTH * NPASS * PAIRS)
                step = [0]

                def link(ins):
                    step[0] += 1
                    ins.then_inc(dve_step.sem, 1)
                    dve.wait_ge(dve_step.sem, dve_step.at(l, step[0]))

                def done(j):
                    dve.wait_ge(job_done.sem, job_done.at(l, j + 1))
                    return slotp[j % 2]

                def take_done(j):
                    dve.wait_ge(taken[j % 2].sem, taken[j % 2].at(l, j // 2 + 1))

                def diagonal(n, t):
                    dve.wait_ge(rms_sd.sem, rms_sd.at(l, NT * n + t + 1))
                    link(v.reciprocal(rinv[:, t:t + 1], sd[:, t:t + 1]))
                    v.tensor_scalar(diag[:, t * P:(t + 1) * P], ident, rinv[:, t:t + 1], None,
                                    ALU.mult).then_inc(diag_ready.sem, 1)

                low_parts = [0]

                def split_to(m, qt):
                    for i in range(low_parts[0], QUARTERS * m + qt + 1):
                        n, part = i // QUARTERS, i % QUARTERS
                        dve.wait_ge(hi_ready.sem, hi_ready.at(l, i + 1))
                        v.tensor_tensor(quarter_part(w_lo, n, part),
                                        quarter_of(ring[:, SPLIT_UNITS[n] % MIX_RING, :], n, part),
                                        quarter_part(w_hi, n, part), ALU.subtract).then_inc(lo_ready.sem, 1)
                    low_parts[0] = max(low_parts[0], QUARTERS * m + qt + 1)

                def take_hT(n, t, gain):
                    j = (J_NORM1, J_NORM2)[n] + t
                    o = done(j)
                    v.tensor_tensor(hT[:, :, t * P:(t + 1) * P], o[:, :].rearrange("p (c t) -> p c t", c=DC),
                                    gain.unsqueeze(2).broadcast_to((P, DC, P)), ALU.mult)\
                        .then_inc(taken[j % 2].sem, 1)

                dve.wait_ge(x_in, 16)
                for t in range(NT):
                    diagonal(0, t)
                dve.wait_ge(par_in, 16 * l + 16)
                v.memset(xpad[:, :, 0:TAPS - 1], 0.0).then_inc(pad_ready.sem, 1)
                v.scalar_tensor_tensor(out=spz, in0=q("lam"), scalar=-1.0, in1=q("lam"), op0=ALU.mult,
                                       op1=ALU.max).then_inc(lam_abs.sem, 1)
                split_to(0, 0)
                for t in range(NT):
                    take_hT(0, t, q("gain1"))
                for t in range(NT):
                    s = slice(t * P, (t + 1) * P)
                    dve.wait_ge(hT_hi_ready.sem, hT_hi_ready.at(l, t + 1))
                    v.tensor_tensor(hT_lo[:, :, s], hT[:, :, s], hT_hi[:, :, s], ALU.subtract)\
                        .then_inc(hT_lo_ready.sem, 1)
                split_to(0, QUARTERS - 1)
                dve.wait_ge(lam_exp.sem, lam_exp.at(l, 1))
                link(v.tensor_scalar(sps, spz, 2.0, None, ALU.add))
                link(v.reciprocal(sps, sps))
                link(v.tensor_tensor(sps, sps, spz, ALU.mult))
                link(v.tensor_tensor(sp2, sps, sps, ALU.mult))
                link(v.tensor_scalar(spp, sp2, 1.0 / 17, None, ALU.mult))
                for odd in (15, 13, 11, 9, 7, 5, 3):
                    link(v.scalar_tensor_tensor(out=spp, in0=spp, scalar=1.0 / odd, in1=sp2, op0=ALU.add, op1=ALU.mult))
                link(v.scalar_tensor_tensor(out=spp, in0=spp, scalar=1.0, in1=sps, op0=ALU.add, op1=ALU.mult))
                link(v.tensor_scalar(sps, q("lam"), -1.0, 0.0, ALU.mult, ALU.max))
                link(v.scalar_tensor_tensor(out=spp, in0=spp, scalar=2.0, in1=sps, op0=ALU.mult, op1=ALU.add))
                link(v.tensor_scalar(sp_pos, spp, 8.0, None, ALU.mult))
                v.tensor_scalar(sp_neg, spp, -8.0, None, ALU.mult).then_inc(lam_ready.sem, 1)

                split_to(1, 2)
                dve.wait_ge(z_ps.sem, z_ps.at(l, 1))
                for g in range(2):
                    link(v.tensor_scalar(la[:, g * T:(g + 1) * T], M0[:, g * T:(g + 1) * T],
                                         q("gate_b")[:, g:g + 1], None, ALU.add))
                v.scalar_tensor_tensor(out=cum, in0=la, scalar=-1.0, in1=la, op0=ALU.mult, op1=ALU.max)\
                    .then_inc(z_abs.sem, 1)
                split_to(1, 3)
                dve.wait_ge(decay_ln.sem, decay_ln.at(l, 1))
                link(v.scalar_tensor_tensor(out=la, in0=la, scalar=0.0, in1=cum, op0=ALU.min, op1=ALU.subtract))
                for n in range(NT * T // CH):
                    s = slice(n * CH, (n + 1) * CH)
                    w = v.tensor_tensor_scan(cum[:, s], ones[:, 0:CH], la[:, s], 0.0, ALU.mult, ALU.add)
                link(w)
                cumv = cum.rearrange("p (n t) -> p n t", t=CH)
                v.tensor_tensor(la.rearrange("p (n t) -> p n t", t=CH), cumv,
                                cumv[:, :, CH - 1:CH].broadcast_to((P, NT * T // CH, CH)), ALU.subtract)\
                    .then_inc(cum_ready.sem, 1)

                split_to(2, 3)
                dve.wait_ge(exps_ready.sem, exps_ready.at(l, 1))
                take_done(J_QK)
                v.tensor_tensor(k_dec, k_dec, qk_ch[:, 512:1024], ALU.mult)
                v.tensor_tensor(k_inv, k_inv, qk_ch[:, 512:1024], ALU.mult)
                v.tensor_tensor(q_dec, q_dec, qk_ch[:, 0:512], ALU.mult).then_inc(gqk_ready.sem, 1)

                split_to(3, 2)
                take_done(J_XB)
                split_to(3, 3)
                for cc in range(WC):
                    if cc:
                        split_to(4, cc - 1)
                    o = xc[:, cc * T:(cc + 1) * T]
                    link(v.tensor_scalar(o, xpad[:, cc, 0:T], q("conv_w")[:, cc:cc + 1],
                                         q("conv_b")[:, cc:cc + 1], ALU.mult, ALU.add))
                    for k in range(1, TAPS):
                        w = v.scalar_tensor_tensor(out=o, in0=xpad[:, cc, k:k + T],
                                                   scalar=q("conv_w")[:, k * WC + cc:k * WC + cc + 1],
                                                   in1=o, op0=ALU.mult, op1=ALU.add)
                        if (cc, k) != (WC - 1, TAPS - 1):
                            link(w)
                w.then_inc(xc_ready.sem, 1)

                split_to(5, 2)
                dve.wait_ge(lru_at.sem, lru_at.at(l, 1))
                link(v.tensor_tensor(a_sq, gate_r, gate_r, ALU.mult))
                v.scalar_tensor_tensor(out=tanh_y, in0=a_sq, scalar=1.0, in1=tanh_y, op0=ALU.add,
                                       op1=ALU.mult).then_inc(lru_m.sem, 1)
                split_to(5, 3)
                dve.wait_ge(xc_ready.sem, xc_ready.at(l, 1))
                link(v.tensor_tensor(gate_i, gate_i, xc, ALU.mult))
                dve.wait_ge(lru_sqrt.sem, lru_sqrt.at(l, 1))
                link(v.tensor_tensor(gate_i, gate_i, tanh_y, ALU.mult))
                for cc in range(WC):
                    s = slice(cc * T, (cc + 1) * T)
                    w = v.tensor_tensor_scan(xc[:, s], gate_r[:, s], gate_i[:, s], 0.0, ALU.mult, ALU.add)
                link(w)
                take_done(J_YB)
                v.tensor_tensor(br[1], br[1], xc, ALU.mult).then_inc(brB_ready.sem, 1)

                def qk_norm(u):
                    split_to(6 + u, 3)
                    dve.wait_ge(att_sd.sem, att_sd.at(l, u + 1))
                    link(v.reciprocal(arinv, asd[u % 2]))
                    raw = qk_raw[u].rearrange("p (g d) -> p g d", d=DH)
                    for g in range(NT * NH):
                        w = v.scalar_tensor_tensor(out=raw[:, g], in0=raw[:, g], scalar=arinv[:, g:g + 1],
                                                   in1=q("q_gain" if u < NPAT else "k_gain"),
                                                   op0=ALU.mult, op1=ALU.mult)
                    link(w)
                    x1 = raw[:, :, 0:ROPE].rearrange("p (t h) d -> p t h d", t=NT)
                    x2 = raw[:, :, ROPE:2 * ROPE].rearrange("p (t h) d -> p t h d", t=NT)
                    cs = cosb[:, :, :].unsqueeze(2).broadcast_to((P, NT, NH, ROPE))
                    sn = sinb[:, :, :].unsqueeze(2).broadcast_to((P, NT, NH, ROPE))
                    tmp = [rope_tmp[:, i, :].rearrange("p (t h d) -> p t h d", t=NT, h=NH) for i in range(4)]
                    v.tensor_tensor(tmp[0], x1, cs, ALU.mult)
                    v.tensor_tensor(tmp[1], x2, sn, ALU.mult)
                    v.tensor_tensor(tmp[2], x2, cs, ALU.mult)
                    link(v.tensor_tensor(tmp[3], x1, sn, ALU.mult))
                    v.tensor_tensor(x1, tmp[0], tmp[1], ALU.subtract)
                    v.tensor_tensor(x2, tmp[2], tmp[3], ALU.add).then_inc(att_in.sem, 1)

                qk_norm(0)
                dve.wait_ge(gsc_ps.sem, gsc_ps.at(l, 1))
                mask = c("gla_mask").unsqueeze(1).broadcast_to((P, 4, P))
                for i in range(2):
                    w = v.tensor_tensor(gsc[:, i * 512:(i + 1) * 512].rearrange("p (n q) -> p n q", n=4),
                                        M1[:, i * 512:(i + 1) * 512].rearrange("p (n q) -> p n q", n=4),
                                        mask, ALU.mult)
                w.then_inc(gsc_sb.sem, 1)
                qk_norm(1)
                dve.wait_ge(kv_ps.sem, kv_ps.at(l, 1))
                for g in range(2):
                    st = [state[:, (g * 3 + n) * DV:(g * 3 + n + 1) * DV] for n in range(3)]
                    link(v.tensor_copy(st[0], M0[:, 512 + g * P:512 + (g + 1) * P]))
                    link(v.scalar_tensor_tensor(out=st[1], in0=st[0], scalar=etot[:, g * 4 + 1:g * 4 + 2],
                                                in1=M0[:, g * P:(g + 1) * P], op0=ALU.mult, op1=ALU.add))
                    w = v.scalar_tensor_tensor(out=st[2], in0=st[1], scalar=etot[:, g * 4 + 2:g * 4 + 3],
                                               in1=M0[:, 768 + g * P:768 + (g + 1) * P], op0=ALU.mult, op1=ALU.add)
                w.then_inc(state_ready.sem, 1)
                qk_norm(2)
                split_to(9, 3)
                dve.wait_ge(grms.sem, grms.at(l, 1))
                take_done(J_OG)
                link(v.reciprocal(gsq, gsq))
                link(v.scalar_tensor_tensor(out=gsq, in0=M1[:, :], scalar=q("out_gain"), in1=gsq,
                                            op0=ALU.mult, op1=ALU.mult))
                for hh in range(2):
                    w = v.tensor_tensor(br[0].rearrange("p (g h t) -> p g h t", g=2, h=2)[:, :, hh, :],
                                        gsq[:, hh * 512:(hh + 1) * 512].rearrange("p (g t) -> p g t", g=2),
                                        og.rearrange("p (g h t) -> p g h t", g=2, h=2)[:, :, hh, :], ALU.mult)
                w.then_inc(brA_ready.sem, 1)
                for u in (3, 4, 5):
                    qk_norm(u)

                for i in range(len(GATE_JOBS)):
                    kind, n, half = GATE_JOBS[i]
                    j = J_G + i
                    if j in SPLIT_JOBS[:-1]:
                        split_to(SPLIT_JOBS.index(j) + 1, 3)
                    if kind == "p":
                        o = done(j)
                        take_done(J_G + GATE_JOBS.index(("g", n, half)))
                        mg = merged[:, half * BLK:(half + 1) * BLK]
                        if n == 0:
                            v.tensor_tensor(mg, sig[half], o[:, :], ALU.mult).then_inc(taken[j % 2].sem, 1)
                        else:
                            v.tensor_tensor(sig[half], sig[half], o[:, :], ALU.mult).then_inc(taken[j % 2].sem, 1)
                            take_done(j)
                            if n > 1:
                                dve.wait_ge(merged_ready.sem, merged_ready.at(l, half + 1))
                            v.tensor_tensor(mg, mg, sig[half], ALU.add).then_inc(merged_ready.sem, 1)
                    if i < STEPS:
                        s, t = i, i % NT
                        wide = NPAT * (t + 1) * P
                        dve.wait_ge(sc_ps.sem, sc_ps.at(l, s + 1))
                        if s >= 1:
                            dve.wait_ge(sc_exp.sem, sc_exp.at(l, s))
                        band = c("band").rearrange("p (n k) -> p n k", n=NPAT)[:, :, (NT - 1 - t) * P:]
                        v.tensor_tensor(sc[:, 0:wide].rearrange("p (n k) -> p n k", n=NPAT),
                                        M0[:, 0:wide].rearrange("p (n k) -> p n k", n=NPAT), band, ALU.add)\
                            .then_inc(sc_sb.sem, 1)
                        dve.wait_ge(sc_sb.sem, sc_sb.at(l, s + 1))
                        link(v.tensor_reduce(amax, sc[:, 0:wide], AX.X, ALU.max))
                        v.tensor_scalar(anegm, amax, -ASCALE, None, ALU.mult).then_inc(sc_max.sem, 1)
                        dve.wait_ge(sc_exp.sem, sc_exp.at(l, s + 1))
                        link(v.reciprocal(arden, aden))
                        v.tensor_scalar(prob[:, 0:wide], prob[:, 0:wide], arden, None, ALU.mult)\
                            .then_inc(prob_ready.sem, 1)

                for t in range(NT):
                    j = J_OUT + t
                    o = done(j)
                    v.tensor_tensor(xs[:, t, :], xs[:, t, :], o[:, :], ALU.add).then_inc(taken[j % 2].sem, 1)
                    diagonal(1, t)
                dve.wait_ge(gain2_in, 16 * l + 16)
                for t in range(NT):
                    link(v.tensor_scalar(hn[:, t * D:(t + 1) * D], xs[:, t, :], rinv[:, t:t + 1], None, ALU.mult))
                    take_hT(1, t, g2[:, :])

                def e16(i):
                    return rt(i).rearrange("p (t e) -> p t e", t=NT)

                def e4(i, n=NT * NG):
                    return rt(i, n).rearrange("p (t g) -> p t g", t=NT)

                def per_tile(ap):
                    return ap.unsqueeze(2).broadcast_to((P, NT, NE))

                member, logit, ex, top1, top2 = (rt(i) for i in range(5))
                red = [blk(5, off=512 + 8 * i, width=NT) for i in range(8)]
                dve.wait_ge(logit_ps.sem, logit_ps.at(l, 1))
                link(v.tensor_tensor(e16(1), M0[:, 0:NT * NE].rearrange("p (t e) -> p t e", t=NT),
                                     c("router_b").unsqueeze(1).broadcast_to((P, NT, NE)), ALU.add))
                link(v.tensor_reduce(red[0], e16(1), AX.X, ALU.max))
                v.tensor_tensor(e16(1), e16(1), per_tile(red[0]), ALU.subtract).then_inc(rt_max.sem, 1)
                dve.wait_ge(rt_exp.sem, rt_exp.at(l, 1))
                link(v.tensor_reduce(red[1], e16(2), AX.X, ALU.add))
                link(v.reciprocal(red[2], red[1]))
                link(v.tensor_tensor(e16(2), e16(2), per_tile(red[2]), ALU.mult))
                ev = ex.rearrange("p (g e) -> p g e", e=NE // NG)
                hi1, lo1, hi2, lo2, m1, m2, gs, gsel = (blk(5, off=608 + 8 * i, width=8) for i in range(8))
                v.tensor_tensor(hi1, ev[:, :, 0], ev[:, :, 1], ALU.max)
                v.tensor_tensor(lo1, ev[:, :, 0], ev[:, :, 1], ALU.min)
                v.tensor_tensor(hi2, ev[:, :, 2], ev[:, :, 3], ALU.max)
                link(v.tensor_tensor(lo2, ev[:, :, 2], ev[:, :, 3], ALU.min))
                v.tensor_tensor(m1, hi1, hi2, ALU.max)
                v.tensor_tensor(m2, hi1, hi2, ALU.min)
                link(v.tensor_tensor(lo1, lo1, lo2, ALU.max))
                link(v.tensor_tensor(m2, m2, lo1, ALU.max))
                link(v.tensor_tensor(gs, m1, m2, ALU.add))

                def first_max(dst, src, keys, top, shape):
                    key = blk(5, off=672, width=shape[1] * shape[2]).rearrange("p (t e) -> p t e", t=NT)
                    kt = blk(5, off=712, width=NT)
                    link(v.tensor_reduce(top, src, AX.X, ALU.max))
                    link(v.tensor_tensor(key, src, top.unsqueeze(2).broadcast_to(shape), ALU.is_equal))
                    link(v.tensor_tensor(key, key, keys.unsqueeze(1).broadcast_to(shape), ALU.mult))
                    link(v.tensor_reduce(kt, key, AX.X, ALU.max))
                    link(v.tensor_tensor(dst, key, kt.unsqueeze(2).broadcast_to(shape), ALU.is_equal))

                gsv = gs.rearrange("p (t g) -> p t g", t=NT)
                gselv = gsel.rearrange("p (t g) -> p t g", t=NT)
                first_max(gselv, gsv, c("key4"), red[3], (P, NT, NG))
                gb = gsel.unsqueeze(2).broadcast_to((P, NT * NG, NE // NG))
                link(v.tensor_tensor(ev, ev, gb, ALU.mult))
                link(v.tensor_tensor(ev, ev, gb, ALU.add))
                link(v.tensor_scalar(ev, ev, -1.0, None, ALU.add))
                first_max(e16(3), e16(2), c("key16"), red[4], (P, NT, NE))
                link(v.scalar_tensor_tensor(out=ex, in0=top1, scalar=-4.0, in1=ex, op0=ALU.mult, op1=ALU.add))
                first_max(e16(4), e16(2), c("key16"), red[5], (P, NT, NE))
                link(v.tensor_tensor(red[6], red[4], red[5], ALU.add))
                link(v.reciprocal(red[6], red[6]))
                v.tensor_tensor(red[4], red[4], red[6], ALU.mult)
                v.tensor_tensor(red[5], red[5], red[6], ALU.mult)
                v.tensor_tensor(member, top1, top2, ALU.add).then_inc(member_ready.sem, 1)
                dve.wait_ge(member_ready.sem, member_ready.at(l, 1))
                link(v.tensor_tensor(e16(3), e16(3), per_tile(red[4]), ALU.mult))
                link(v.tensor_tensor(e16(4), e16(4), per_tile(red[5]), ALU.mult))
                link(v.tensor_tensor(gw2, e16(3).rearrange("p t e -> p e t"), e16(4).rearrange("p t e -> p e t"),
                                     ALU.add))
                dve.wait_ge(rank_ps.sem, rank_ps.at(l, 1))
                link(v.scalar_tensor_tensor(out=logit, in0=M1[:, 0:NT * NE], scalar=1.0, in1=member,
                                            op0=ALU.add, op1=ALU.mult))
                link(v.tensor_scalar(rank2, e16(1).rearrange("p t e -> p e t"), -1.0, None, ALU.add))

                def select(n, it):
                    e = 2 * (it % PAIRS)
                    base = nc.s_assert_within((it - start) // PAIRS * CAP, 0, T,
                                              skip_runtime_bounds_check_because="npass is at most T / CAP")
                    for i in range(2):
                        sv = sel.rearrange("p (t i s) -> p i t s", t=NT, i=2)[:, i]
                        w = v.tensor_tensor(sv, c("iota")[:, bass.ds(base, CAP)].unsqueeze(1).broadcast_to((P, NT, CAP)),
                                            rank2[:, bass.ds(e + i, 1), :].rearrange("p o t -> p (o t)").unsqueeze(2)
                                            .broadcast_to((P, NT, CAP)), ALU.is_equal)
                    w.then_inc(sel_hot, 1)
                    dve.wait_ge(sel_hot, n + 1)
                    for i in range(2):
                        w = v.tensor_tensor(selw.rearrange("p (t i s) -> p i t s", t=NT, i=2)[:, i],
                                            sel.rearrange("p (t i s) -> p i t s", t=NT, i=2)[:, i],
                                            gw2[:, bass.ds(e + i, 1), :].rearrange("p o t -> p (o t)").unsqueeze(2)
                                            .broadcast_to((P, NT, CAP)), ALU.mult)
                    w.then_inc(sel_ready, 1)

                def take_gather(n):
                    dve.wait_ge(xg_ps, n + 1 + BASE)
                    v.tensor_tensor(xgT, slotp[0][:, :].rearrange("p (c s) -> p c s", c=DC),
                                    g2[:, :].unsqueeze(2).broadcast_to((P, DC, P)), ALU.mult).then_inc(xg_sb, 1)

                select(start + l, start)
                link(v.tensor_reduce(mxc, M1[0:1, 512:512 + NE], AX.X, ALU.max))
                link(v.tensor_scalar(cmp4, c("caps")[0:1, :], mxc, None, ALU.is_lt))
                link(v.tensor_reduce(npass, cmp4, AX.X, ALU.add))
                link(v.scalar_tensor_tensor(out=total_pairs, in0=npass, scalar=float(PAIRS), in1=total_pairs,
                                            op0=ALU.mult, op1=ALU.add))
                v.tensor_copy(pairs_end[0:1, 0:1], total_pairs).then_inc(pairs_known, 1)
                dve.wait_ge(pairs_known, l + 2)
                settle(dve)
                end = dve.value_load(pairs_end[0:1, 0:1], min_val=0, max_val=DEPTH * NPASS * PAIRS)
                take_gather(start + l)
                with dve.Fori(start, end) as it:
                    dve.wait_ge(selT_ps, it + 1 + BASE)
                    dve.wait_ge(xg_ps, it + l + 1 + BASE)
                    select(it + l + 1, it + 1)
                    dve.wait_ge(silu_ready, it + 1)
                    dve.wait_ge(gu_ps, it + 1 + BASE)
                    v.tensor_tensor(hs, silu_g, M0[:, FF:2 * FF], ALU.mult).then_inc(h_ready, 1)
                    dve.wait_ge(y_ps, it + 1 + BASE)
                    v.tensor_copy(ysb[:, 512:1024], slotp[1][:, 512:1024]).then_inc(y_sb, 1)
                    take_gather(it + l + 1)
                    for t in range(NT):
                        dve.wait_ge(mix_ps, NT * it + t + 1 + BASE)
                        v.tensor_tensor(xs[:, t, :], xs[:, t, :], (M0, M1)[t][:, :], ALU.add).then_inc(x_add[t], 1)
                assert step[0] == dve_step.per, step[0]


def constants(router_w, router_b):
    k = np.zeros((P, NCONST), np.float32)

    def put(name, value):
        a, b = CONST[name]
        k[:, a:b] = value

    i, j = np.arange(P)[:, None], np.arange(P)[None, :]
    put("ident", i == j)
    put("mean", 1.0 / P)
    put("ones", 1.0)
    put("before", i < j)
    put("gla_mask", (i // CH == j // CH) & (i <= j))
    dist = P + np.arange(P)[:, None] - np.arange(T)[None, :]
    band = [np.where((dist >= 0) & (dist % dil == 0) & (dist // dil <= window // dil), 0.0, -1e30)
            for window, dil in PATTERNS]
    put("band", np.concatenate(band, 1))
    put("iota", np.arange(T + CAP)[None, :])
    put("caps", (CAP * np.arange(NPASS))[None, :])
    put("key4", (NG - np.arange(NG))[None, :])
    put("key16", (NE - np.arange(NE))[None, :])
    put("freq", (THETA ** (-np.arange(ROPE) / ROPE))[None, :])
    put("eps", EPS)
    put("one", 1.0)
    put("router_w", router_w.reshape(DC, P, NE).transpose(1, 0, 2).reshape(P, -1))
    put("router_b", router_b[None, :])
    return k


def parameters(a):
    k = np.zeros((DEPTH, P, NPAR), np.float32)
    for l in range(DEPTH):
        def put(name, value, rows=P):
            s, e = PAR[name]
            k[l, 0:rows, s:e] = value

        def cols(v):
            return v.reshape(-1, P).T

        def blocks(w):
            o = np.zeros((P, WC, P), np.float32)
            for n in range(2 * WC):
                b = (n % 2) * 64
                o[b:b + 64, n // 2, b:b + 64] = w[n]
            return o.reshape(P, -1)

        put("gain1", cols(a["norm1_gain"][l]))
        put("gate_b", cols(a["gla_gate_bias"][l]))
        put("out_gain", cols(a["gla_out_gain"][l]))
        put("conv_w", a["lru_conv_w"][l].reshape(TAPS, WC, P).transpose(2, 0, 1).reshape(P, -1))
        put("conv_b", cols(a["lru_conv_b"][l]))
        put("b_a", cols(a["lru_b_a"][l]))
        put("b_x", cols(a["lru_b_x"][l]))
        put("lam", cols(a["lru_lambda"][l]))
        put("w_a", blocks(a["lru_w_a"][l]))
        put("w_x", blocks(a["lru_w_x"][l]))
        put("q_gain", a["q_norm_gain"][l][None, :])
        put("k_gain", a["k_norm_gain"][l][None, :])
        put("low", a["w_in"][l][:, C_LOW:C_LOW + RANK].reshape(DC, P, RANK).transpose(1, 0, 2).reshape(P, -1))
        put("gate_up", a["gla_gate_up"][l], RANK)
    return k


def kernel(**inputs):
    import concourse.bacc as _bacc
    from concourse.bass_utils import run_bass_kernel_spmd as _run

    a = {name: np.ascontiguousarray(v) for name, v in inputs.items()}
    arrays = {
        "x": a["x"], "positions": a["positions"],
        "const": constants(a["router_w"], a["router_b"]), "par": parameters(a),
        "gain2": np.ascontiguousarray(a["norm2_gain"].reshape(DEPTH, DC, P).transpose(0, 2, 1)),
    }
    for name in ("w_in", "w_branch", "w_out", "w_gate", "w_up", "w_down"):
        arrays[name] = a[name]
    nc = _bacc.Bacc("TRN2", target_bir_lowering=False, num_devices=1)
    args = [nc.dram_tensor(f"in_{n}", v.shape, mybir.dt.from_np(v.dtype), kind="ExternalInput").ap()
            for n, v in arrays.items()]
    out = nc.dram_tensor("out_x", a["x"].shape, F32, kind="ExternalOutput").ap()
    build(nc, *args, out)
    r = _run(nc, [{f"in_{n}": v for n, v in arrays.items()}], core_ids=[0])
    return r.results[0]["out_x"]
```

```python
from contextlib import ExitStack

import numpy as np
import concourse.bass as bass
from concourse import mybir

F32 = mybir.dt.float32
F32R = mybir.dt.float32r
I32 = mybir.dt.int32
ALU = mybir.AluOpType
ACT = mybir.ActivationFunctionType
AX = mybir.AxisListType

P = 128
D = 1024
T = 256
NT = T // P
DC = D // P
DEPTH = 2
EPS = 1e-6
HG, DK, DV, CH = 4, 64, 128, 64
RANK = 16
W = 512
WC = W // P
TAPS = 4
NPAT, NH, DH = 3, 4, 128
PATTERNS = ((128, 1), (512, 4), (2048, 16))
ROPE = 16
THETA = 500000.0
ASCALE = float(DH) ** -0.5
NE, NG, FF = 16, 4, 512
FC = FF // P
CAP = 64
PAIRS = NE // 2
NPASS = T // CAP
UNIT = 4096
BLK = 1024
RING = 9
MIX_RING = 3
BASE = 1

C_QK, C_VA, C_OG, C_LOW = 0, 512, 1024, 1536
C_XB = C_LOW + RANK
C_YB = C_XB + W
C_Q = C_YB + W
C_K = C_Q + NPAT * 512
C_V = C_K + NPAT * 512
C_G = C_V + NPAT * 512

TIME_MAJOR = {C_VA} | {a + 512 * p for a in (C_Q, C_K, C_V) for p in range(NPAT)}

MIXER_UNITS = ([("in", C_QK), ("in", C_VA), ("in", C_XB), ("in", C_YB), ("in", C_OG)]
               + [("in", C_Q + 512 * p) for p in range(NPAT)]
               + [("in", C_K + 512 * p) for p in range(NPAT)]
               + [("in", C_V + 512 * p) for p in range(NPAT)]
               + [("in", C_G), ("branch", 0), ("in", C_G + 512),
                  ("in", C_G + 1024), ("branch", 1), ("in", C_G + 1536),
                  ("in", C_G + 2048), ("in", C_G + 2560), ("branch", 2),
                  ("out", 0), ("out", 1)])
MIX_USES = [len(MIXER_UNITS[s::MIX_RING]) if s < MIX_RING else 0 for s in range(RING)]
GATE, UP, DOWN = (0, 1), (2, 3), (4, 5)
EARLY, EARLY_ODD, LATE = (0, 1, 2), (6, 7, 8), (3, 4, 5)
EXPERT_SLOTS = ((GATE, UP), ((6, 7), (8, 3)))

J_NORM1, J_QK, J_VA, J_XB, J_YB, J_OG, J_Q, J_K, J_V, J_G = 0, 2, 3, 4, 5, 6, 7, 10, 13, 16
GATE_JOBS = (("g", 0, 0), ("p", 0, 0), ("g", 0, 1), ("p", 0, 1),
             ("g", 1, 0), ("p", 1, 0), ("g", 1, 1), ("p", 1, 1),
             ("g", 2, 0), ("g", 2, 1), ("p", 2, 0), ("p", 2, 1))
J_OUT = J_G + len(GATE_JOBS)
J_NORM2 = J_OUT + NT
JOBS = J_NORM2 + NT
STEPS = NH * NT
PIECES = 4
PIECE = UNIT // PIECES
PLAN = [(J_QK + k, k, n) for k in range(J_G - J_QK) for n in range(PIECES)]
for _i, (_kind, _n, _half) in enumerate(GATE_JOBS):
    if _kind == "g":
        _k = MIXER_UNITS.index(("in", C_G + 512 * (2 * _n + _half)))
        PLAN += [(J_G + _i, _k, n) for n in range(PIECES)]
    else:
        _k = MIXER_UNITS.index(("branch", _n))
        PLAN += [(J_G + _i, _k, 2 * _half + n) for n in range(2)]
PLAN += [(J_OUT, MIXER_UNITS.index(("out", k)), n) for k in range(2) for n in range(PIECES)]


def last_piece(job):
    return max(i for i, (j, _, _) in enumerate(PLAN) if j == job)


def unit_pieces(unit):
    return max(i for i, (_, k, _) in enumerate(PLAN) if k == unit) + 1


def pieces_used(i):
    return sum(n != last_piece(PLAN[n][0]) for n in range(min(i + 1, len(PLAN) - PIECES)))


def columns(widths):
    out, at = {}, 0
    for name, width in widths:
        out[name] = (at, at + width)
        at += width
    return out, at


CONST, NCONST = columns([
    ("ident", P), ("freq", ROPE), ("eps", 1), ("mean", 1), ("ones", P), ("before", P), ("gla_mask", P),
    ("band", NPAT * T), ("iota", T + CAP), ("caps", NPASS), ("key4", NG), ("key16", NE),
    ("one", 1), ("router_w", DC * NE), ("router_b", NE)])
NFIRST = CONST["eps"][1]
PAR, NPAR = columns([
    ("gain1", DC), ("gate_b", 2), ("out_gain", 1), ("conv_w", TAPS * WC), ("conv_b", WC), ("b_a", WC),
    ("b_x", WC), ("lam", WC), ("w_a", WC * P), ("w_x", WC * P), ("q_gain", P), ("k_gain", P),
    ("low", DC * RANK), ("gate_up", 2 * P)])


def build(nc, x, positions, const, par, gain2, w_in, w_branch, w_out, w_gate, w_up, w_down, out):
    with ExitStack() as ctx:
        def sb(name, shape, dt=F32):
            return ctx.enter_context(nc.sbuf_tensor(name, shape, dt))

        class Signal:

            def __init__(self, name, per, base=0):
                self.sem = ctx.enter_context(nc.semaphore(name))
                self.per = per
                self.base = base

            def at(self, l, k):
                return l * self.per + k + self.base

        def sem(name):
            return ctx.enter_context(nc.semaphore(name))

        ring = sb("ring", [P, MIX_RING, UNIT])
        with nc.sbuf_tensor("w_hi", [P, PIECES, PIECE], F32R) as w_hi, \
                nc.sbuf_tensor("w_lo", [P, PIECES, PIECE], F32R) as w_lo:
            pass
        ring_down = sb("ring_down", [P, len(DOWN), UNIT])
        with nc.sbuf_tensor("br_hi", [P, 2, BLK], F32R) as br_hi, nc.sbuf_tensor("br_lo", [P, 2, BLK], F32R) as br_lo:
            pass
        ring_up = sb("ring_up", [P, UNIT])
        arena = sb("arena", [P, 16 * BLK])
        hn = sb("hn", [P, NT * D])
        with nc.sbuf_tensor("hT_hi", [P, DC, T], F32R) as hT_hi, nc.sbuf_tensor("hT_lo", [P, DC, T], F32R) as hT_lo:
            pass
        ring_odd = sb("ring_odd", [P, UNIT])
        xs = sb("xs", [P, NT, D])
        cst = sb("cst", [P, NCONST])
        prm = sb("prm", [P, NPAR])
        g2 = sb("g2", [P, DC])
        cosb = sb("cosb", [P, NT, ROPE])
        sinb = sb("sinb", [P, NT, ROPE])
        small = sb("small", [P, 96])
        pairs_end = sb("pairs_end", [1, 1], I32)
        pos_i = sb("pos_i", [P, NT], I32)

        slotp = [ctx.enter_context(nc.psum_tensor(f"slot{i}", [P, 1024], F32)) for i in range(2)]
        M0 = ctx.enter_context(nc.psum_tensor("M0", [P, 1024], F32))
        M1 = ctx.enter_context(nc.psum_tensor("M1", [P, 1024], F32))

        def c(name):
            a, b = CONST[name]
            return cst[:, a:b]

        def q(name):
            a, b = PAR[name]
            return prm[:, a:b]

        def blk(i, n=1, off=0, width=None):
            a = i * BLK + off
            return arena[:, a:a + (width or n * BLK)]

        def h0(a, b):
            return hn[:, a:b]

        ident, ones = c("ident"), c("ones")
        eps, one = c("eps"), c("one")

        def slot_mem(slot):
            if slot in EARLY_ODD[:2]:
                return blk(8 + 4 * EARLY_ODD.index(slot), 4)
            if slot == EARLY_ODD[2]:
                return ring_odd[:, :]
            if slot == UP[1]:
                return ring_up[:, :]
            return ring_down[:, DOWN.index(slot), :] if slot in DOWN else ring[:, slot, :]

        hT = blk(0, 2).rearrange("p (c t) -> p c t", c=DC)
        diag = blk(2, width=NT * P)
        rope_tmp = blk(8, width=4 * P).rearrange("p (i r) -> p i r", i=4)
        qk_raw = [blk(u) for u in range(2 * NPAT)]
        xc, gate_r, tanh_y, gate_i = blk(3), blk(4), blk(5), blk(6)
        xpad = arena[:, 7 * BLK:7 * BLK + WC * (T + TAPS - 1)].rearrange("p (c t) -> p c t", c=WC)
        a_sq = arena[:, 7 * BLK:8 * BLK]
        k_dec = blk(8, off=512, width=512)
        kdT = k_dec
        br = [blk(9), blk(10), blk(11)]
        qk_ch, sq_att = blk(11), blk(11)
        va, og = blk(12), blk(13)
        gsc, gsq = blk(14), blk(15)
        la, cum = h0(0, 512), h0(512, 1024)
        q_dec, k_inv = h0(1024, 1536), h0(1536, 2048)
        state = h0(0, 768)
        v_att = [blk(6), blk(7), blk(8)]
        merged = blk(12, 2)
        sig = [blk(14), blk(15)]
        sc = h0(0, 768)
        prob = h0(1024, 1792)
        wa0 = PAR["w_a"][0]
        probT = prm[:, wa0:wa0 + 768]
        xgT = blk(0).rearrange("p (c s) -> p c s", c=DC)
        sel = blk(1, width=256)
        selw = blk(1, off=256, width=256)
        selT = blk(1, off=512, width=256)
        silu_g = blk(2, width=FF)
        hs = blk(2, off=FF, width=FF)
        hTs = blk(3, width=FC * P)
        ysb = blk(4)
        rank2 = blk(6, width=NE * NT).rearrange("p (e t) -> p e t", e=NE)
        gw2 = blk(6, off=64, width=NE * NT).rearrange("p (e t) -> p e t", e=NE)

        def rt(i, n=NT * NE):
            return blk(5, off=32 * i, width=n)

        ss, sd, rinv = small[:, 0:2], small[:, 2:4], small[:, 4:6]
        etot = small[:, 6:14]
        asum, arinv = small[:, 14:22], small[:, 30:38]
        grinv = small[:, 85:93]
        asd = (small[:, 22:30], small[:, 76:84])
        amax, anegm, aden, arden = (small[:, 38 + i:39 + i] for i in range(4))
        posf = small[:, 42:44]
        spz, sps, sp2, spp, sp_neg, sp_pos = (small[:, 44 + 4 * i:48 + 4 * i] for i in range(6))
        total_pairs = small[0:1, 68:69]
        npass = small[0:1, 69:70]
        cmp4 = small[0:1, 70:74]
        mxc = small[0:1, 74:75]

        loaded = [sem(f"loaded{s}") for s in range(RING)]
        consts_in, more_consts_in, x_in, x_out = sem("consts_in"), sem("more_consts_in"), sem("x_in"), sem("x_out")
        par_in, gain2_in = sem("par_in"), sem("gain2_in")
        setup_step, setup_act, rope_ready = sem("setup_step"), sem("setup_act"), sem("rope_ready")
        pairs_known = sem("pairs_known")
        job_done = Signal("job_done", JOBS)
        hi_ready, lo_ready = Signal("hi_ready", len(PLAN)), Signal("lo_ready", len(PLAN))
        piece_used = Signal("piece_used", pieces_used(len(PLAN) - 1))
        br_hi_ready, br_lo_ready = Signal("br_hi_ready", 3), Signal("br_lo_ready", 3)
        mg_hi_ready, mg_lo_ready = Signal("mg_hi_ready", 2), Signal("mg_lo_ready", 2)
        hT_hi_ready, hT_lo_ready = Signal("hT_hi_ready", NT), Signal("hT_lo_ready", NT)
        taken = [Signal(f"taken{i}", JOBS // 2, BASE) for i in range(2)]
        dve_step = Signal("dve_step", 108)
        rms_sq, rms_sd, diag_ready = (Signal(n, 2 * NT) for n in ("rms_sq", "rms_sd", "diag_ready"))
        low_ps, low_sb, z_ps = Signal("low_ps", 1), Signal("low_sb", 1), Signal("z_ps", 1)
        z_abs, decay_exp, decay_ln = Signal("z_abs", 1), Signal("decay_exp", 1), Signal("decay_ln", 1)
        cum_ready, exps_ready, gqk_ready = Signal("cum_ready", 1), Signal("exps_ready", 1), Signal("gqk_ready", 1)
        gsc_ps, gsc_sb = Signal("gsc_ps", 1), Signal("gsc_sb", 1)
        kdT_ps, kdT_sb = Signal("kdT_ps", 1), Signal("kdT_sb", 1)
        kv_ps, state_ready = Signal("kv_ps", 1), Signal("state_ready", 1)
        go_ps, go_sq, gmean_ps, grms = Signal("go_ps", 1), Signal("go_sq", 1), Signal("gmean_ps", 1), Signal("grms", 1)
        gdiag_ready, grinv_ps = Signal("gdiag_ready", 1), Signal("grinv_ps", 1)
        brA_ready = Signal("brA_ready", 1)
        lam_abs, lam_exp, lam_ready = Signal("lam_abs", 1), Signal("lam_exp", 1), Signal("lam_ready", 1)
        pad_ready, xc_ready = Signal("pad_ready", 1), Signal("xc_ready", 1)
        lru_ps, lru_sig, lru_at = Signal("lru_ps", 2), Signal("lru_sig", 2), Signal("lru_at", 1)
        lru_m, lru_sqrt, brB_ready = Signal("lru_m", 1), Signal("lru_sqrt", 1), Signal("brB_ready", 1)
        att_sq, att_sd, att_in = Signal("att_sq", 6), Signal("att_sd", 6), Signal("att_in", 6)
        attT_ps, attT_sb = Signal("attT_ps", 6), Signal("attT_sb", 6)
        sc_ps, sc_sb, sc_max, sc_exp, prob_ready = (Signal(n, STEPS) for n in
                                                    ("sc_ps", "sc_sb", "sc_max", "sc_exp", "prob_ready"))
        probT_ps, probT_sb, ao_ps, ao_sb = (Signal(n, STEPS) for n in ("probT_ps", "probT_sb", "ao_ps", "ao_sb"))
        merged_ready = Signal("merged_ready", 4)
        logit_ps, rt_max, rt_exp = Signal("logit_ps", 1), Signal("rt_max", 1), Signal("rt_exp", 1)
        member_ready, rank_ps = Signal("member_ready", 1), Signal("rank_ps", 1)
        sel_ready, sel_hot, xg_ps, xg_sb = sem("sel_ready"), sem("sel_hot"), sem("xg_ps"), sem("xg_sb")
        gate_ps, gu_ps, silu_ready, h_ready = sem("gate_ps"), sem("gu_ps"), sem("silu_ready"), sem("h_ready")
        hT_ps, hT_sb, selT_ps, selT_sb = sem("hT_ps"), sem("hT_sb"), sem("selT_ps"), sem("selT_sb")
        y_ps, y_sb, mix_ps = sem("y_ps"), sem("y_sb"), sem("mix_ps")
        x_add = [sem(f"x_add{t}") for t in range(NT)]
        slot_done = (gate_ps, gate_ps, gu_ps, gu_ps, y_ps, y_ps, gate_ps, gate_ps, gu_ps)

        block = ctx.enter_context(nc.Block())

        settled = sem("settled")

        def settle(eng):
            eng.sem_inc(settled, 1)

        def arrivals(slot, l, start, k):
            return 16 * (l * MIX_USES[slot] + k) + start * (8 if slot in EARLY else 16)

        def expert_arrivals(slot, l, it):
            if slot in EARLY:
                return 16 * (l + 1) * MIX_USES[slot] + 8 * it + 16
            if slot in EARLY_ODD:
                return 8 * it + 8
            return 16 * (l + 1) * MIX_USES[slot] + 16 * (it + 1)

        def in_layout(i, flat):
            kind, at = MIXER_UNITS[PLAN[i][1]]
            if kind == "branch":
                return flat.rearrange("p (c n) -> p c n", c=WC)
            return flat if kind == "out" or at in TIME_MAJOR else flat.rearrange("p (c n) -> p c n", c=DC)

        def source(i):
            _, k, n = PLAN[i]
            view = in_layout(i, ring[:, k % MIX_RING, :])
            if len(view.shape) == 2:
                return view[:, n * PIECE:(n + 1) * PIECE]
            width = view.shape[2] // PIECES
            return view[:, :, n * width:(n + 1) * width]

        def piece_of(parts, i):
            return in_layout(i, parts[:, i % PIECES, :])

        @block.sync
        def _(sp):
            sp.dma_start(pos_i[:, :], positions.rearrange("b (t p) -> p (b t)", p=P),
                         allow_slow_non_contiguous=True).then_inc(consts_in, 16)
            sp.dma_start(cst[:, 0:NFIRST], const[:, 0:NFIRST]).then_inc(consts_in, 16)
            sp.dma_start(xs[:, :, :], x.rearrange("b (t p) d -> p (b t) d", p=P)).then_inc(x_in, 16)
            sp.dma_start(cst[:, NFIRST:], const[:, NFIRST:]).then_inc(more_consts_in, 16)
            sp.dma_start(prm[:, :], par[0]).then_inc(par_in, 16)

            with sp.Fori(0, DEPTH) as l:
                sp.wait_ge(pairs_known, l + 1)
                settle(sp)
                start = sp.value_load(pairs_end[0:1, 0:1], min_val=0, max_val=DEPTH * NPASS * PAIRS)

                def unit_used(k):
                    sp.wait_ge(lo_ready.sem, lo_ready.at(l, unit_pieces(k)))

                def mixer_unit(k):
                    slot = k % MIX_RING
                    kind, at = MIXER_UNITS[k]
                    if k < MIX_RING:
                        sp.wait_ge(slot_done[slot], start + BASE)
                    else:
                        unit_used(k - MIX_RING)
                    settle(sp)
                    dst = ring[:, slot, :]
                    if kind == "in":
                        src = w_in[bass.ds(l, 1), :, at:at + 512].rearrange("o (c p) n -> p (o c) n", p=P)
                        dst = dst.rearrange("p (c n) -> p c n", c=DC)
                    elif kind == "branch":
                        src = w_branch[bass.ds(l, 1), at].rearrange("o (c p) n -> p (o c) n", p=P)
                        dst = dst.rearrange("p (c n) -> p c n", c=WC)
                    else:
                        src = w_out[bass.ds(l, 1), at * 512:(at + 1) * 512].rearrange("o (c p) n -> p (o c) n", p=P)
                        dst = dst.rearrange("p (c n) -> p c n", c=WC)
                    sp.dma_start(dst, src).then_inc(loaded[slot], 16)

                for k in range(len(MIXER_UNITS)):
                    mixer_unit(k)
                    if k == MIX_RING - 1:
                        sp.wait_ge(x_add[NT - 1], start + BASE)
                        settle(sp)
                        sp.dma_start(g2[:, :], gain2[bass.ds(l, 1)].rearrange("o p n -> p (o n)"))\
                            .then_inc(gain2_in, 16)

                def expert_weights(slot, it):
                    w = (w_gate, w_up, w_down, w_gate, w_up)[slot // 2]
                    e = 2 * (it % PAIRS) + slot % 2
                    rows = FC if slot in DOWN else DC
                    src = w[bass.ds(l, 1), bass.ds(e, 1)].rearrange("o e (c p) n -> p (o e c) n", p=P)
                    sp.dma_start(slot_mem(slot).rearrange("p (c n) -> p c n", c=rows), src)\
                        .then_inc(loaded[slot], 16)

                units = range(len(MIXER_UNITS) - MIX_RING, len(MIXER_UNITS))
                for k in units[:1]:
                    unit_used(k)
                    settle(sp)
                    expert_weights(k % MIX_RING, start)
                sp.wait_ge(job_done.sem, job_done.at(l, J_OUT))
                settle(sp)
                expert_weights(UP[1], start)
                for k in units[1:]:
                    unit_used(k)
                    settle(sp)
                    expert_weights(k % MIX_RING, start)
                sp.wait_ge(job_done.sem, job_done.at(l, J_OUT + NT))
                settle(sp)
                for slot in DOWN:
                    expert_weights(slot, start)
                for slot in EARLY_ODD:
                    expert_weights(slot, start + 1)

                def refill(slots, it):
                    for slot in slots:
                        sp.wait_ge(slot_done[slot], it + BASE)
                        settle(sp)
                        expert_weights(slot, it)

                def refill_early(slots, it):
                    for slot in slots:
                        sp.wait_ge(slot_done[slot], it - 1 + BASE)
                        settle(sp)
                        expert_weights(slot, it)

                def pair(it, early_next):
                    refill(LATE[:1], it)
                    refill_early(early_next[:1], it + 1)
                    refill(LATE[1:], it)
                    refill_early(early_next[1:], it + 1)

                refill_early(EARLY, start + 2)
                refill(LATE, start + 1)
                with sp.Fori(start + 2, start + PAIRS - 2, 2) as it:
                    pair(it, EARLY_ODD)
                    pair(it + 1, EARLY)
                pair(start + PAIRS - 2, EARLY_ODD)
                refill(LATE, start + PAIRS - 1)
                sp.wait_ge(job_done.sem, job_done.at(l, JOBS))
                settle(sp)
                nxt = (l + 1) % DEPTH
                sp.wait_ge(pairs_known, l + 2)
                sp.dma_start(prm[:, :], par[bass.ds(nxt, 1)].rearrange("o p n -> p (o n)")).then_inc(par_in, 16)
                settle(sp)
                end = sp.value_load(pairs_end[0:1, 0:1], min_val=0, max_val=DEPTH * NPASS * PAIRS)
                with sp.If(end > start + PAIRS):
                    with sp.Fori(start + PAIRS, end, 2) as it:
                        refill_early(EARLY, it)
                        refill(LATE, it)
                        refill_early(EARLY_ODD, it + 1)
                        refill(LATE, it + 1)

            total = sp.value_load(pairs_end[0:1, 0:1], min_val=0, max_val=DEPTH * NPASS * PAIRS)
            for t in range(NT):
                sp.wait_ge(x_add[t], total + BASE)
                settle(sp)
                sp.dma_start(out.rearrange("b (t p) d -> p (b t) d", p=P)[:, t, :], xs[:, t, :]).then_inc(x_out, 16)
            sp.wait_ge(x_out, 16 * NT)
            sp.wait_ge(par_in, 16 * (DEPTH + 1))
            sp.wait_ge(gain2_in, 16 * DEPTH)

        @block.tensor
        def _(pe):
            mm = nc.tensor.matmul
            for s in (taken[0].sem, taken[1].sem, *x_add, gate_ps, gu_ps, y_ps, selT_ps, xg_ps, xg_sb, mix_ps):
                pe.sem_inc(s, BASE)
            pe.wait_ge(consts_in, 32)
            pe.wait_ge(more_consts_in, 16)

            with pe.Fori(0, DEPTH) as l:
                pe.wait_ge(pairs_known, l + 1)
                settle(pe)
                start = pe.value_load(pairs_end[0:1, 0:1], min_val=0, max_val=DEPTH * NPASS * PAIRS)
                for t in range(NT):
                    pe.wait_ge(x_add[t], start + BASE)
                pe.wait_ge(par_in, 16 * l + 16)

                def taken_wait(j):
                    pe.wait_ge(taken[j % 2].sem, taken[j % 2].at(l, j // 2 + 1))

                def open_slot(j):
                    pe.wait_ge(taken[j % 2].sem, taken[j % 2].at(l, j // 2))
                    return slotp[j % 2]

                def transposes(j, n):
                    o = open_slot(j)
                    t = j - (J_NORM1, J_NORM2)[n]
                    pe.wait_ge(diag_ready.sem, diag_ready.at(l, NT * n + t + 1))
                    for cc in range(DC):
                        last = mm(o[:, cc * P:(cc + 1) * P], xs[:, t, cc * P:(cc + 1) * P],
                                  diag[:, t * P:(t + 1) * P], start=True, stop=True)
                    last.then_inc(job_done.sem, 1)

                def parts_of(i, h_hi, h_lo):
                    pe.wait_ge(lo_ready.sem, lo_ready.at(l, i + 1))
                    hi, lo = piece_of(w_hi, i), piece_of(w_lo, i)
                    return (hi, h_hi), (hi, h_lo), (lo, h_hi)

                def piece_done(i, last):
                    ends = i == last_piece(PLAN[i][0])
                    last.then_inc(job_done.sem if ends else piece_used.sem, 1)

                def channel_major(j, h_hi, h_lo, middle=None):
                    pieces = [i for i in range(len(PLAN)) if PLAN[i][0] == j]
                    tiles = WC // len(pieces)
                    rows = h_hi.shape[1]
                    o = open_slot(j)
                    for n, i in enumerate(pieces):
                        parts = parts_of(i, h_hi, h_lo)
                        for m in range(tiles):
                            for cc in range(rows):
                                for k, (w, h) in enumerate(parts):
                                    last = mm(o[:, (n * tiles + m) * T:(n * tiles + m + 1) * T],
                                              w[:, cc, m * P:(m + 1) * P], h[:, cc, :],
                                              start=cc == k == 0, stop=cc == rows - 1 and k == 2)
                        piece_done(i, last)
                        if (n + 1) * tiles == 2 and middle:
                            middle()

                def time_major(j):
                    pieces = [i for i in range(len(PLAN)) if PLAN[i][0] == j]
                    o = open_slot(j)
                    for n, i in enumerate(pieces):
                        parts = parts_of(i, hT_hi, hT_lo)
                        for t in range(NT):
                            for cc in range(2):
                                for k, (w, h) in enumerate(parts):
                                    last = mm(o[:, t * 512:(t + 1) * 512], h[:, 2 * n + cc, t * P:(t + 1) * P],
                                              w[:, cc * 512:(cc + 1) * 512], start=n == cc == k == 0,
                                              stop=n == PIECES - 1 and cc == 1 and k == 2)
                        piece_done(i, last)

                for j in (0, 1):
                    transposes(j, 0)
                taken_wait(0)
                taken_wait(1)

                low = q("low").rearrange("p (c r) -> p c r", c=DC)
                for cc in range(DC):
                    last = mm(M0[0:RANK, 512:512 + T], low[:, cc, :], hT[:, cc, :], start=cc == 0, stop=cc == DC - 1)
                last.then_inc(low_ps.sem, 1)
                pe.wait_ge(hT_lo_ready.sem, hT_lo_ready.at(l, NT))
                channel_major(J_QK, hT_hi, hT_lo)
                pe.wait_ge(low_sb.sem, low_sb.at(l, 1))
                a = PAR["gate_up"][0]
                for g in range(2):
                    last = mm(M0[:, g * T:(g + 1) * T], prm[0:RANK, a + g * P:a + (g + 1) * P],
                              h0(0, T)[0:RANK, :], start=True, stop=True)
                last.then_inc(z_ps.sem, 1)
                time_major(J_VA)
                for j in (J_XB, J_YB):
                    channel_major(j, hT_hi, hT_lo)
                xcv = xc.rearrange("p (c t) -> p c t", c=WC)

                def lru_gates(name, dst):
                    wv = q(name).rearrange("p (c n) -> p c n", c=WC)
                    for cc in range(WC):
                        last = mm(dst[:, cc * T:(cc + 1) * T], wv[:, cc, :], xcv[:, cc, :], start=True, stop=True)
                    last.then_inc(lru_ps.sem, 1)

                channel_major(J_OG, hT_hi, hT_lo)
                pe.wait_ge(xc_ready.sem, xc_ready.at(l, 1))
                lru_gates("w_a", M1)
                pe.wait_ge(z_abs.sem, z_abs.at(l, 1))
                lru_gates("w_x", M0)

                time_major(J_Q)
                pe.wait_ge(gqk_ready.sem, gqk_ready.at(l, 1))
                pe.wait_ge(lru_sig.sem, lru_sig.at(l, 1))
                for hh in range(2):
                    for g in range(2):
                        for t in range(NT):
                            cols = slice(g * T + t * P, g * T + (t + 1) * P)
                            last = mm(M1[:, (hh * 4 + g * 2 + t) * P:(hh * 4 + g * 2 + t + 1) * P],
                                      k_inv[hh * DK:(hh + 1) * DK, cols], q_dec[hh * DK:(hh + 1) * DK, cols],
                                      start=True, stop=True)
                last.then_inc(gsc_ps.sem, 1)
                pe.wait_ge(lru_sig.sem, lru_sig.at(l, 2))
                for i in range(4):
                    last = nc.tensor.transpose(M0[:, i * P:(i + 1) * P], k_dec[:, i * P:(i + 1) * P], ident)
                last.then_inc(kdT_ps.sem, 1)

                time_major(J_Q + 1)
                pe.wait_ge(kdT_sb.sem, kdT_sb.at(l, 1))
                settle(pe)
                for n in (0, 2, 1):
                    b = (n % 2) * CH
                    for g in range(2):
                        col = (512 if n % 2 == 0 else 0) + (n // 2 * 2 + g) * P
                        for hh in range(2):
                            kd = kdT[b:b + CH, (g * 2 + n // 2) * P + hh * DK:(g * 2 + n // 2) * P + (hh + 1) * DK]
                            vv = va[b:b + CH, (n // 2) * 512 + (2 * g + hh) * DV:(n // 2) * 512 + (2 * g + hh + 1) * DV]
                            last = mm(M0[hh * DK:(hh + 1) * DK, col:col + DV], kd, vv, start=True, stop=True)
                last.then_inc(kv_ps.sem, 1)

                time_major(J_Q + 2)
                pe.wait_ge(gsc_sb.sem, gsc_sb.at(l, 1))
                pe.wait_ge(state_ready.sem, state_ready.at(l, 1))
                for hh in range(2):
                    for g in range(2):
                        for t in range(NT):
                            o = M1[:, (hh * 4 + g * 2 + t) * P:(hh * 4 + g * 2 + t + 1) * P]
                            hd = 2 * g + hh
                            last = mm(o, va[:, t * 512 + hd * DV:t * 512 + (hd + 1) * DV],
                                      gsc[:, (hh * 4 + g * 2 + t) * P:(hh * 4 + g * 2 + t + 1) * P],
                                      start=True, stop=False, skip_group_check=True)
                            for n in range(2 * t, 2 * t + 2):
                                if n:
                                    last = mm(M1[:, (hh * 4 + g * 2) * P + n * CH:(hh * 4 + g * 2) * P + (n + 1) * CH],
                                              state[hh * DK:(hh + 1) * DK, (g * 3 + n - 1) * DV:(g * 3 + n) * DV],
                                              q_dec[hh * DK:(hh + 1) * DK, g * T + n * CH:g * T + (n + 1) * CH],
                                              start=False, stop=n == 2 * t + 1, skip_group_check=True)
                last.then_inc(go_ps.sem, 1)

                time_major(J_K)
                pe.wait_ge(go_sq.sem, go_sq.at(l, 1))
                for b in range(NT * HG):
                    last = mm(M0[:, b:b + 1], gsq[:, b * P:(b + 1) * P], c("mean"), start=True, stop=True)
                last.then_inc(gmean_ps.sem, 1)

                def att_transposes(u):
                    dst = (M0, M1)[u % 2]
                    if u == 0:
                        pe.wait_ge(brA_ready.sem, brA_ready.at(l, 1))
                    if u >= 2:
                        pe.wait_ge(attT_sb.sem, attT_sb.at(l, u - 1))
                    pe.wait_ge(att_in.sem, att_in.at(l, u + 1))
                    for h in range(NH):
                        for t in range(NT):
                            last = nc.tensor.transpose(dst[:, h * T + t * P:h * T + (t + 1) * P],
                                                       qk_raw[u][:, t * 512 + h * P:t * 512 + (h + 1) * P], ident)
                    last.then_inc(attT_ps.sem, 1)

                time_major(J_K + 1)
                pe.wait_ge(gdiag_ready.sem, gdiag_ready.at(l, 1))
                for i in range(2):
                    last = mm(M0[:, i * 512:(i + 1) * 512], ones, gsq[:, i * 512:(i + 1) * 512],
                              start=True, stop=True)
                last.then_inc(grinv_ps.sem, 1)
                for u, j in enumerate(range(J_K + 2, J_G)):
                    time_major(j)
                    if u == 0:
                        att_transposes(0)
                    att_transposes(u + 1)
                att_transposes(5)

                def att_scores(s):
                    h, t = s // NT, s % NT
                    wide = (t + 1) * P
                    if s == 0:
                        pe.wait_ge(attT_sb.sem, attT_sb.at(l, 6))
                    if s >= 1:
                        pe.wait_ge(sc_sb.sem, sc_sb.at(l, s))
                    if s >= 2:
                        pe.wait_ge(ao_sb.sem, ao_sb.at(l, s - 1))
                    for p in range(NPAT):
                        last = mm(M0[:, p * wide:(p + 1) * wide],
                                  qk_raw[p][:, h * T + t * P:h * T + (t + 1) * P],
                                  qk_raw[NPAT + p][:, h * T:h * T + wide], start=True, stop=True)
                    last.then_inc(sc_ps.sem, 1)

                def att_prob_transposes(s):
                    t = s % NT
                    pe.wait_ge(prob_ready.sem, prob_ready.at(l, s + 1))
                    if s >= 1:
                        pe.wait_ge(probT_sb.sem, probT_sb.at(l, s))
                    for i in range(NPAT * (t + 1)):
                        last = nc.tensor.transpose(M1[:, i * P:(i + 1) * P], prob[:, i * P:(i + 1) * P], ident)
                    last.then_inc(probT_ps.sem, 1)

                def att_out(s):
                    h, t = s // NT, s % NT
                    pe.wait_ge(probT_sb.sem, probT_sb.at(l, s + 1))
                    pe.wait_ge(sc_sb.sem, sc_sb.at(l, min(s + 2, STEPS)))
                    n = NPAT * (t + 1)
                    for i in range(n):
                        p, kt = i // (t + 1), i % (t + 1)
                        last = mm(M0[:, 896:1024], v_att[p][:, kt * 512 + h * P:kt * 512 + (h + 1) * P],
                                  probT[:, i * P:(i + 1) * P], start=i == 0, stop=i == n - 1, skip_group_check=True)
                    last.then_inc(ao_ps.sem, 1)

                for i, (kind, n, half) in enumerate(GATE_JOBS):
                    j = J_G + i
                    middle = (lambda s=i - 2: att_out(s)) if 0 <= i - 2 < STEPS else None
                    if kind == "g":
                        channel_major(j, hT_hi, hT_lo, middle=middle)
                    else:
                        if half == 0:
                            pe.wait_ge(br_lo_ready.sem, br_lo_ready.at(l, n + 1))
                        channel_major(j, *(b[:, n % 2, :].rearrange("p (c t) -> p c t", c=WC) for b in (br_hi, br_lo)),
                                      middle=middle)
                    if 0 <= i - 1 < STEPS:
                        att_prob_transposes(i - 1)
                    if i < STEPS:
                        att_scores(i)

                def out_product(t, cc, parts):
                    for half in range(2):
                        for k, (w, h) in enumerate(parts):
                            last = mm(slotp[t][:, half * 512:(half + 1) * 512], h[:, cc, t * P:(t + 1) * P],
                                      w[:, half * 512:(half + 1) * 512], start=cc == k == 0,
                                      stop=cc == DC - 1 and k == 2)
                    return last

                piece0 = len(PLAN) - DC
                pe.wait_ge(mg_lo_ready.sem, mg_lo_ready.at(l, 1))
                for cc in range(WC):
                    parts = parts_of(piece0 + cc, hT_hi, hT_lo)
                    for t in range(NT):
                        if cc == 0:
                            open_slot(J_OUT + t)
                        last = out_product(t, cc, parts)
                    last.then_inc(piece_used.sem, 1)
                pe.wait_ge(mg_lo_ready.sem, mg_lo_ready.at(l, 2))
                for t in range(NT):
                    for cc in range(WC, DC):
                        last = out_product(t, cc, parts_of(piece0 + cc, hT_hi, hT_lo))
                    last.then_inc(job_done.sem, 1)

                for t in range(NT):
                    transposes(J_NORM2 + t, 1)
                rw = c("router_w").rearrange("p (c e) -> p c e", c=DC)
                for t in range(NT):
                    taken_wait(J_NORM2 + t)
                    for cc in range(DC):
                        last = mm(M0[:, t * NE:(t + 1) * NE], hT[:, cc, t * P:(t + 1) * P], rw[:, cc, :],
                                  start=cc == 0, stop=cc == DC - 1)
                last.then_inc(logit_ps.sem, 1)
                pe.wait_ge(member_ready.sem, member_ready.at(l, 1))
                member = rt(0)
                mm(M1[:, 0:NE], c("before"), member[:, 0:NE], start=True, stop=True)
                mm(M1[:, NE:2 * NE], c("before"), member[:, NE:2 * NE], start=True, stop=False, skip_group_check=True)
                mm(M1[:, NE:2 * NE], ones, member[:, 0:NE], start=False, stop=True, skip_group_check=True)
                mm(M1[:, 512:512 + NE], ones, member[:, 0:NE], start=True, stop=False, skip_group_check=True)
                mm(M1[:, 512:512 + NE], ones, member[:, NE:2 * NE], start=False, stop=True,
                   skip_group_check=True).then_inc(rank_ps.sem, 1)

                G0, G1 = slotp

                def gather(n, chunks=range(DC)):
                    if chunks[0] == 0:
                        pe.wait_ge(sel_hot, n + 1)
                        pe.wait_ge(xg_sb, n + BASE)
                    for cc in chunks:
                        for t in range(NT):
                            last = mm(G0[:, cc * P:(cc + 1) * P], hn[:, t * D + cc * P:t * D + (cc + 1) * P],
                                      sel[:, t * P:(t + 1) * P], start=t == 0, stop=t == NT - 1)
                    if chunks[-1] == DC - 1:
                        last.then_inc(xg_ps, 1)

                def expert_loaded(slot, it):
                    pe.wait_ge(loaded[slot], expert_arrivals(slot, l, it))

                gather(start + l)
                pe.wait_ge(pairs_known, l + 2)
                settle(pe)
                end = pe.value_load(pairs_end[0:1, 0:1], min_val=0, max_val=DEPTH * NPASS * PAIRS)
                def pair(it, odd):
                    pe.wait_ge(sel_ready, it + l + 1)
                    for t in range(NT):
                        last = nc.tensor.transpose(G1[:, t * P:(t + 1) * P], selw[:, t * P:(t + 1) * P], ident)
                    last.then_inc(selT_ps, 1)
                    pe.wait_ge(xg_sb, it + l + 1 + BASE)
                    pe.wait_ge(x_add[0], it + BASE)
                    for stage, slots in enumerate(EXPERT_SLOTS[odd]):
                        for cc in range(DC):
                            for i in range(2):
                                if cc == 0:
                                    expert_loaded(slots[i], it)
                                wv = slot_mem(slots[i]).rearrange("p (c n) -> p c n", c=DC)
                                last = mm(M0[i * CAP:(i + 1) * CAP, stage * FF:(stage + 1) * FF],
                                          xgT[:, cc, i * CAP:(i + 1) * CAP], wv[:, cc, :],
                                          start=cc == 0, stop=cc == DC - 1)
                        last.then_inc((gate_ps, gu_ps)[stage], 1)
                    gather(it + l + 1, range(0, 4))
                    pe.wait_ge(h_ready, it + 1)
                    pe.wait_ge(x_add[1], it + BASE)
                    for f in range(FC):
                        last = nc.tensor.transpose(M1[:, FF + f * P:FF + (f + 1) * P], hs[:, f * P:(f + 1) * P], ident)
                    last.then_inc(hT_ps, 1)
                    gather(it + l + 1, range(4, 6))
                    pe.wait_ge(hT_sb, it + 1)
                    pe.wait_ge(selT_sb, it + 1)
                    for half in range(2):
                        for f in range(FC):
                            for i in range(2):
                                if half == 0 and f == 0:
                                    expert_loaded(DOWN[i], it)
                                wv = slot_mem(DOWN[i]).rearrange("p (c n) -> p c n", c=FC)
                                last = mm(G1[i * CAP:(i + 1) * CAP, half * 512:(half + 1) * 512],
                                          hTs[:, f * P + i * CAP:f * P + (i + 1) * CAP],
                                          wv[:, f, half * 512:(half + 1) * 512], start=f == 0, stop=f == FC - 1)
                    last.then_inc(y_ps, 1)
                    gather(it + l + 1, range(6, DC))
                    pe.wait_ge(y_sb, 2 * it + 2)
                    for t in range(NT):
                        o = (M0, M1)[t]
                        for half in range(2):
                            last = mm(o[:, half * 512:(half + 1) * 512], selT[:, t * P:(t + 1) * P],
                                      ysb[:, half * 512:(half + 1) * 512], start=True, stop=True)
                        last.then_inc(mix_ps, 1)

                with pe.Fori(start, end, 2) as it:
                    pair(it, False)
                    pair(it + 1, True)

        @block.scalar
        def _(act):
            A = nc.scalar.activation
            act.wait_ge(setup_act, 1)
            A(sinb[:, :, :], sinb[:, :, :], ACT.Sin).then_inc(rope_ready, 1)
            A(cosb[:, :, :], cosb[:, :, :], ACT.Sin).then_inc(rope_ready, 1)
            with act.Fori(0, DEPTH) as l:
                act.wait_ge(pairs_known, l + 1)
                settle(act)
                start = act.value_load(pairs_end[0:1, 0:1], min_val=0, max_val=DEPTH * NPASS * PAIRS)

                high_parts = [0]

                def split_ahead(j, n):
                    for i in range(high_parts[0], min(last_piece(j) + n + 1, len(PLAN))):
                        _, k, _ = PLAN[i]
                        slot = k % MIX_RING
                        if all(PLAN[b][1] != k for b in range(i)):
                            act.wait_ge(loaded[slot], arrivals(slot, l, start, k // MIX_RING + 1))
                        if i >= PIECES:
                            before = i - PIECES
                            if before == last_piece(PLAN[before][0]):
                                act.wait_ge(job_done.sem, job_done.at(l, PLAN[before][0] + 1))
                            else:
                                act.wait_ge(piece_used.sem, piece_used.at(l, pieces_used(before)))
                        A(piece_of(w_hi, i), source(i), ACT.Copy).then_inc(hi_ready.sem, 1)
                        high_parts[0] = i + 1

                def done(j):
                    split_ahead(j, PIECES - 1)
                    act.wait_ge(job_done.sem, job_done.at(l, j + 1))
                    return slotp[j % 2]

                def warm_sqrt():
                    A(small[:, 84:85], eps, ACT.Sqrt)

                def norm_stats(n, t):
                    A(blk(3 + t), xs[:, t, :], ACT.Square, accum_out=ss[:, t:t + 1]).then_inc(rms_sq.sem, 1)
                    act.wait_ge(rms_sq.sem, rms_sq.at(l, NT * n + t + 1))
                    A(sd[:, t:t + 1], ss[:, t:t + 1], ACT.Sqrt, bias=eps, scale=1.0 / D).then_inc(rms_sd.sem, 1)

                warm_sqrt()
                for t in range(NT):
                    act.wait_ge(x_in, 16)
                    act.wait_ge(x_add[t], start + BASE)
                    norm_stats(0, t)
                act.wait_ge(par_in, 16 * l + 16)
                act.wait_ge(lam_abs.sem, lam_abs.at(l, 1))
                A(spz, spz, ACT.Exp, scale=-1.0).then_inc(lam_exp.sem, 1)
                split_ahead(J_QK, 1 - PIECES)
                for t in range(NT):
                    act.wait_ge(taken[t].sem, taken[t].at(l, 1))
                    A(hT_hi[:, :, t * P:(t + 1) * P], hT[:, :, t * P:(t + 1) * P], ACT.Copy).then_inc(hT_hi_ready.sem, 1)
                split_ahead(J_QK, 0)

                act.wait_ge(low_ps.sem, low_ps.at(l, 1))
                A(h0(0, T)[0:RANK, :], M0[0:RANK, 512:512 + T], ACT.Copy).then_inc(low_sb.sem, 1)
                o = done(J_QK)
                A(qk_ch[:, 0:512], o[:, 0:512], ACT.Copy, scale=DK ** -0.5)
                A(qk_ch[:, 512:1024], o[:, 512:1024], ACT.Copy).then_inc(taken[0].sem, 1)
                split_ahead(J_QK, PIECES)
                act.wait_ge(z_abs.sem, z_abs.at(l, 1))
                A(cum, cum, ACT.Exp, scale=-1.0).then_inc(decay_exp.sem, 1)
                act.wait_ge(decay_exp.sem, decay_exp.at(l, 1))
                A(cum, cum, ACT.Ln, bias=one).then_inc(decay_ln.sem, 1)
                o = done(J_VA)
                A(va, o[:, :], ACT.Copy).then_inc(taken[1].sem, 1)
                split_ahead(J_VA, PIECES)
                act.wait_ge(cum_ready.sem, cum_ready.at(l, 1))
                A(q_dec, cum, ACT.Exp, scale=1.0 / 16)
                A(k_inv, cum, ACT.Exp, scale=-1.0 / 16)
                A(etot, cum.rearrange("p (n t) -> p n t", t=CH)[:, :, CH - 1], ACT.Exp, scale=1.0 / 16)
                A(k_dec, la, ACT.Exp, scale=-1.0 / 16).then_inc(exps_ready.sem, 1)
                o = done(J_XB)
                act.wait_ge(pad_ready.sem, pad_ready.at(l, 1))
                A(xpad[:, :, TAPS - 1:], o[:, :].rearrange("p (c t) -> p c t", c=WC), ACT.Copy)\
                    .then_inc(taken[0].sem, 1)
                split_ahead(J_XB, PIECES)
                o = done(J_YB)
                A(br[1], o[:, :], ACT.Gelu_apprx_tanh).then_inc(taken[1].sem, 1)
                split_ahead(J_YB, PIECES)
                o = done(J_OG)
                A(og, o[:, :], ACT.Silu).then_inc(taken[0].sem, 1)
                split_ahead(J_OG, PIECES)
                act.wait_ge(lru_ps.sem, lru_ps.at(l, 1))
                for cc in range(WC):
                    w = A(gate_r[:, cc * T:(cc + 1) * T], M1[:, cc * T:(cc + 1) * T], ACT.Sigmoid,
                          bias=q("b_a")[:, cc:cc + 1])
                w.then_inc(lru_sig.sem, 1)
                act.wait_ge(lru_ps.sem, lru_ps.at(l, 2))
                for cc in range(WC):
                    w = A(gate_i[:, cc * T:(cc + 1) * T], M0[:, cc * T:(cc + 1) * T], ACT.Sigmoid,
                          bias=q("b_x")[:, cc:cc + 1])
                w.then_inc(lru_sig.sem, 1)
                act.wait_ge(lru_sig.sem, lru_sig.at(l, 2))
                act.wait_ge(lam_ready.sem, lam_ready.at(l, 1))
                for cc in range(WC):
                    A(tanh_y[:, cc * T:(cc + 1) * T], gate_r[:, cc * T:(cc + 1) * T], ACT.Tanh,
                      scale=sp_pos[:, cc:cc + 1])
                for cc in range(WC):
                    w = A(gate_r[:, cc * T:(cc + 1) * T], gate_r[:, cc * T:(cc + 1) * T], ACT.Exp,
                          scale=sp_neg[:, cc:cc + 1])
                w.then_inc(lru_at.sem, 1)
                split_ahead(J_Q, 2)
                act.wait_ge(lru_m.sem, lru_m.at(l, 1))
                A(tanh_y, tanh_y, ACT.Sqrt).then_inc(lru_sqrt.sem, 1)

                def take_qk(u):
                    j = J_Q + u
                    o = done(j)
                    if u == 3:
                        act.wait_ge(brB_ready.sem, brB_ready.at(l, 1))
                    A(qk_raw[u], o[:, :], ACT.Copy).then_inc(taken[j % 2].sem, 1)
                    split_ahead(j, PIECES)

                def qk_stats(u):
                    j = J_Q + u
                    if u == 0:
                        act.wait_ge(gqk_ready.sem, gqk_ready.at(l, 1))
                    if u >= 2:
                        act.wait_ge(att_in.sem, att_in.at(l, u - 1))
                    act.wait_ge(taken[j % 2].sem, taken[j % 2].at(l, j // 2 + 1))
                    for g in range(NT * NH):
                        s = slice(g * DH, (g + 1) * DH)
                        w = A(sq_att[:, s], qk_raw[u][:, s], ACT.Square, accum_out=asum[:, g:g + 1])
                    w.then_inc(att_sq.sem, 1)
                    act.wait_ge(att_sq.sem, att_sq.at(l, u + 1))
                    A(asd[u % 2], asum, ACT.Sqrt, bias=eps, scale=1.0 / DH).then_inc(att_sd.sem, 1)

                take_qk(0)
                qk_stats(0)
                act.wait_ge(kdT_ps.sem, kdT_ps.at(l, 1))
                A(kdT, M0[:, 0:512], ACT.Copy).then_inc(kdT_sb.sem, 1)
                take_qk(1)
                qk_stats(1)
                take_qk(2)
                qk_stats(2)
                act.wait_ge(go_ps.sem, go_ps.at(l, 1))
                A(gsq, M1[:, :], ACT.Square).then_inc(go_sq.sem, 1)
                take_qk(3)
                act.wait_ge(gmean_ps.sem, gmean_ps.at(l, 1))
                A(grinv, M0[:, 0:NT * HG], ACT.Sqrt, bias=eps).then_inc(grms.sem, 1)
                qk_stats(3)
                def branch_high(n):
                    if n == 0:
                        act.wait_ge(brA_ready.sem, brA_ready.at(l, 1))
                    if n == 2:
                        act.wait_ge(job_done.sem, job_done.at(l, J_G + GATE_JOBS.index(("p", 0, 1)) + 1))
                    A(br_hi[:, n % 2, :], br[n], ACT.Copy).then_inc(br_hi_ready.sem, 1)

                for u in range(6):
                    j = J_K + 1 + u
                    if u < 2:
                        take_qk(4 + u)
                        qk_stats(4 + u)
                    elif j < J_G:
                        o = done(j)
                        if u == 4:
                            act.wait_ge(att_in.sem, att_in.at(l, 6))
                        A(v_att[u - 2], o[:, :], ACT.Copy).then_inc(taken[j % 2].sem, 1)
                        split_ahead(j, PIECES)
                    for n in ((), (0, 1), (2,), (3,), (4,), (5,))[u]:
                        act.wait_ge(attT_ps.sem, attT_ps.at(l, n + 1))
                        A(qk_raw[n], (M0, M1)[n % 2][:, :], ACT.Copy).then_inc(attT_sb.sem, 1)
                    if u in (2, 3):
                        branch_high(u - 2)

                def merged_high(half):
                    act.wait_ge(merged_ready.sem, merged_ready.at(l, 3 + half))
                    A(hT_hi[:, half * WC:(half + 1) * WC, :],
                      merged[:, half * BLK:(half + 1) * BLK].rearrange("p (c t) -> p c t", c=WC), ACT.Copy)\
                        .then_inc(mg_hi_ready.sem, 1)

                for i in range(len(GATE_JOBS)):
                    kind, n, half = GATE_JOBS[i]
                    j = J_G + i
                    s = i - 2
                    if 0 <= s < STEPS:
                        h, t = s // NT, s % NT
                        act.wait_ge(ao_ps.sem, ao_ps.at(l, s + 1))
                        A(br[2][:, h * T + t * P:h * T + (t + 1) * P], M0[:, 896:1024], ACT.Copy)\
                            .then_inc(ao_sb.sem, 1)
                    if s == STEPS - 1:
                        act.wait_ge(ao_sb.sem, ao_sb.at(l, STEPS))
                        branch_high(2)
                    if (kind, n, half) == ("p", 2, 1):
                        merged_high(0)
                    split_ahead(j, PIECES - 1)
                    s = i - 1
                    if 0 <= s < STEPS:
                        wide = NPAT * (s % NT + 1) * P
                        act.wait_ge(probT_ps.sem, probT_ps.at(l, s + 1))
                        if s >= 1:
                            act.wait_ge(ao_ps.sem, ao_ps.at(l, s))
                        A(probT[:, 0:wide], M1[:, 0:wide], ACT.Copy).then_inc(probT_sb.sem, 1)
                    if kind == "p":
                        split_ahead(j, PIECES)
                    if kind == "g":
                        o = done(j)
                        if n == 0 and half == 1:
                            act.wait_ge(brA_ready.sem, brA_ready.at(l, 1))
                        if n == 1:
                            before = J_G + GATE_JOBS.index(("p", 0, half))
                            act.wait_ge(taken[before % 2].sem, taken[before % 2].at(l, before // 2 + 1))
                        if n == 2:
                            act.wait_ge(merged_ready.sem, merged_ready.at(l, half + 1))
                        A(sig[half], o[:, :], ACT.Sigmoid).then_inc(taken[j % 2].sem, 1)
                        split_ahead(j, PIECES)
                    s = i
                    if s < STEPS:
                        wide = NPAT * (s % NT + 1) * P
                        act.wait_ge(sc_max.sem, sc_max.at(l, s + 1))
                        if s >= 1:
                            act.wait_ge(probT_ps.sem, probT_ps.at(l, s))
                        A(prob[:, 0:wide], sc[:, 0:wide], ACT.Exp, bias=anegm, scale=ASCALE,
                          accum_out=aden).then_inc(sc_exp.sem, 1)

                merged_high(1)
                split_ahead(J_OUT, 0)
                warm_sqrt()
                for t in range(NT):
                    j = J_OUT + t
                    act.wait_ge(taken[j % 2].sem, taken[j % 2].at(l, j // 2 + 1))
                    norm_stats(1, t)
                act.wait_ge(rt_max.sem, rt_max.at(l, 1))
                A(rt(2), rt(1), ACT.Exp).then_inc(rt_exp.sem, 1)

                act.wait_ge(pairs_known, l + 2)
                settle(act)
                end = act.value_load(pairs_end[0:1, 0:1], min_val=0, max_val=DEPTH * NPASS * PAIRS)
                with act.Fori(start, end) as it:
                    act.wait_ge(selT_ps, it + 1 + BASE)
                    act.wait_ge(mix_ps, NT * it + BASE)
                    A(selT, slotp[1][:, 0:NT * P], ACT.Copy).then_inc(selT_sb, 1)
                    act.wait_ge(gate_ps, it + 1 + BASE)
                    A(silu_g, M0[:, 0:FF], ACT.Silu).then_inc(silu_ready, 1)
                    act.wait_ge(hT_ps, it + 1)
                    act.wait_ge(y_ps, it + BASE)
                    A(hTs, M1[:, FF:FF + FC * P], ACT.Copy).then_inc(hT_sb, 1)
                    act.wait_ge(y_ps, it + 1 + BASE)
                    A(ysb[:, 0:512], slotp[1][:, 0:512], ACT.Copy).then_inc(y_sb, 1)

        @block.vector
        def _(dve):
            v = nc.vector
            setup = [0]

            def first(ins):
                setup[0] += 1
                ins.then_inc(setup_step, 1)
                dve.wait_ge(setup_step, setup[0])

            first(v.memset(total_pairs, 0.0))
            v.tensor_copy(pairs_end[0:1, 0:1], total_pairs).then_inc(pairs_known, 1)
            dve.wait_ge(consts_in, 32)
            first(v.tensor_copy(posf, pos_i[:, :]))
            for t in range(NT):
                first(v.tensor_scalar(sinb[:, t, :], c("freq"), posf[:, t:t + 1], None, ALU.mult))
            turns = rope_tmp[:, 0, 0:NT * ROPE].rearrange("p (t r) -> p t r", t=NT)
            first(v.tensor_scalar(turns, sinb[:, :, :], float(np.float32(1 / (2 * np.pi))), None, ALU.mult))
            first(v.tensor_scalar(turns, turns, float(1.5 * 2 ** 23), None, ALU.add))
            first(v.tensor_scalar(turns, turns, float(-1.5 * 2 ** 23), None, ALU.add))
            rest = 2 * np.pi
            for bits in (8, 8, 8, 24):
                scale = 2.0 ** (bits - 1 - np.floor(np.log2(abs(rest))))
                part = np.rint(rest * scale) / scale
                rest -= part
                first(v.scalar_tensor_tensor(out=sinb[:, :, :], in0=turns, scalar=float(-part), in1=sinb[:, :, :],
                                             op0=ALU.mult, op1=ALU.add))
            below_pi = float(np.nextafter(np.float32(np.pi), np.float32(0)))
            first(v.tensor_scalar(sinb[:, :, :], sinb[:, :, :], below_pi, -below_pi, ALU.min, ALU.max))
            first(v.scalar_tensor_tensor(out=cosb[:, :, :], in0=sinb[:, :, :], scalar=-1.0, in1=sinb[:, :, :],
                                         op0=ALU.mult, op1=ALU.min))
            v.tensor_scalar(cosb[:, :, :], cosb[:, :, :], float(np.pi / 2), None, ALU.add).then_inc(setup_act, 1)
            dve.wait_ge(rope_ready, 2)
            dve.wait_ge(more_consts_in, 16)

            with dve.Fori(0, DEPTH) as l:
                dve.wait_ge(pairs_known, l + 1)
                settle(dve)
                start = dve.value_load(pairs_end[0:1, 0:1], min_val=0, max_val=DEPTH * NPASS * PAIRS)
                step = [0]

                def link(ins):
                    step[0] += 1
                    ins.then_inc(dve_step.sem, 1)
                    dve.wait_ge(dve_step.sem, dve_step.at(l, step[0]))

                def done(j):
                    dve.wait_ge(job_done.sem, job_done.at(l, j + 1))
                    return slotp[j % 2]

                def take_done(j):
                    dve.wait_ge(taken[j % 2].sem, taken[j % 2].at(l, j // 2 + 1))

                def diagonal(n, t):
                    dve.wait_ge(rms_sd.sem, rms_sd.at(l, NT * n + t + 1))
                    link(v.reciprocal(rinv[:, t:t + 1], sd[:, t:t + 1]))
                    v.tensor_scalar(diag[:, t * P:(t + 1) * P], ident, rinv[:, t:t + 1], None,
                                    ALU.mult).then_inc(diag_ready.sem, 1)

                low_parts = [0]

                def split_ahead(j, n):
                    for i in range(low_parts[0], min(last_piece(j) + n + 1, len(PLAN))):
                        dve.wait_ge(hi_ready.sem, hi_ready.at(l, i + 1))
                        v.tensor_tensor(piece_of(w_lo, i), source(i), piece_of(w_hi, i), ALU.subtract)\
                            .then_inc(lo_ready.sem, 1)
                        low_parts[0] = i + 1

                def take_hT(n, t, gain):
                    j = (J_NORM1, J_NORM2)[n] + t
                    o = done(j)
                    v.tensor_tensor(hT[:, :, t * P:(t + 1) * P], o[:, :].rearrange("p (c t) -> p c t", c=DC),
                                    gain.unsqueeze(2).broadcast_to((P, DC, P)), ALU.mult)\
                        .then_inc(taken[j % 2].sem, 1)

                dve.wait_ge(x_in, 16)
                for t in range(NT):
                    diagonal(0, t)
                dve.wait_ge(par_in, 16 * l + 16)
                v.memset(xpad[:, :, 0:TAPS - 1], 0.0).then_inc(pad_ready.sem, 1)
                v.scalar_tensor_tensor(out=spz, in0=q("lam"), scalar=-1.0, in1=q("lam"), op0=ALU.mult,
                                       op1=ALU.max).then_inc(lam_abs.sem, 1)
                for t in range(NT):
                    take_hT(0, t, q("gain1"))
                for t in range(NT):
                    s = slice(t * P, (t + 1) * P)
                    dve.wait_ge(hT_hi_ready.sem, hT_hi_ready.at(l, t + 1))
                    v.tensor_tensor(hT_lo[:, :, s], hT[:, :, s], hT_hi[:, :, s], ALU.subtract)\
                        .then_inc(hT_lo_ready.sem, 1)
                split_ahead(J_QK, 0)
                dve.wait_ge(lam_exp.sem, lam_exp.at(l, 1))
                link(v.tensor_scalar(sps, spz, 2.0, None, ALU.add))
                link(v.reciprocal(sps, sps))
                link(v.tensor_tensor(sps, sps, spz, ALU.mult))
                link(v.tensor_tensor(sp2, sps, sps, ALU.mult))
                link(v.tensor_scalar(spp, sp2, 1.0 / 17, None, ALU.mult))
                for odd in (15, 13, 11, 9, 7, 5, 3):
                    link(v.scalar_tensor_tensor(out=spp, in0=spp, scalar=1.0 / odd, in1=sp2, op0=ALU.add, op1=ALU.mult))
                link(v.scalar_tensor_tensor(out=spp, in0=spp, scalar=1.0, in1=sps, op0=ALU.add, op1=ALU.mult))
                link(v.tensor_scalar(sps, q("lam"), -1.0, 0.0, ALU.mult, ALU.max))
                link(v.scalar_tensor_tensor(out=spp, in0=spp, scalar=2.0, in1=sps, op0=ALU.mult, op1=ALU.add))
                link(v.tensor_scalar(sp_pos, spp, 8.0, None, ALU.mult))
                v.tensor_scalar(sp_neg, spp, -8.0, None, ALU.mult).then_inc(lam_ready.sem, 1)

                split_ahead(J_QK, PIECES - 1)
                dve.wait_ge(z_ps.sem, z_ps.at(l, 1))
                for g in range(2):
                    link(v.tensor_scalar(la[:, g * T:(g + 1) * T], M0[:, g * T:(g + 1) * T],
                                         q("gate_b")[:, g:g + 1], None, ALU.add))
                v.scalar_tensor_tensor(out=cum, in0=la, scalar=-1.0, in1=la, op0=ALU.mult, op1=ALU.max)\
                    .then_inc(z_abs.sem, 1)
                split_ahead(J_QK, PIECES)
                dve.wait_ge(decay_ln.sem, decay_ln.at(l, 1))
                link(v.scalar_tensor_tensor(out=la, in0=la, scalar=0.0, in1=cum, op0=ALU.min, op1=ALU.subtract))
                for n in range(NT * T // CH):
                    s = slice(n * CH, (n + 1) * CH)
                    w = v.tensor_tensor_scan(cum[:, s], ones[:, 0:CH], la[:, s], 0.0, ALU.mult, ALU.add)
                link(w)
                cumv = cum.rearrange("p (n t) -> p n t", t=CH)
                v.tensor_tensor(la.rearrange("p (n t) -> p n t", t=CH), cumv,
                                cumv[:, :, CH - 1:CH].broadcast_to((P, NT * T // CH, CH)), ALU.subtract)\
                    .then_inc(cum_ready.sem, 1)

                split_ahead(J_VA, PIECES)
                dve.wait_ge(exps_ready.sem, exps_ready.at(l, 1))
                take_done(J_QK)
                v.tensor_tensor(k_dec, k_dec, qk_ch[:, 512:1024], ALU.mult)
                v.tensor_tensor(k_inv, k_inv, qk_ch[:, 512:1024], ALU.mult)
                v.tensor_tensor(q_dec, q_dec, qk_ch[:, 0:512], ALU.mult).then_inc(gqk_ready.sem, 1)

                split_ahead(J_XB, PIECES - 1)
                take_done(J_XB)
                split_ahead(J_XB, PIECES)
                for k in range(TAPS):
                    if k:
                        split_ahead(J_YB, k)
                    for cc in range(WC):
                        o = xc[:, cc * T:(cc + 1) * T]
                        tap = q("conv_w")[:, k * WC + cc:k * WC + cc + 1]
                        if k == 0:
                            w = v.tensor_scalar(o, xpad[:, cc, 0:T], tap, q("conv_b")[:, cc:cc + 1], ALU.mult, ALU.add)
                        else:
                            w = v.scalar_tensor_tensor(out=o, in0=xpad[:, cc, k:k + T], scalar=tap, in1=o,
                                                       op0=ALU.mult, op1=ALU.add)
                    if k < TAPS - 1:
                        link(w)
                w.then_inc(xc_ready.sem, 1)

                split_ahead(J_OG, PIECES)
                dve.wait_ge(lru_at.sem, lru_at.at(l, 1))
                link(v.tensor_tensor(a_sq, gate_r, gate_r, ALU.mult))
                v.scalar_tensor_tensor(out=tanh_y, in0=a_sq, scalar=1.0, in1=tanh_y, op0=ALU.add,
                                       op1=ALU.mult).then_inc(lru_m.sem, 1)
                dve.wait_ge(xc_ready.sem, xc_ready.at(l, 1))
                link(v.tensor_tensor(gate_i, gate_i, xc, ALU.mult))
                split_ahead(J_Q, 2)
                dve.wait_ge(lru_sqrt.sem, lru_sqrt.at(l, 1))
                link(v.tensor_tensor(gate_i, gate_i, tanh_y, ALU.mult))
                for cc in range(WC):
                    s = slice(cc * T, (cc + 1) * T)
                    w = v.tensor_tensor_scan(xc[:, s], gate_r[:, s], gate_i[:, s], 0.0, ALU.mult, ALU.add)
                link(w)
                take_done(J_YB)
                v.tensor_tensor(br[1], br[1], xc, ALU.mult).then_inc(brB_ready.sem, 1)

                def qk_norm(u):
                    split_ahead(J_Q + u, PIECES)
                    dve.wait_ge(att_sd.sem, att_sd.at(l, u + 1))
                    link(v.reciprocal(arinv, asd[u % 2]))
                    raw = qk_raw[u].rearrange("p (g d) -> p g d", d=DH)
                    for g in range(NT * NH):
                        w = v.scalar_tensor_tensor(out=raw[:, g], in0=raw[:, g], scalar=arinv[:, g:g + 1],
                                                   in1=q("q_gain" if u < NPAT else "k_gain"),
                                                   op0=ALU.mult, op1=ALU.mult)
                    link(w)
                    x1 = raw[:, :, 0:ROPE].rearrange("p (t h) d -> p t h d", t=NT)
                    x2 = raw[:, :, ROPE:2 * ROPE].rearrange("p (t h) d -> p t h d", t=NT)
                    cs = cosb[:, :, :].unsqueeze(2).broadcast_to((P, NT, NH, ROPE))
                    sn = sinb[:, :, :].unsqueeze(2).broadcast_to((P, NT, NH, ROPE))
                    tmp = [rope_tmp[:, i, :].rearrange("p (t h d) -> p t h d", t=NT, h=NH) for i in range(4)]
                    v.tensor_tensor(tmp[0], x1, cs, ALU.mult)
                    v.tensor_tensor(tmp[1], x2, sn, ALU.mult)
                    v.tensor_tensor(tmp[2], x2, cs, ALU.mult)
                    link(v.tensor_tensor(tmp[3], x1, sn, ALU.mult))
                    v.tensor_tensor(x1, tmp[0], tmp[1], ALU.subtract)
                    v.tensor_tensor(x2, tmp[2], tmp[3], ALU.add).then_inc(att_in.sem, 1)

                qk_norm(0)
                dve.wait_ge(gsc_ps.sem, gsc_ps.at(l, 1))
                mask = c("gla_mask").unsqueeze(1).broadcast_to((P, 4, P))
                for i in range(2):
                    w = v.tensor_tensor(gsc[:, i * 512:(i + 1) * 512].rearrange("p (n q) -> p n q", n=4),
                                        M1[:, i * 512:(i + 1) * 512].rearrange("p (n q) -> p n q", n=4),
                                        mask, ALU.mult)
                w.then_inc(gsc_sb.sem, 1)
                qk_norm(1)
                dve.wait_ge(kv_ps.sem, kv_ps.at(l, 1))
                for g in range(2):
                    st = [state[:, (g * 3 + n) * DV:(g * 3 + n + 1) * DV] for n in range(3)]
                    link(v.tensor_copy(st[0], M0[:, 512 + g * P:512 + (g + 1) * P]))
                    link(v.scalar_tensor_tensor(out=st[1], in0=st[0], scalar=etot[:, g * 4 + 1:g * 4 + 2],
                                                in1=M0[:, g * P:(g + 1) * P], op0=ALU.mult, op1=ALU.add))
                    w = v.scalar_tensor_tensor(out=st[2], in0=st[1], scalar=etot[:, g * 4 + 2:g * 4 + 3],
                                               in1=M0[:, 768 + g * P:768 + (g + 1) * P], op0=ALU.mult, op1=ALU.add)
                w.then_inc(state_ready.sem, 1)
                qk_norm(2)
                split_ahead(J_K, PIECES)
                dve.wait_ge(grms.sem, grms.at(l, 1))
                link(v.reciprocal(grinv, grinv))
                v.tensor_tensor(gsq.rearrange("p (b t) -> p b t", b=NT * HG),
                                ident.unsqueeze(1).broadcast_to((P, NT * HG, P)),
                                grinv.unsqueeze(2).broadcast_to((P, NT * HG, P)), ALU.mult).then_inc(gdiag_ready.sem, 1)
                qk_norm(3)
                split_ahead(J_K + 1, PIECES)
                def by_half(ap, hh):
                    return ap.rearrange("p (g h t) -> p g h t", g=2, h=2)[:, :, hh, :]

                def from_half(ap, hh):
                    return ap[:, hh * 512:(hh + 1) * 512].rearrange("p (g t) -> p g t", g=2)

                take_done(J_OG)
                for hh in range(2):
                    w = v.scalar_tensor_tensor(out=by_half(og, hh), in0=from_half(M1, hh), scalar=q("out_gain"),
                                               in1=by_half(og, hh), op0=ALU.mult, op1=ALU.mult)
                link(w)
                dve.wait_ge(grinv_ps.sem, grinv_ps.at(l, 1))
                for hh in range(2):
                    w = v.tensor_tensor(by_half(br[0], hh), from_half(M0, hh), by_half(og, hh), ALU.mult)
                w.then_inc(brA_ready.sem, 1)
                for u in (4, 5):
                    qk_norm(u)

                def branch_low(n):
                    dve.wait_ge(br_hi_ready.sem, br_hi_ready.at(l, n + 1))
                    v.tensor_tensor(br_lo[:, n % 2, :], br[n], br_hi[:, n % 2, :], ALU.subtract)\
                        .then_inc(br_lo_ready.sem, 1)

                for n in range(2):
                    split_ahead(J_K + 4 + n, PIECES)
                    branch_low(n)

                def merged_low(half):
                    dve.wait_ge(mg_hi_ready.sem, mg_hi_ready.at(l, half + 1))
                    rows = slice(half * WC, (half + 1) * WC)
                    v.tensor_tensor(hT_lo[:, rows, :],
                                    merged[:, half * BLK:(half + 1) * BLK].rearrange("p (c t) -> p c t", c=WC),
                                    hT_hi[:, rows, :], ALU.subtract).then_inc(mg_lo_ready.sem, 1)

                for i in range(len(GATE_JOBS)):
                    kind, n, half = GATE_JOBS[i]
                    j = J_G + i
                    if i == STEPS + 1:
                        branch_low(2)
                    if (kind, n, half) == ("p", 2, 1):
                        merged_low(0)
                    split_ahead(j, PIECES - 1)
                    if i < STEPS:
                        s, t = i, i % NT
                        wide = NPAT * (t + 1) * P
                        dve.wait_ge(sc_ps.sem, sc_ps.at(l, s + 1))
                        if s >= 1:
                            dve.wait_ge(sc_exp.sem, sc_exp.at(l, s))
                        band = c("band").rearrange("p (n k) -> p n k", n=NPAT)[:, :, (NT - 1 - t) * P:]
                        v.tensor_tensor(sc[:, 0:wide].rearrange("p (n k) -> p n k", n=NPAT),
                                        M0[:, 0:wide].rearrange("p (n k) -> p n k", n=NPAT), band, ALU.add)\
                            .then_inc(sc_sb.sem, 1)
                        dve.wait_ge(sc_sb.sem, sc_sb.at(l, s + 1))
                        link(v.tensor_reduce(amax, sc[:, 0:wide], AX.X, ALU.max))
                        v.tensor_scalar(anegm, amax, -ASCALE, None, ALU.mult).then_inc(sc_max.sem, 1)
                    if kind == "p":
                        o = done(j)
                        take_done(J_G + GATE_JOBS.index(("g", n, half)))
                        mg = merged[:, half * BLK:(half + 1) * BLK]
                        if n == 0:
                            v.tensor_tensor(mg, sig[half], o[:, :], ALU.mult).then_inc(taken[j % 2].sem, 1)
                        else:
                            v.tensor_tensor(sig[half], sig[half], o[:, :], ALU.mult).then_inc(taken[j % 2].sem, 1)
                            take_done(j)
                            if n > 1:
                                dve.wait_ge(merged_ready.sem, merged_ready.at(l, half + 1))
                            v.tensor_tensor(mg, mg, sig[half], ALU.add).then_inc(merged_ready.sem, 1)
                    split_ahead(j, PIECES)
                    if i < STEPS:
                        dve.wait_ge(sc_exp.sem, sc_exp.at(l, s + 1))
                        link(v.reciprocal(arden, aden))
                        v.tensor_scalar(prob[:, 0:wide], prob[:, 0:wide], arden, None, ALU.mult)\
                            .then_inc(prob_ready.sem, 1)

                merged_low(1)
                split_ahead(J_OUT, 0)
                for t in range(NT):
                    j = J_OUT + t
                    o = done(j)
                    v.tensor_tensor(xs[:, t, :], xs[:, t, :], o[:, :], ALU.add).then_inc(taken[j % 2].sem, 1)
                    diagonal(1, t)
                dve.wait_ge(gain2_in, 16 * l + 16)
                for t in range(NT):
                    link(v.tensor_scalar(hn[:, t * D:(t + 1) * D], xs[:, t, :], rinv[:, t:t + 1], None, ALU.mult))
                    take_hT(1, t, g2[:, :])

                def e16(i):
                    return rt(i).rearrange("p (t e) -> p t e", t=NT)

                def per_tile(ap):
                    return ap.unsqueeze(2).broadcast_to((P, NT, NE))

                member, _, ex, top1, top2 = (rt(i) for i in range(5))
                red = [blk(5, off=512 + 8 * i, width=NT) for i in range(8)]
                dve.wait_ge(logit_ps.sem, logit_ps.at(l, 1))
                link(v.tensor_tensor(e16(1), M0[:, 0:NT * NE].rearrange("p (t e) -> p t e", t=NT),
                                     c("router_b").unsqueeze(1).broadcast_to((P, NT, NE)), ALU.add))
                link(v.tensor_reduce(red[0], e16(1), AX.X, ALU.max))
                v.tensor_tensor(e16(1), e16(1), per_tile(red[0]), ALU.subtract).then_inc(rt_max.sem, 1)
                dve.wait_ge(rt_exp.sem, rt_exp.at(l, 1))
                link(v.tensor_reduce(red[1], e16(2), AX.X, ALU.add))
                link(v.reciprocal(red[2], red[1]))
                link(v.tensor_tensor(e16(2), e16(2), per_tile(red[2]), ALU.mult))
                ev = ex.rearrange("p (g e) -> p g e", e=NE // NG)
                hi1, lo1, hi2, lo2, m1, m2, gs, gsel = (blk(5, off=608 + 8 * i, width=8) for i in range(8))
                v.tensor_tensor(hi1, ev[:, :, 0], ev[:, :, 1], ALU.max)
                v.tensor_tensor(lo1, ev[:, :, 0], ev[:, :, 1], ALU.min)
                v.tensor_tensor(hi2, ev[:, :, 2], ev[:, :, 3], ALU.max)
                link(v.tensor_tensor(lo2, ev[:, :, 2], ev[:, :, 3], ALU.min))
                v.tensor_tensor(m1, hi1, hi2, ALU.max)
                v.tensor_tensor(m2, hi1, hi2, ALU.min)
                link(v.tensor_tensor(lo1, lo1, lo2, ALU.max))
                link(v.tensor_tensor(m2, m2, lo1, ALU.max))
                link(v.tensor_tensor(gs, m1, m2, ALU.add))

                def first_max(dst, src, keys, top, shape):
                    key = blk(5, off=672, width=shape[1] * shape[2]).rearrange("p (t e) -> p t e", t=NT)
                    kt = blk(5, off=712, width=NT)
                    link(v.tensor_reduce(top, src, AX.X, ALU.max))
                    for t in range(NT):
                        w = v.scalar_tensor_tensor(out=key[:, t, :], in0=src[:, t, :], scalar=top[:, t:t + 1],
                                                   in1=keys, op0=ALU.is_equal, op1=ALU.mult)
                    link(w)
                    link(v.tensor_reduce(kt, key, AX.X, ALU.max))
                    link(v.tensor_tensor(dst, key, kt.unsqueeze(2).broadcast_to(shape), ALU.is_equal))

                gsv = gs.rearrange("p (t g) -> p t g", t=NT)
                gselv = gsel.rearrange("p (t g) -> p t g", t=NT)
                first_max(gselv, gsv, c("key4"), red[3], (P, NT, NG))
                gb = gsel.unsqueeze(2).broadcast_to((P, NT * NG, NE // NG))
                out_of_group = gs
                v.tensor_scalar(out_of_group, gsel, -1.0, None, ALU.add)
                link(v.tensor_tensor(ev, ev, gb, ALU.mult))
                link(v.tensor_tensor(ev, ev, out_of_group.unsqueeze(2).broadcast_to((P, NT * NG, NE // NG)), ALU.add))
                first_max(e16(3), e16(2), c("key16"), red[4], (P, NT, NE))
                link(v.scalar_tensor_tensor(out=ex, in0=top1, scalar=-4.0, in1=ex, op0=ALU.mult, op1=ALU.add))
                first_max(e16(4), e16(2), c("key16"), red[5], (P, NT, NE))
                v.tensor_tensor(member, top1, top2, ALU.add).then_inc(member_ready.sem, 1)
                link(v.tensor_tensor(red[6], red[4], red[5], ALU.add))
                link(v.reciprocal(red[6], red[6]))
                v.tensor_tensor(red[4], red[4], red[6], ALU.mult)
                link(v.tensor_tensor(red[5], red[5], red[6], ALU.mult))
                link(v.tensor_tensor(e16(3), e16(3), per_tile(red[4]), ALU.mult))
                link(v.tensor_tensor(e16(4), e16(4), per_tile(red[5]), ALU.mult))
                link(v.tensor_tensor(gw2, e16(3).rearrange("p t e -> p e t"), e16(4).rearrange("p t e -> p e t"),
                                     ALU.add))
                dve.wait_ge(rank_ps.sem, rank_ps.at(l, 1))
                link(v.scalar_tensor_tensor(out=rank2, in0=M1[:, 0:NT * NE].rearrange("p (t e) -> p e t", t=NT),
                                            scalar=1.0, in1=e16(0).rearrange("p t e -> p e t"),
                                            op0=ALU.add, op1=ALU.mult))

                def select(n, it):
                    e = 2 * (it % PAIRS)
                    base = nc.s_assert_within((it - start) // PAIRS * CAP, 0, T,
                                              skip_runtime_bounds_check_because="npass is at most T / CAP")
                    for i in range(2):
                        sv = sel.rearrange("p (t i s) -> p i t s", t=NT, i=2)[:, i]
                        w = v.tensor_tensor(sv, c("iota")[:, bass.ds(base, CAP)].unsqueeze(1).broadcast_to((P, NT, CAP)),
                                            rank2[:, bass.ds(e + i, 1), :].rearrange("p o t -> p (o t)").unsqueeze(2)
                                            .broadcast_to((P, NT, CAP)), ALU.is_equal)
                    w.then_inc(sel_hot, 1)
                    dve.wait_ge(sel_hot, n + 1)
                    for i in range(2):
                        w = v.tensor_tensor(selw.rearrange("p (t i s) -> p i t s", t=NT, i=2)[:, i],
                                            sel.rearrange("p (t i s) -> p i t s", t=NT, i=2)[:, i],
                                            gw2[:, bass.ds(e + i, 1), :].rearrange("p o t -> p (o t)").unsqueeze(2)
                                            .broadcast_to((P, NT, CAP)), ALU.mult)
                    w.then_inc(sel_ready, 1)

                def take_gather(n):
                    dve.wait_ge(xg_ps, n + 1 + BASE)
                    v.tensor_tensor(xgT, slotp[0][:, :].rearrange("p (c s) -> p c s", c=DC),
                                    g2[:, :].unsqueeze(2).broadcast_to((P, DC, P)), ALU.mult).then_inc(xg_sb, 1)

                select(start + l, start)
                link(v.tensor_reduce(mxc, M1[0:1, 512:512 + NE], AX.X, ALU.max))
                link(v.tensor_scalar(cmp4, c("caps")[0:1, :], mxc, None, ALU.is_lt))
                link(v.tensor_reduce(npass, cmp4, AX.X, ALU.add))
                link(v.scalar_tensor_tensor(out=total_pairs, in0=npass, scalar=float(PAIRS), in1=total_pairs,
                                            op0=ALU.mult, op1=ALU.add))
                v.tensor_copy(pairs_end[0:1, 0:1], total_pairs).then_inc(pairs_known, 1)
                dve.wait_ge(pairs_known, l + 2)
                settle(dve)
                end = dve.value_load(pairs_end[0:1, 0:1], min_val=0, max_val=DEPTH * NPASS * PAIRS)
                take_gather(start + l)
                with dve.Fori(start, end) as it:
                    dve.wait_ge(selT_ps, it + 1 + BASE)
                    dve.wait_ge(xg_ps, it + l + 1 + BASE)
                    select(it + l + 1, it + 1)
                    dve.wait_ge(silu_ready, it + 1)
                    dve.wait_ge(gu_ps, it + 1 + BASE)
                    v.tensor_tensor(hs, silu_g, M0[:, FF:2 * FF], ALU.mult).then_inc(h_ready, 1)
                    dve.wait_ge(y_ps, it + 1 + BASE)
                    v.tensor_copy(ysb[:, 512:1024], slotp[1][:, 512:1024]).then_inc(y_sb, 1)
                    take_gather(it + l + 1)
                    for t in range(NT):
                        dve.wait_ge(mix_ps, NT * it + t + 1 + BASE)
                        v.tensor_tensor(xs[:, t, :], xs[:, t, :], (M0, M1)[t][:, :], ALU.add).then_inc(x_add[t], 1)
                assert step[0] == dve_step.per, step[0]


def constants(router_w, router_b):
    k = np.zeros((P, NCONST), np.float32)

    def put(name, value):
        a, b = CONST[name]
        k[:, a:b] = value

    i, j = np.arange(P)[:, None], np.arange(P)[None, :]
    put("ident", i == j)
    put("mean", 1.0 / P)
    put("ones", 1.0)
    put("before", i < j)
    put("gla_mask", (i // CH == j // CH) & (i <= j))
    dist = P + np.arange(P)[:, None] - np.arange(T)[None, :]
    band = [np.where((dist >= 0) & (dist % dil == 0) & (dist // dil <= window // dil), 0.0, -1e30)
            for window, dil in PATTERNS]
    put("band", np.concatenate(band, 1))
    put("iota", 1 + np.arange(T + CAP)[None, :])
    put("caps", (CAP * np.arange(NPASS))[None, :])
    put("key4", (NG - np.arange(NG))[None, :])
    put("key16", (NE - np.arange(NE))[None, :])
    put("freq", (THETA ** (-np.arange(ROPE) / ROPE))[None, :])
    put("eps", EPS)
    put("one", 1.0)
    put("router_w", router_w.reshape(DC, P, NE).transpose(1, 0, 2).reshape(P, -1))
    put("router_b", router_b[None, :])
    return k


def parameters(a):
    k = np.zeros((DEPTH, P, NPAR), np.float32)
    for l in range(DEPTH):
        def put(name, value, rows=P):
            s, e = PAR[name]
            k[l, 0:rows, s:e] = value

        def cols(v):
            return v.reshape(-1, P).T

        def blocks(w):
            o = np.zeros((P, WC, P), np.float32)
            for n in range(2 * WC):
                b = (n % 2) * 64
                o[b:b + 64, n // 2, b:b + 64] = w[n]
            return o.reshape(P, -1)

        put("gain1", cols(a["norm1_gain"][l]))
        put("gate_b", cols(a["gla_gate_bias"][l]))
        put("out_gain", cols(a["gla_out_gain"][l]))
        put("conv_w", a["lru_conv_w"][l].reshape(TAPS, WC, P).transpose(2, 0, 1).reshape(P, -1))
        put("conv_b", cols(a["lru_conv_b"][l]))
        put("b_a", cols(a["lru_b_a"][l]))
        put("b_x", cols(a["lru_b_x"][l]))
        put("lam", cols(a["lru_lambda"][l]))
        put("w_a", blocks(a["lru_w_a"][l]))
        put("w_x", blocks(a["lru_w_x"][l]))
        put("q_gain", a["q_norm_gain"][l][None, :])
        put("k_gain", a["k_norm_gain"][l][None, :])
        put("low", a["w_in"][l][:, C_LOW:C_LOW + RANK].reshape(DC, P, RANK).transpose(1, 0, 2).reshape(P, -1))
        put("gate_up", a["gla_gate_up"][l], RANK)
    return k


def kernel(**inputs):
    import concourse.bacc as _bacc
    from concourse.bass_utils import run_bass_kernel_spmd as _run

    a = {name: np.ascontiguousarray(v) for name, v in inputs.items()}
    arrays = {
        "x": a["x"], "positions": a["positions"],
        "const": constants(a["router_w"], a["router_b"]), "par": parameters(a),
        "gain2": np.ascontiguousarray(a["norm2_gain"].reshape(DEPTH, DC, P).transpose(0, 2, 1)),
    }
    for name in ("w_in", "w_branch", "w_out", "w_gate", "w_up", "w_down"):
        arrays[name] = a[name]
    nc = _bacc.Bacc("TRN2", target_bir_lowering=False, num_devices=1)
    args = [nc.dram_tensor(f"in_{n}", v.shape, mybir.dt.from_np(v.dtype), kind="ExternalInput").ap()
            for n, v in arrays.items()]
    out = nc.dram_tensor("out_x", a["x"].shape, F32, kind="ExternalOutput").ap()
    build(nc, *args, out)
    r = _run(nc, [{f"in_{n}": v for n, v in arrays.items()}], core_ids=[0])
    return r.results[0]["out_x"]
```
